# Optimizing a Trainium2 kernel written in Bass

```python
import jax, jax.numpy as jnp
from jax import lax
import numpy as np

'''
One inference step of a hybrid autoregressive decoder (DEPTH layers), run for two request groups that share every weight.

Layer (pre-norm, plain residual adds):
  h = RMSNorm(x); p = h @ w_in  (ONE combined input projection, columns partitioned among head groups)
    head group A (8 heads): multi-head latent attention, low-rank q latent (192) and kv latent (128, RMSNormed, cached),
      decoupled rotary key (32, shared across heads, cached), causal softmax over the whole past (paged cache).
    head group B (8 heads): dilated sliding-window attention, patterns (window, dilation) = (128,1),(512,4),(2048,16);
      query t reads t, t-d, t-2d, ... t-window (keys gathered by stride), ALiBi penalty -m_h*(t-s);
      the three pattern outputs are merged per position and head with weights proportional to their softmax denominators.
  x += concat(RMSNorm(o_A), RMSNorm(o_B)) @ w_out   (ONE output projection)
  x += hierarchical MoE(RMSNorm(x)): top-1 of 4 expert groups, then top-2 of 8 SwiGLU experts inside the group.
Final RMSNorm on the trunk output.

Inputs:
  x_prompt (BATCH, SEQ, D_MODEL) positions 0..SEQ-1
  x_sample (DEC_BATCH, DEC_SEQ, D_MODEL) positions PAST_LEN..PAST_LEN+DEC_SEQ-1
  cache_kv_latent (DEPTH, N_POOL, PAGE_SIZE, KV_LORA)  paged MLA latent pool
  cache_k_rope    (DEPTH, N_POOL, PAGE_SIZE, QK_ROPE)  paged MLA rotated rope key pool
  state_sw_k, state_sw_v (DEPTH, DEC_BATCH, min(WINDOW_MAX, PAST_LEN), SW_HEADS, SW_DIM) last rows, oldest first
  page_table (DEC_BATCH, N_PAGES) int32, N_PAGES = PAST_LEN // PAGE_SIZE, N_POOL = 5/4 * DEC_BATCH * N_PAGES
  then the weights (leading DEPTH axis) and norm_final (D_MODEL,).
Output tuple:
  (y_prompt (BATCH, SEQ, D_MODEL),
   y_sample (DEC_BATCH, DEC_SEQ, D_MODEL),
   kv_latent_prompt (DEPTH, BATCH, SEQ, KV_LORA), k_rope_prompt (DEPTH, BATCH, SEQ, QK_ROPE),
   sw_k_prompt, sw_v_prompt (DEPTH, BATCH, min(WINDOW_MAX, SEQ), SW_HEADS, SW_DIM),
   kv_latent_sample (DEPTH, DEC_BATCH, DEC_SEQ, KV_LORA), k_rope_sample (DEPTH, DEC_BATCH, DEC_SEQ, QK_ROPE),
   sw_k_sample, sw_v_sample (DEPTH, DEC_BATCH, min(WINDOW_MAX, PAST_LEN), SW_HEADS, SW_DIM))
'''

D_MODEL = 1024
BATCH = 1
SEQ = 1024
DEPTH = 1
DEC_BATCH = 8
DEC_SEQ = 8
PAST_LEN = 8192
PAGE_SIZE = 128

MLA_HEADS = 8
Q_LORA = 192
KV_LORA = 128
QK_NOPE = 64
QK_ROPE = 32
V_DIM = 64
ROPE_THETA = 10000.0
MLA_SCALE = (QK_NOPE + QK_ROPE) ** -0.5
SW_HEADS = 8
SW_DIM = 64
SW_SCALE = SW_DIM ** -0.5
DILATED_PATTERNS = ((128, 1), (512, 4), (2048, 16))
WINDOW_MAX = 2048
MLA_WIDTH = MLA_HEADS * V_DIM
SW_WIDTH = SW_HEADS * SW_DIM
MIX_WIDTH = MLA_WIDTH + SW_WIDTH
IN_WIDTH = Q_LORA + KV_LORA + QK_ROPE + 3 * SW_WIDTH
N_GROUPS = 4
EXPERTS_PER_GROUP = 8
N_EXPERTS = N_GROUPS * EXPERTS_PER_GROUP
TOP_K = 2
D_EXPERT = 512
MOE_BLOCK = 128
Q_BLOCK = 128
POOL_NUM = 5
POOL_DEN = 4
RMS_EPS = 1e-6
MASK_VALUE = -1e30

kernel_name = 'hymba_mla_dilated_hmoe_step'

def rmsnorm(x, g):
    xf = x.astype(jnp.float32)
    y = xf * lax.rsqrt(jnp.mean(xf * xf, axis=-1, keepdims=True) + RMS_EPS)
    return (y * g.astype(jnp.float32)).astype(x.dtype)

def alibi_slopes(n_heads):
    return 2.0 ** (-8.0 * jnp.arange(1, n_heads + 1, dtype=jnp.float32) / n_heads)

def rope(x, pos):
    half = x.shape[-1] // 2
    inv = ROPE_THETA ** (-jnp.arange(half, dtype=jnp.float32) / half)
    ang = pos[:, None] * inv[None, :]
    cos = jnp.cos(ang)[None, :, None, :]
    sin = jnp.sin(ang)[None, :, None, :]
    xf = x.astype(jnp.float32)
    x1, x2 = xf[..., :half], xf[..., half:]
    return jnp.concatenate([x1 * cos - x2 * sin, x1 * sin + x2 * cos], axis=-1).astype(x.dtype)

def mixer_inputs(x, pos, norm_g, w_in, norm_q, norm_kv, w_uq):
    b, t, _ = x.shape
    p = jnp.einsum('btd,de->bte', rmsnorm(x, norm_g), w_in)
    o1 = Q_LORA
    o2 = o1 + KV_LORA
    o3 = o2 + QK_ROPE
    o4 = o3 + SW_WIDTH
    o5 = o4 + SW_WIDTH
    c_q, c_kv, k_r = p[..., :o1], p[..., o1:o2], p[..., o2:o3]
    q_sw = p[..., o3:o4].reshape(b, t, SW_HEADS, SW_DIM)
    k_sw = p[..., o4:o5].reshape(b, t, SW_HEADS, SW_DIM)
    v_sw = p[..., o5:].reshape(b, t, SW_HEADS, SW_DIM)
    q = jnp.einsum('btc,che->bthe', rmsnorm(c_q, norm_q), w_uq)
    q_nope = q[..., :QK_NOPE]
    q_rope = rope(q[..., QK_NOPE:], pos)
    c_kv = rmsnorm(c_kv, norm_kv)
    k_rope = rope(k_r[:, :, None, :], pos)[:, :, 0, :]
    return q_nope, q_rope, c_kv, k_rope, q_sw, k_sw, v_sw

def mla_prompt(q_nope, q_rope, c_kv, k_rope, w_uk, w_uv):
    b, s = c_kv.shape[:2]
    k_nope = jnp.einsum('bsc,chd->bshd', c_kv, w_uk)
    v = jnp.einsum('bsc,chd->bshd', c_kv, w_uv)
    n_blk = s // Q_BLOCK

    def blocks(t):
        return jnp.moveaxis(t.reshape((b, n_blk, Q_BLOCK) + t.shape[2:]), 1, 0)

    key_pos = jnp.arange(s)

    def one_block(args):
        i, qn, qr = args
        sc = jnp.einsum('bqhd,bshd->bhqs', qn, k_nope) + jnp.einsum('bqhr,bsr->bhqs', qr, k_rope)
        sc = sc.astype(jnp.float32) * MLA_SCALE
        q_pos = i * Q_BLOCK + jnp.arange(Q_BLOCK)
        sc = jnp.where(key_pos[None, :] <= q_pos[:, None], sc, MASK_VALUE)
        p = jax.nn.softmax(sc, axis=-1).astype(v.dtype)
        return jnp.einsum('bhqs,bshd->bqhd', p, v)

    o = lax.map(one_block, (jnp.arange(n_blk), blocks(q_nope), blocks(q_rope)))
    return jnp.moveaxis(o, 0, 1).reshape(b, s, MLA_WIDTH)

def mla_sample(q_nope, q_rope, c_kv_new, k_rope_new, pool_kv, pool_kr, page_table, w_uk, w_uv):
    bd, t = c_kv_new.shape[:2]
    past_kv = pool_kv[page_table].reshape(bd, -1, KV_LORA)
    past_kr = pool_kr[page_table].reshape(bd, -1, QK_ROPE)
    q_lat = jnp.einsum('bthd,chd->bthc', q_nope, w_uk)

    def scores(kv, kr):
        sc = jnp.einsum('bthc,bsc->bhts', q_lat, kv) + jnp.einsum('bthr,bsr->bhts', q_rope, kr)
        return sc.astype(jnp.float32) * MLA_SCALE

    s_past = scores(past_kv, past_kr)
    causal = jnp.tril(jnp.ones((t, t), dtype=bool))
    s_new = jnp.where(causal, scores(c_kv_new, k_rope_new), MASK_VALUE)
    p = jax.nn.softmax(jnp.concatenate([s_past, s_new], axis=-1), axis=-1).astype(c_kv_new.dtype)
    n_past = past_kv.shape[1]
    o_lat = (jnp.einsum('bhts,bsc->bthc', p[..., :n_past], past_kv)
             + jnp.einsum('bhts,bsc->bthc', p[..., n_past:], c_kv_new))
    o = jnp.einsum('bthc,chd->bthd', o_lat, w_uv)
    return o.reshape(bd, t, MLA_WIDTH)

def dilated_pattern_prompt(q, k, v, slopes, band, dil):
    b, s, h, dh = q.shape
    unit = band * dil
    s_pad = -(-s // unit) * unit
    n_sub = s_pad // dil
    nb = n_sub // band

    def to_blocks(t):
        t = jnp.pad(t, ((0, 0), (0, s_pad - s), (0, 0), (0, 0)))
        t = t.reshape(b, n_sub, dil, h, dh).transpose(0, 2, 1, 3, 4)
        return t.reshape(b, dil, nb, band, h, dh)

    qb, kb, vb = to_blocks(q), to_blocks(k), to_blocks(v)

    def with_prev(t):
        prev = jnp.pad(t, ((0, 0), (0, 0), (1, 0), (0, 0), (0, 0), (0, 0)))[:, :, :-1]
        return jnp.concatenate([prev, t], axis=3)

    k2, v2 = with_prev(kb), with_prev(vb)
    sc = jnp.einsum('brnqhd,brnkhd->brnhqk', qb, k2).astype(jnp.float32) * SW_SCALE
    qi = jnp.arange(band)
    ki = jnp.arange(2 * band)
    dist = qi[:, None] + band - ki[None, :]
    valid = (dist >= 0) & (dist <= band)
    valid = valid[None] & ((jnp.arange(nb)[:, None, None] > 0) | (ki[None, None, :] >= band))
    sc = sc - slopes[:, None, None] * (dist * dil).astype(jnp.float32)
    sc = jnp.where(valid[None, None, :, None], sc, MASK_VALUE)
    lse = jax.nn.logsumexp(sc, axis=-1)
    p = jnp.exp(sc - lse[..., None]).astype(v.dtype)
    o = jnp.einsum('brnhqk,brnkhd->brnqhd', p, v2)
    o = o.reshape(b, dil, n_sub, h, dh).transpose(0, 2, 1, 3, 4).reshape(b, s_pad, h, dh)[:, :s]
    lse = lse.transpose(0, 1, 2, 4, 3).reshape(b, dil, n_sub, h).transpose(0, 2, 1, 3).reshape(b, s_pad, h)[:, :s]
    return o, lse

def merge_patterns(outs, lses):
    w = jax.nn.softmax(jnp.stack(lses, axis=0), axis=0)
    o = jnp.einsum('pbth,pbthd->bthd', w.astype(outs[0].dtype), jnp.stack(outs, axis=0))
    return o.reshape(o.shape[0], o.shape[1], SW_WIDTH)

def dilated_prompt(q, k, v, slopes):
    outs, lses = [], []
    for window, dil in DILATED_PATTERNS:
        o, lse = dilated_pattern_prompt(q, k, v, slopes, window // dil, dil)
        outs.append(o)
        lses.append(lse)
    return merge_patterns(outs, lses)

def dilated_sample(q, k_new, v_new, buf_k, buf_v, slopes):
    t = q.shape[1]
    n_buf = buf_k.shape[1]
    ext_k = jnp.concatenate([buf_k, k_new], axis=1)
    ext_v = jnp.concatenate([buf_v, v_new], axis=1)
    outs, lses = [], []
    for window, dil in DILATED_PATTERNS:
        band = window // dil
        steps = jnp.arange(band + 1)
        idx = n_buf + jnp.arange(t)[:, None] - steps[None, :] * dil
        valid = idx >= 0
        idx_c = jnp.maximum(idx, 0)
        kg = ext_k[:, idx_c]
        vg = ext_v[:, idx_c]
        sc = jnp.einsum('bthd,btkhd->bhtk', q, kg).astype(jnp.float32) * SW_SCALE
        sc = sc - slopes[:, None, None] * (steps * dil).astype(jnp.float32)[None, None, :]
        sc = jnp.where(valid[None, None], sc, MASK_VALUE)
        lse = jax.nn.logsumexp(sc, axis=-1)
        p = jnp.exp(sc - lse[..., None]).astype(vg.dtype)
        outs.append(jnp.einsum('bhtk,btkhd->bthd', p, vg))
        lses.append(jnp.transpose(lse, (0, 2, 1)))
    return merge_patterns(outs, lses), ext_k[:, t:], ext_v[:, t:]

def mix_output(o_a, o_b, g_a, g_b, w_out):
    cat = jnp.concatenate([rmsnorm(o_a, g_a), rmsnorm(o_b, g_b)], axis=-1)
    return jnp.einsum('btm,md->btd', cat, w_out)

def routed_experts(h, expert, gates, w_gate, w_up, w_down):
    n, d = h.shape
    n_assign = n * TOP_K
    a_exp = expert.reshape(-1)
    a_tok = jnp.repeat(jnp.arange(n, dtype=jnp.int32), TOP_K)
    a_gate = gates.reshape(-1)
    order = jnp.argsort(a_exp)
    s_exp, s_tok, s_gate = a_exp[order], a_tok[order], a_gate[order]
    counts = jnp.bincount(a_exp, length=N_EXPERTS)
    starts = jnp.cumsum(counts) - counts
    padded = (counts + MOE_BLOCK - 1) // MOE_BLOCK * MOE_BLOCK
    p_ends = jnp.cumsum(padded)
    p_starts = p_ends - padded
    dest = p_starts[s_exp] + (jnp.arange(n_assign) - starts[s_exp])
    n_rows = (-(-n_assign // MOE_BLOCK) + N_EXPERTS) * MOE_BLOCK
    n_blocks = n_rows // MOE_BLOCK
    tok_buf = jnp.zeros((n_rows,), jnp.int32).at[dest].set(s_tok)
    gate_buf = jnp.zeros((n_rows,), h.dtype).at[dest].set(s_gate.astype(h.dtype))
    block_exp = jnp.minimum(jnp.searchsorted(p_ends, jnp.arange(n_blocks) * MOE_BLOCK, side='right'), N_EXPERTS - 1)
    xb = h[tok_buf].reshape(n_blocks, MOE_BLOCK, d)

    def expert_block(args):
        xe, e = args
        return (jax.nn.silu(xe @ w_gate[e]) * (xe @ w_up[e])) @ w_down[e]

    yb = lax.map(expert_block, (xb, block_exp)).reshape(n_rows, d)
    return jax.ops.segment_sum(yb * gate_buf[:, None], tok_buf, num_segments=n)

def hier_moe(x, norm_g, w_rg, b_rg, w_re, b_re, w_gate, w_up, w_down):
    b, t, d = x.shape
    h = rmsnorm(x, norm_g).reshape(b * t, d)
    g_prob = jax.nn.softmax((h @ w_rg).astype(jnp.float32) + b_rg.astype(jnp.float32), axis=-1)
    g_idx = jnp.argmax(g_prob, axis=-1)
    g_gate = jnp.take_along_axis(g_prob, g_idx[:, None], axis=-1)
    e_logits = ((h @ w_re).astype(jnp.float32) + b_re.astype(jnp.float32)).reshape(-1, N_GROUPS, EXPERTS_PER_GROUP)
    e_logits = jnp.take_along_axis(e_logits, g_idx[:, None, None], axis=1)[:, 0]
    top_p, top_i = lax.top_k(jax.nn.softmax(e_logits, axis=-1), TOP_K)
    gates = g_gate * top_p / jnp.sum(top_p, axis=-1, keepdims=True)
    expert = (g_idx[:, None] * EXPERTS_PER_GROUP + top_i).astype(jnp.int32)
    return routed_experts(h, expert, gates, w_gate, w_up, w_down).reshape(b, t, d)

def setup_inputs(seed: int = 0) -> dict:
    key = jax.random.key(seed)
    ks = jax.random.split(key, 32)
    f32 = jnp.float32
    n_pages = PAST_LEN // PAGE_SIZE
    n_pool = (DEC_BATCH * n_pages * POOL_NUM) // POOL_DEN
    sw_buf = min(WINDOW_MAX, PAST_LEN)

    def w(k, shape, fan_in):
        return jax.random.normal(k, shape, f32) * fan_in ** -0.5

    def gain(k, shape):
        return 1.0 + 0.02 * jax.random.normal(k, shape, f32)

    page_table = jax.random.permutation(ks[6], n_pool)[:DEC_BATCH * n_pages].reshape(DEC_BATCH, n_pages).astype(jnp.int32)
    return {
        'x_prompt': jax.random.normal(ks[0], (BATCH, SEQ, D_MODEL), f32),
        'x_sample': jax.random.normal(ks[1], (DEC_BATCH, DEC_SEQ, D_MODEL), f32),
        'cache_kv_latent': jax.random.normal(ks[2], (DEPTH, n_pool, PAGE_SIZE, KV_LORA), f32),
        'cache_k_rope': jax.random.normal(ks[3], (DEPTH, n_pool, PAGE_SIZE, QK_ROPE), f32),
        'state_sw_k': jax.random.normal(ks[4], (DEPTH, DEC_BATCH, sw_buf, SW_HEADS, SW_DIM), f32),
        'state_sw_v': jax.random.normal(ks[5], (DEPTH, DEC_BATCH, sw_buf, SW_HEADS, SW_DIM), f32),
        'page_table': page_table,
        'norm_mix': gain(ks[7], (DEPTH, D_MODEL)),
        'w_in': w(ks[8], (DEPTH, D_MODEL, IN_WIDTH), D_MODEL),
        'norm_q_latent': gain(ks[9], (DEPTH, Q_LORA)),
        'norm_kv_latent': gain(ks[10], (DEPTH, KV_LORA)),
        'w_uq': w(ks[11], (DEPTH, Q_LORA, MLA_HEADS, QK_NOPE + QK_ROPE), Q_LORA),
        'w_uk': w(ks[12], (DEPTH, KV_LORA, MLA_HEADS, QK_NOPE), KV_LORA),
        'w_uv': w(ks[13], (DEPTH, KV_LORA, MLA_HEADS, V_DIM), KV_LORA),
        'norm_out_mla': gain(ks[14], (DEPTH, MLA_WIDTH)),
        'norm_out_sw': gain(ks[15], (DEPTH, SW_WIDTH)),
        'w_out': w(ks[16], (DEPTH, MIX_WIDTH, D_MODEL), MIX_WIDTH),
        'norm_ffn': gain(ks[17], (DEPTH, D_MODEL)),
        'w_router_group': w(ks[18], (DEPTH, D_MODEL, N_GROUPS), D_MODEL),
        'b_router_group': 0.01 * jax.random.normal(ks[19], (DEPTH, N_GROUPS), f32),
        'w_router_expert': w(ks[20], (DEPTH, D_MODEL, N_EXPERTS), D_MODEL),
        'b_router_expert': 0.01 * jax.random.normal(ks[21], (DEPTH, N_EXPERTS), f32),
        'w_expert_gate': w(ks[22], (DEPTH, N_EXPERTS, D_MODEL, D_EXPERT), D_MODEL),
        'w_expert_up': w(ks[23], (DEPTH, N_EXPERTS, D_MODEL, D_EXPERT), D_MODEL),
        'w_expert_down': w(ks[24], (DEPTH, N_EXPERTS, D_EXPERT, D_MODEL), D_EXPERT),
        'norm_final': gain(ks[25], (D_MODEL,)),
    }

def reference(x_prompt, x_sample, cache_kv_latent, cache_k_rope, state_sw_k, state_sw_v, page_table,
              norm_mix, w_in, norm_q_latent, norm_kv_latent, w_uq, w_uk, w_uv, norm_out_mla, norm_out_sw, w_out,
              norm_ffn, w_router_group, b_router_group, w_router_expert, b_router_expert,
              w_expert_gate, w_expert_up, w_expert_down, norm_final):
    s = x_prompt.shape[1]
    t = x_sample.shape[1]
    past_len = page_table.shape[1] * cache_kv_latent.shape[2]
    pos_p = jnp.arange(s, dtype=jnp.float32)
    pos_s = past_len + jnp.arange(t, dtype=jnp.float32)
    slopes = alibi_slopes(SW_HEADS)
    sw_keep = min(WINDOW_MAX, s)
    hp, hs = x_prompt, x_sample
    kvp, krp, swkp, swvp, kvs, krs, swks, swvs = [], [], [], [], [], [], [], []
    for l in range(DEPTH):
        q_n, q_r, c_kv, k_r, q_sw, k_sw, v_sw = mixer_inputs(hp, pos_p, norm_mix[l], w_in[l], norm_q_latent[l], norm_kv_latent[l], w_uq[l])
        o_a = mla_prompt(q_n, q_r, c_kv, k_r, w_uk[l], w_uv[l])
        o_b = dilated_prompt(q_sw, k_sw, v_sw, slopes)
        hp = hp + mix_output(o_a, o_b, norm_out_mla[l], norm_out_sw[l], w_out[l])
        hp = hp + hier_moe(hp, norm_ffn[l], w_router_group[l], b_router_group[l], w_router_expert[l], b_router_expert[l],
                           w_expert_gate[l], w_expert_up[l], w_expert_down[l])
        kvp.append(c_kv)
        krp.append(k_r)
        swkp.append(k_sw[:, s - sw_keep:])
        swvp.append(v_sw[:, s - sw_keep:])
        q_n, q_r, c_kv, k_r, q_sw, k_sw, v_sw = mixer_inputs(hs, pos_s, norm_mix[l], w_in[l], norm_q_latent[l], norm_kv_latent[l], w_uq[l])
        o_a = mla_sample(q_n, q_r, c_kv, k_r, cache_kv_latent[l], cache_k_rope[l], page_table, w_uk[l], w_uv[l])
        o_b, new_k, new_v = dilated_sample(q_sw, k_sw, v_sw, state_sw_k[l], state_sw_v[l], slopes)
        hs = hs + mix_output(o_a, o_b, norm_out_mla[l], norm_out_sw[l], w_out[l])
        hs = hs + hier_moe(hs, norm_ffn[l], w_router_group[l], b_router_group[l], w_router_expert[l], b_router_expert[l],
                           w_expert_gate[l], w_expert_up[l], w_expert_down[l])
        kvs.append(c_kv)
        krs.append(k_r)
        swks.append(new_k)
        swvs.append(new_v)
    y_prompt = rmsnorm(hp, norm_final)
    y_sample = rmsnorm(hs, norm_final)
    kv_latent_prompt = jnp.stack(kvp)
    k_rope_prompt = jnp.stack(krp)
    sw_k_prompt = jnp.stack(swkp)
    sw_v_prompt = jnp.stack(swvp)
    kv_latent_sample = jnp.stack(kvs)
    k_rope_sample = jnp.stack(krs)
    sw_k_sample = jnp.stack(swks)
    sw_v_sample = jnp.stack(swvs)
    return (y_prompt, y_sample, kv_latent_prompt, k_rope_prompt, sw_k_prompt, sw_v_prompt,
            kv_latent_sample, k_rope_sample, sw_k_sample, sw_v_sample)


_drawn_inputs = setup_inputs


def setup_inputs(seed=0):
    import zlib

    import numpy as np

    out = dict(_drawn_inputs(seed))
    spreads = {}
    factors = {'norm_q_latent': 3.553,
     'norm_out_mla': 11.52,
     'norm_out_sw': 10.712,
     'b_router_group': 22.462,
     'b_router_expert': 37.752,
     'norm_final': 7.831,
     'norm_ffn': 4.899}
    for name, (base, spread) in spreads.items():
        noise = np.random.default_rng([zlib.crc32(name.encode()), seed]).standard_normal(out[name].shape)
        drawn = base * np.exp(spread * noise) if base else spread * noise
        out[name] = __import__('jax').numpy.asarray(drawn.astype(out[name].dtype))
    for name, factor in factors.items():
        out[name] = (out[name] * factor).astype(out[name].dtype)
    return out
```

```python
from contextlib import ExitStack
import math

import concourse.bass as bass
from concourse import mybir

F32 = mybir.dt.float32
I32 = mybir.dt.int32
U32 = mybir.dt.uint32
ALU = mybir.AluOpType
ACT = mybir.ActivationFunctionType
AX = mybir.AxisListType

P = 128
D_MODEL = 1024
SEQ = 1024
DEC_BATCH, DEC_SEQ = 8, 8
N_SAMPLE = DEC_BATCH * DEC_SEQ
PROMPT_TILES = SEQ // P
TILES = PROMPT_TILES + 1
ROWS = TILES * P
PAST_LEN = 8192
PAGE = 128
N_PAGES = PAST_LEN // PAGE
HEADS = 8
Q_LORA, KV_LORA, NOPE, ROPE = 192, 128, 64, 32
QK = NOPE + ROPE
V_DIM = 64
HALF = ROPE // 2
MLA_SCALE = QK ** -0.5
SW_SCALE = 64 ** -0.5
SW_WIDTH = 512
LATENTS = Q_LORA + KV_LORA + ROPE
IN_WIDTH = LATENTS + 3 * SW_WIDTH
WINDOW = 2048
PATTERNS = ((128, 1), (512, 4), (2048, 16))
EPS = 1e-6
MASK = -1e30
KC = D_MODEL // P
GROUPS, PER_GROUP, EXPERTS, TOP_K = 4, 8, 32, 2
D_EXPERT = 512
FC = D_EXPERT // P
N_TOKENS = SEQ + N_SAMPLE
MAX_BLOCKS = -(-N_TOKENS * TOP_K // P) + EXPERTS
OLD_J = (WINDOW - 512) // 16
OLD_KEYS = OLD_J * DEC_SEQ
NEAR_TILES = 512 // P
WIN_KEYS = OLD_KEYS + 512
WIN_ALL = WIN_KEYS + DEC_SEQ


class Chain:

    def __init__(self, eng, sem, base=0):
        self.eng, self.sem, self.base, self.n = eng, sem, base, 0

    def link(self, ins):
        self.n += 1
        ins.then_inc(self.sem, 1)
        self.eng.wait_ge(self.sem, self.base + self.n)


def after(eng, sem, value):
    if not isinstance(value, int) or value > 0:
        eng.wait_ge(sem, value)


def wait_apart(eng, t, sem, value):
    eng.wait_ge(t["ident_in"], 16)
    eng.wait_ge(sem, value)


def stepped(eng, n):
    def run(step):
        step(0)
        with eng.Fori(1, n) as i:
            step(i)
    return run


def phase_semaphore(nc, sems, name):
    s = nc.alloc_semaphore(name)
    sems.append(s)
    return s


def row_broadcast(vector):
    return vector.partition_broadcast(P)


def project(nc, t, ident):
    with ExitStack() as ctx:
        def sb(name, shape, dt=F32):
            return ctx.enter_context(nc.sbuf_tensor(f"a_{name}", shape, dt))

        def sem(name):
            return phase_semaphore(nc, t["phase_sems"], f"a_{name}")

        w_in = sb("w_in", [P, KC, IN_WIDTH])
        w_uq0, w_uq1 = sb("w_uq0", [P, HEADS * QK]), sb("w_uq1", [Q_LORA - P, HEADS * QK])
        w_uk, w_uv = sb("w_uk", [P, 512]), sb("w_uv", [P, 512])
        g_mix, g_q, g_kv = sb("g_mix", [P, D_MODEL]), sb("g_q", [P, Q_LORA]), sb("g_kv", [P, KV_LORA])
        x, squares, xn = sb("x", [P, D_MODEL]), sb("squares", [P, D_MODEL]), sb("xn", [P, D_MODEL])
        x_t = sb("x_t", [P, KC, P])
        angles = sb("angles", [P, ROPE])
        stat, stat2 = sb("stat", [P, 3]), sb("stat2", [P, 6])
        cq, ckv, kr = sb("cq", [P, Q_LORA]), sb("ckv", [P, KV_LORA]), sb("kr", [P, ROPE])
        rot = sb("rot", [P, 4, HEADS, HALF])
        rot_k = sb("rot_k", [P, 4, HALF])
        cq_t0, cq_t1 = sb("cq_t0", [P, P]), sb("cq_t1", [Q_LORA - P, P])
        ckv_t, kr_t = sb("ckv_t", [P, P]), sb("kr_t", [ROPE, P])
        q = sb("q", [P, HEADS, QK])
        q_t, kn_t, v = sb("q_t", [QK, HEADS, P]), sb("kn_t", [P, 4, P]), sb("v", [P, 512])
        q_sw, k_sw, v_sw = sb("q_sw", [P, 512]), sb("k_sw", [P, 512]), sb("v_sw", [P, 512])
        q_sw_t, k_sw_t = sb("q_sw_t", [P, 4, P]), sb("k_sw_t", [P, 4, P])
        bank = [ctx.enter_context(nc.psum_tensor(f"a_bank{n}", [P, 512], F32)) for n in range(8)]
        proj = bank[0:4]
        turn0, turn1, up0, up1 = bank[4:8]

        def quarters(b, rows=P):
            return b[0:rows, :].rearrange("p (a c) -> p a c", a=4)

        weights_in = sem("weights_in")
        x_in, angles_in = sem("x_in"), sem("angles_in")
        x_squared, x_root, xn_done = sem("x_squared"), sem("x_root"), sem("xn_done")
        dve_link = sem("dve_link")
        x_turned, x_t_lo, x_t_hi = sem("x_turned"), sem("x_t_lo"), sem("x_t_hi")
        projected = sem("projected")
        lat_squared, lat_root, lat_normed, k_rotated = sem("lat_squared"), sem("lat_root"), sem("lat_normed"), sem("k_rotated")
        lat_turned, lat_t = sem("lat_turned"), sem("lat_t")
        q_up, kn_up, v_up = sem("q_up"), sem("kn_up"), sem("v_up")
        q_copied, q_rotated, kn_copied, v_copied = sem("q_copied"), sem("q_rotated"), sem("kn_copied"), sem("v_copied")
        q_sw_copied, k_sw_copied, v_sw_copied = sem("q_sw_copied"), sem("k_sw_copied"), sem("v_sw_copied")
        q_sw_turned, k_sw_turned, q_turned = sem("q_sw_turned"), sem("k_sw_turned"), sem("q_turned")
        q_sw_t_copied, k_sw_t_copied, q_t_lo, q_t_hi = sem("q_sw_t_copied"), sem("k_sw_t_copied"), sem("q_t_lo"), sem("q_t_hi")
        st = {n: sem(f"stored_{n}") for n in ("ckv", "kr", "k_sw", "v_sw", "q_t", "kn_t", "kr_t", "v", "q_sw_t", "k_sw_t")}
        N_W, LINKS = 9, 7
        block = ctx.enter_context(nc.Block())

        @block.sync
        def _(sp):
            def wait(sem, value):
                wait_apart(sp, t, sem, value)

            def load_x(row):
                sp.dma_start(x[:, :], t["x_all"][bass.ds(row, P), :]).then_inc(x_in, 16)
                sp.dma_start(angles[:, :], t["c_angles"][bass.ds(row, P), :]).then_inc(angles_in, 16)

            def store(done, row):
                at = bass.ds(row, P)
                wait(lat_normed, done)
                sp.dma_start(t["kv_all"][at, :], ckv[:, :]).then_inc(st["ckv"], 16)
                wait(k_rotated, done)
                sp.dma_start(t["kr_all"][at, :], kr[:, :]).then_inc(st["kr"], 16)
                wait(k_sw_copied, done)
                sp.dma_start(t["swk_all"][at, :], k_sw[:, :]).then_inc(st["k_sw"], 16)
                wait(v_sw_copied, done)
                sp.dma_start(t["swv_all"][at, :], v_sw[:, :]).then_inc(st["v_sw"], 16)
                wait(lat_t, done)
                sp.dma_start(t["kr_t"][:, at], kr_t[:, :]).then_inc(st["kr_t"], 16)
                wait(kn_copied, done)
                sp.dma_start(t["kn_t"].rearrange("(c p) n -> p c n", p=P)[:, :, at], kn_t[:, :, :]).then_inc(st["kn_t"], 16)
                wait(v_copied, done)
                sp.dma_start(t["v_mla"][at, :], v[:, :]).then_inc(st["v"], 16)
                wait(q_sw_t_copied, done)
                sp.dma_start(t["q_sw_t"].rearrange("(c p) n -> p c n", p=P)[:, :, at], q_sw_t[:, :, :]).then_inc(st["q_sw_t"], 16)
                wait(k_sw_t_copied, done)
                sp.dma_start(t["k_sw_t"].rearrange("(c p) n -> p c n", p=P)[:, :, at], k_sw_t[:, :, :]).then_inc(st["k_sw_t"], 16)
                wait(q_t_lo, done)
                wait(q_t_hi, done)
                sp.dma_start(t["q_t"].rearrange("h e n -> e h n")[:, :, at], q_t[:, :, :]).then_inc(st["q_t"], 16)

            load_x(0)
            sp.dma_start(g_mix[:, :], row_broadcast(t["norm_mix"])).then_inc(weights_in, 16)
            for k0 in (0, 4):
                sp.dma_start(w_in[:, k0:k0 + 4, :], t["w_in"].rearrange("(k p) n -> p k n", p=P)[:, k0:k0 + 4, :]).then_inc(weights_in, 16)
            sp.dma_start(w_uq0[:, :], t["w_uq"][0:P, :]).then_inc(weights_in, 16)
            sp.dma_start(w_uq1[:, :], t["w_uq"][P:Q_LORA, :]).then_inc(weights_in, 16)
            sp.dma_start(w_uk[:, :], t["w_uk"]).then_inc(weights_in, 16)
            sp.dma_start(w_uv[:, :], t["w_uv"]).then_inc(weights_in, 16)
            sp.dma_start(g_q[:, :], row_broadcast(t["norm_q_latent"])).then_inc(weights_in, 16)
            sp.dma_start(g_kv[:, :], row_broadcast(t["norm_kv_latent"])).then_inc(weights_in, 16)

            @stepped(sp, TILES - 1)
            def _(i):
                wait(xn_done, i + 1)
                wait(q_rotated, i + 1)
                load_x(i * P + P)
                store(i + 1, i * P)
            store(TILES, (TILES - 1) * P)
            for s in st.values():
                sp.wait_ge(s, 16 * TILES)

        @block.scalar
        def _(act):
            @stepped(act, TILES)
            def _(i):
                act.wait_ge(x_in, 16 * i + 16)
                nc.scalar.activation(squares[:, :], x[:, :], ACT.Square, accum_out=stat[:, 0:1]).then_inc(x_squared, 1)
                act.wait_ge(dve_link, LINKS * i + 1)
                nc.scalar.activation(stat[:, 2:3], stat[:, 1:2], ACT.Sqrt).then_inc(x_root, 1)
                act.wait_ge(x_turned, 2 * i + 2)
                nc.scalar.activation(x_t[:, 4:8, :], quarters(turn1), ACT.Copy).then_inc(x_t_hi, 1)
                act.wait_ge(projected, 4 * i + 1)
                nc.scalar.activation(squares[:, 0:Q_LORA], proj[0][:, 0:Q_LORA], ACT.Square, accum_out=stat2[:, 0:1]).then_inc(lat_squared, 1)
                nc.scalar.activation(squares[:, Q_LORA:Q_LORA + KV_LORA], proj[0][:, Q_LORA:Q_LORA + KV_LORA], ACT.Square,
                                     accum_out=stat2[:, 1:2]).then_inc(lat_squared, 1)
                act.wait_ge(dve_link, LINKS * i + 4)
                nc.scalar.activation(stat2[:, 4:6], stat2[:, 2:4], ACT.Sqrt).then_inc(lat_root, 1)
                act.wait_ge(projected, 4 * i + 2)
                nc.scalar.activation(q_sw[:, :], proj[1][:, :], ACT.Copy, scale=SW_SCALE).then_inc(q_sw_copied, 1)
                act.wait_ge(projected, 4 * i + 4)
                after(act, st["v_sw"], 16 * i)
                nc.scalar.activation(v_sw[:, :], proj[3][:, :], ACT.Copy).then_inc(v_sw_copied, 1)
                act.wait_ge(q_up, i + 1)
                nc.scalar.activation(q[:, 0:4, :], up0[:, 0:4 * QK].rearrange("p (h e) -> p h e", h=4), ACT.Copy,
                                     scale=MLA_SCALE).then_inc(q_copied, 1)
                nc.scalar.activation(q[:, 4:8, :], up1[:, 0:4 * QK].rearrange("p (h e) -> p h e", h=4), ACT.Copy,
                                     scale=MLA_SCALE).then_inc(q_copied, 1)
                act.wait_ge(v_up, i + 1)
                after(act, st["v"], 16 * i)
                nc.scalar.activation(v[:, :], proj[0][:, :], ACT.Copy).then_inc(v_copied, 1)
                act.wait_ge(k_sw_turned, i + 1)
                after(act, st["k_sw_t"], 16 * i)
                nc.scalar.activation(k_sw_t[:, :, :], quarters(turn1), ACT.Copy).then_inc(k_sw_t_copied, 1)
                act.wait_ge(q_turned, 2 * i + 2)
                after(act, st["q_t"], 16 * i)
                nc.scalar.activation(q_t[:, 4:8, :], quarters(up1, QK), ACT.Copy).then_inc(q_t_hi, 1)

        @block.vector
        def _(dve):
            v_ = nc.vector

            def rotate(link, out_lo, out_hi, lo, hi, cos, sin, tmp, final):
                v_.tensor_tensor(tmp[0], lo, cos, ALU.mult)
                v_.tensor_tensor(tmp[1], hi, sin, ALU.mult)
                v_.tensor_tensor(tmp[2], lo, sin, ALU.mult)
                link(v_.tensor_tensor(tmp[3], hi, cos, ALU.mult))
                v_.tensor_tensor(out_lo, tmp[0], tmp[1], ALU.subtract)
                v_.tensor_tensor(out_hi, tmp[2], tmp[3], ALU.add).then_inc(final, 1)

            @stepped(dve, TILES)
            def _(i):
                chain = Chain(dve, dve_link, LINKS * i)
                link = chain.link
                dve.wait_ge(x_squared, i + 1)
                link(v_.tensor_scalar(stat[:, 1:2], stat[:, 0:1], 1.0 / D_MODEL, EPS, ALU.mult, ALU.add))
                dve.wait_ge(x_root, i + 1)
                link(v_.reciprocal(stat[:, 0:1], stat[:, 2:3]))
                dve.wait_ge(weights_in, 16 * N_W)
                after(dve, x_turned, 2 * i)
                v_.scalar_tensor_tensor(xn[:, :], x[:, :], stat[:, 0:1], g_mix[:, :], ALU.mult, ALU.mult).then_inc(xn_done, 1)
                dve.wait_ge(x_turned, 2 * i + 1)
                v_.tensor_copy(x_t[:, 0:4, :], quarters(turn0)).then_inc(x_t_lo, 1)
                dve.wait_ge(lat_squared, 2 * i + 2)
                link(v_.tensor_scalar(stat2[:, 2:3], stat2[:, 0:1], 1.0 / Q_LORA, EPS, ALU.mult, ALU.add))
                link(v_.tensor_scalar(stat2[:, 3:4], stat2[:, 1:2], 1.0 / KV_LORA, EPS, ALU.mult, ALU.add))
                dve.wait_ge(lat_root, i + 1)
                link(v_.reciprocal(stat2[:, 0:2], stat2[:, 4:6]))
                after(dve, st["ckv"], 16 * i)
                after(dve, lat_turned, i)
                v_.scalar_tensor_tensor(cq[:, :], proj[0][:, 0:Q_LORA], stat2[:, 0:1], g_q[:, :], ALU.mult, ALU.mult)
                v_.scalar_tensor_tensor(ckv[:, :], proj[0][:, Q_LORA:Q_LORA + KV_LORA], stat2[:, 1:2], g_kv[:, :],
                                        ALU.mult, ALU.mult).then_inc(lat_normed, 1)
                dve.wait_ge(angles_in, 16 * i + 16)
                after(dve, st["kr"], 16 * i)
                k0 = Q_LORA + KV_LORA
                rotate(link, kr[:, 0:HALF], kr[:, HALF:ROPE], proj[0][:, k0:k0 + HALF], proj[0][:, k0 + HALF:k0 + ROPE],
                       angles[:, 0:HALF], angles[:, HALF:ROPE], [rot_k[:, n, :] for n in range(4)], k_rotated)
                dve.wait_ge(projected, 4 * i + 3)
                after(dve, st["k_sw"], 16 * i)
                after(dve, k_sw_turned, i)
                v_.tensor_copy(k_sw[:, :], proj[2][:, :]).then_inc(k_sw_copied, 1)
                dve.wait_ge(lat_turned, i + 1)
                after(dve, st["kr_t"], 16 * i)
                v_.tensor_copy(cq_t0[:, :], turn0[:, 0:P])
                v_.tensor_copy(cq_t1[:, :], turn0[0:Q_LORA - P, P:2 * P])
                v_.tensor_copy(ckv_t[:, :], turn0[:, 2 * P:3 * P])
                v_.tensor_copy(kr_t[:, :], turn0[0:ROPE, 3 * P:4 * P]).then_inc(lat_t, 1)
                dve.wait_ge(kn_up, i + 1)
                after(dve, st["kn_t"], 16 * i)
                v_.tensor_copy(kn_t[:, :, :], quarters(turn1)).then_inc(kn_copied, 1)
                dve.wait_ge(q_copied, 2 * i + 2)
                cos = angles[:, 0:HALF].unsqueeze(1).broadcast_to([P, HEADS, HALF])
                sin = angles[:, HALF:ROPE].unsqueeze(1).broadcast_to([P, HEADS, HALF])
                rotate(link, q[:, :, NOPE:NOPE + HALF], q[:, :, NOPE + HALF:QK], q[:, :, NOPE:NOPE + HALF],
                       q[:, :, NOPE + HALF:QK], cos, sin, [rot[:, n, :, :] for n in range(4)], q_rotated)
                dve.wait_ge(q_sw_turned, i + 1)
                after(dve, st["q_sw_t"], 16 * i)
                v_.tensor_copy(q_sw_t[:, :, :], quarters(turn0)).then_inc(q_sw_t_copied, 1)
                dve.wait_ge(q_turned, 2 * i + 1)
                after(dve, st["q_t"], 16 * i)
                v_.tensor_copy(q_t[:, 0:4, :], quarters(up0, QK)).then_inc(q_t_lo, 1)
                assert chain.n == LINKS

        @block.tensor
        def _(pe):
            mm, turn = nc.tensor.matmul, nc.tensor.transpose

            def turns(out_bank, src, step=P, rows=P):
                for a in range(4):
                    last = turn(quarters(out_bank, rows)[:, a, :], src(a), ident[:, :])
                return last

            pe.wait_ge(weights_in, 16 * N_W)
            @stepped(pe, TILES)
            def _(i):
                pe.wait_ge(xn_done, i + 1)
                after(pe, q_sw_t_copied, i)
                turns(turn0, lambda a: xn[:, a * P:(a + 1) * P]).then_inc(x_turned, 1)
                after(pe, k_sw_t_copied, i)
                turns(turn1, lambda a: xn[:, (4 + a) * P:(5 + a) * P]).then_inc(x_turned, 1)
                pe.wait_ge(x_t_lo, i + 1)
                pe.wait_ge(x_t_hi, i + 1)
                cols = [(0, LATENTS)] + [(LATENTS + n * 512, 512) for n in range(3)]
                for n, free in enumerate((v_copied, q_sw_copied, k_sw_copied, v_sw_copied)):
                    after(pe, free, i)
                    c0, width = cols[n]
                    for k in range(KC):
                        last = mm(proj[n][:, 0:width], x_t[:, k, :], w_in[:, k, c0:c0 + width], start=(k == 0), stop=(k == KC - 1))
                    last.then_inc(projected, 1)
                pe.wait_ge(lat_normed, i + 1)
                pe.wait_ge(k_rotated, i + 1)
                turn(turn0[:, 0:P], cq[:, 0:P], ident[:, :])
                turn(turn0[0:Q_LORA - P, P:2 * P], cq[:, P:Q_LORA], ident[:, :])
                turn(turn0[:, 2 * P:3 * P], ckv[:, :], ident[:, :])
                turn(turn0[0:ROPE, 3 * P:4 * P], kr[:, :], ident[:, :]).then_inc(lat_turned, 1)
                pe.wait_ge(lat_t, i + 1)
                after(pe, q_t_lo, i)
                after(pe, q_t_hi, i)
                for n, out in enumerate((up0, up1)):
                    at = slice(n * 4 * QK, (n + 1) * 4 * QK)
                    mm(out[:, 0:4 * QK], cq_t0[:, :], w_uq0[:, at], start=True, stop=False)
                    last = mm(out[:, 0:4 * QK], cq_t1[:, :], w_uq1[:, at], start=False, stop=True)
                last.then_inc(q_up, 1)
                for a in range(4):
                    last = mm(turn1[:, a * P:(a + 1) * P], w_uk[:, a * P:(a + 1) * P], ckv_t[:, :], start=True, stop=True)
                last.then_inc(kn_up, 1)
                mm(proj[0][:, :], ckv_t[:, :], w_uv[:, :], start=True, stop=True).then_inc(v_up, 1)
                pe.wait_ge(q_sw_copied, i + 1)
                turns(turn0, lambda a: q_sw[:, a * P:(a + 1) * P]).then_inc(q_sw_turned, 1)
                pe.wait_ge(k_sw_copied, i + 1)
                pe.wait_ge(kn_copied, i + 1)
                turns(turn1, lambda a: k_sw[:, a * P:(a + 1) * P]).then_inc(k_sw_turned, 1)
                pe.wait_ge(q_rotated, i + 1)
                turns(up0, lambda a: q[:, a, :], rows=QK).then_inc(q_turned, 1)
                turns(up1, lambda a: q[:, 4 + a, :], rows=QK).then_inc(q_turned, 1)


def attend_prompt(nc, t, ident):
    with ExitStack() as ctx:
        def sb(name, shape, dt=F32):
            return ctx.enter_context(nc.sbuf_tensor(f"b_{name}", shape, dt))

        def pair(name, shape):
            return [sb(f"{name}{n}", shape) for n in range(2)]

        q_t, k_t = pair("q_t", [QK, SEQ]), pair("k_t", [QK, SEQ])
        v = pair("v", [P, PROMPT_TILES, 64])
        bias = pair("bias", [P, SEQ])
        scores, probs_t = pair("scores", [P, SEQ]), pair("probs_t", [P, PROMPT_TILES, P])
        out = pair("out", [P, PROMPT_TILES, 64])
        top, low = sb("top", [P, 16]), sb("low", [P, 16])
        total, inverse = sb("total", [P, 16]), sb("inverse", [P, 16])
        carrier = sb("carrier", [1, 1])
        score_bank = [ctx.enter_context(nc.psum_tensor(f"b_scorebank{n}", [P, SEQ], F32)) for n in range(2)]
        turn = [ctx.enter_context(nc.psum_tensor(f"b_turn{n}", [P, 4, P], F32)) for n in range(2)]
        out_bank = [ctx.enter_context(nc.psum_tensor(f"b_sum{n}", [P, 512], F32)) for n in range(2)]

        STEPS = [(u, tile) for u in range(2) for tile in range(PROMPT_TILES)]
        N = len(STEPS)
        WIDE = [s for s, (_, tile) in enumerate(STEPS) if tile >= 4]

        for kind in ("latent", "window"):
            latent = kind == "latent"
            dim = QK if latent else 64

            def sem(name):
                return nc.alloc_semaphore(f"b_{kind}_{name}")

            shared_in = sem("shared_in")
            head_in = [sem("head0_in"), sem("head1_in")]
            scored, maxed, lowered, exped, inverted = sem("scored"), sem("maxed"), sem("lowered"), sem("exped"), sem("inverted")
            turned0, turned1, copied0, copied1 = sem("turned0"), sem("turned1"), sem("copied0"), sem("copied1")
            summed, normed = sem("summed"), sem("normed")
            stored = [sem("stored0"), sem("stored1")]
            LOADS = 3 if latent else 4

            def wide_before(s):
                return sum(1 for w in WIDE if w < s)

            with nc.Block() as block:
                @block.sync
                def _(sp):
                    if latent:
                        for u in range(2):
                            sp.dma_start(k_t[u][NOPE:QK, :], t["kr_t"][:, 0:SEQ]).then_inc(shared_in, 16)
                            sp.dma_start(bias[u][:, :], t["c_causal"][0]).then_inc(shared_in, 16)
                    values = (t["v_mla"] if latent else t["swv_all"]).rearrange("(a p) n -> p a n", p=P)

                    @stepped(sp, 4)
                    def _(i):
                        for u in range(2):
                            if not isinstance(i, int):
                                wait_apart(sp, t, summed, N * i - (N // 2) * (1 - u))
                            h = i * 2 + u
                            if latent:
                                sp.dma_start(q_t[u][:, :], t["q_t"][bass.ds(h, 1), :, 0:SEQ].rearrange("a e n -> e (a n)")).then_inc(head_in[u], 16)
                                sp.dma_start(k_t[u][0:NOPE, :], t["kn_t"][bass.ds(h * NOPE, NOPE), 0:SEQ]).then_inc(head_in[u], 16)
                            else:
                                sp.dma_start(q_t[u][0:64, :], t["q_sw_t"][bass.ds(h * 64, 64), 0:SEQ]).then_inc(head_in[u], 16)
                                sp.dma_start(k_t[u][0:64, :], t["k_sw_t"][bass.ds(h * 64, 64), 0:SEQ]).then_inc(head_in[u], 16)
                                sp.dma_start(bias[u][:, :], t["c_window"][bass.ds(h, 1), :, :].rearrange("a e n -> e (a n)")).then_inc(head_in[u], 16)
                            sp.dma_start(v[u][:, :, :], values[:, 0:PROMPT_TILES, bass.ds(h * 64, 64)]).then_inc(head_in[u], 16)

                @block.scalar
                def _(act):
                    o_cat = t["o_cat"].rearrange("(a p) n -> p a n", p=P)
                    new, old = ("sw_k_new", "state_sw_k") if latent else ("sw_v_new", "state_sw_v")

                    def copy_wide(act, i, s):
                        w = len(WIDE) * i + wide_before(s)
                        n = STEPS[s][1] - 3
                        act.wait_ge(turned1, w + 1)
                        after(act, summed, N * i + max(s - 1, 0))
                        nc.scalar.activation(probs_t[s % 2][:, 4:4 + n, :], turn[1][:, 0:n, :], ACT.Copy).then_inc(copied1, 1)

                    def store(act, i, u):
                        act.wait_ge(normed, N * i + PROMPT_TILES * (u + 1))
                        at = i * 128 + (u * 64 + (0 if latent else 512))
                        act.dma_start(o_cat[:, 0:PROMPT_TILES, bass.ds(at, 64)], out[u][:, :, :]).then_inc(stored[u], 16)

                    @stepped(act, 4)
                    def _(i):
                        for u in range(2):
                            act.dma_start(t[new][bass.ds(2 * i + u, 1), 0:WINDOW - DEC_SEQ, :].rearrange("b (a n) f -> (b a) (n f)", a=120),
                                          t[old][bass.ds(2 * i + u, 1), DEC_SEQ:WINDOW, :].rearrange("b (a n) f -> (b a) (n f)", a=120)).then_inc(t["shifted"], 16)
                        for s, (u, tile) in enumerate(STEPS):
                            b, width = s % 2, P * (tile + 1)
                            act.wait_ge(lowered, N * i + s + 1)
                            nc.scalar.activation(scores[b][:, 0:width], scores[b][:, 0:width], ACT.Exp, bias=low[:, s:s + 1],
                                                 accum_out=total[:, s:s + 1]).then_inc(exped, 1)
                            if s >= 1 and STEPS[s - 1][1] >= 4:
                                copy_wide(act, i, s - 1)
                            if s == 9:
                                store(act, i, 0)
                        copy_wide(act, i, N - 1)
                        store(act, i, 1)

                    for u in range(2):
                        act.wait_ge(stored[u], 16 * 4)

                @block.vector
                def _(dve):
                    v_ = nc.vector

                    def copy_first(i, s):
                        n = min(STEPS[s][1] + 1, 4)
                        dve.wait_ge(turned0, N * i + s + 1)
                        after(dve, summed, N * i + max(s - 1, 0))
                        v_.tensor_copy(probs_t[s % 2][:, 0:n, :], turn[0][:, 0:n, :]).then_inc(copied0, 1)

                    def norm(i, s):
                        u, tile = STEPS[s]
                        dve.wait_ge(exped, N * i + s + 1)
                        v_.reciprocal(inverse[:, s:s + 1], total[:, s:s + 1]).then_inc(inverted, 1)
                        dve.wait_ge(inverted, N * i + s + 1)
                        dve.wait_ge(summed, N * i + s + 1)
                        if tile == 0:
                            after(dve, stored[u], 16 * i)
                        v_.tensor_scalar(out[u][:, tile, :], out_bank[s % 2][:, 0:64], inverse[:, s:s + 1], None, ALU.mult).then_inc(normed, 1)

                    @stepped(dve, 4)
                    def _(i):
                        dve.wait_ge(head_in[0], 16 * LOADS * i + 16 * LOADS)
                        if latent:
                            dve.wait_ge(shared_in, 16 * 4)
                        for s, (u, tile) in enumerate(STEPS):
                            b, width = s % 2, P * (tile + 1)
                            if s == PROMPT_TILES:
                                dve.wait_ge(head_in[1], 16 * LOADS * i + 16 * LOADS)
                            if s >= 2:
                                dve.wait_ge(turned0, N * i + s - 1)
                                if STEPS[s - 2][1] >= 4:
                                    dve.wait_ge(turned1, len(WIDE) * i + wide_before(s - 1))
                            dve.wait_ge(scored, N * i + s + 1)
                            v_.memset(carrier[:, :], 0.0)
                            v_.tensor_tensor_reduce(scores[b][:, 0:width], score_bank[b][:, 0:width], bias[u][:, SEQ - width:SEQ], 1.0, -3e38,
                                                    ALU.add, ALU.max, top[:, s:s + 1]).then_inc(maxed, 1)
                            dve.wait_ge(maxed, N * i + s + 1)
                            v_.tensor_scalar(low[:, s:s + 1], top[:, s:s + 1], -1.0, None, ALU.mult).then_inc(lowered, 1)
                            if s >= 1:
                                copy_first(i, s - 1)
                            if s >= 2:
                                norm(i, s - 2)
                        copy_first(i, N - 1)
                        norm(i, N - 2)
                        norm(i, N - 1)

                @block.tensor
                def _(pe):
                    mm, transpose = nc.tensor.matmul, nc.tensor.transpose

                    def score(i, s):
                        u, tile = STEPS[s]
                        if tile == 0:
                            pe.wait_ge(head_in[u], 16 * LOADS * i + 16 * LOADS)
                            if latent:
                                pe.wait_ge(shared_in, 16 * 4)
                        after(pe, maxed, N * i + max(s - 1, 0))
                        width = P * (tile + 1)
                        for c in range(0, width, 512):
                            w = min(512, width - c)
                            last = mm(score_bank[s % 2][:, c:c + w], q_t[u][0:dim, tile * P:(tile + 1) * P], k_t[u][0:dim, c:c + w],
                                      start=True, stop=True)
                        last.then_inc(scored, 1)

                    def turns(i, s):
                        tile = STEPS[s][1]
                        pe.wait_ge(exped, N * i + s + 1)
                        after(pe, copied0, N * i + s)
                        for k in range(min(tile + 1, 4)):
                            last = transpose(turn[0][:, k, :], scores[s % 2][:, k * P:(k + 1) * P], ident[:, :])
                        last.then_inc(turned0, 1)
                        if tile >= 4:
                            after(pe, copied1, len(WIDE) * i + wide_before(s))
                            for k in range(4, tile + 1):
                                last = transpose(turn[1][:, k - 4, :], scores[s % 2][:, k * P:(k + 1) * P], ident[:, :])
                            last.then_inc(turned1, 1)

                    def sums(i, s):
                        u, tile = STEPS[s]
                        pe.wait_ge(copied0, N * i + s + 1)
                        after(pe, normed, N * i + max(s - 1, 0))
                        for k in range(tile + 1):
                            if k == 4:
                                pe.wait_ge(copied1, len(WIDE) * i + wide_before(s) + 1)
                            last = mm(out_bank[s % 2][:, 0:64], probs_t[s % 2][:, k, :], v[u][:, k, :], start=(k == 0), stop=(k == tile))
                        last.then_inc(summed, 1)

                    @stepped(pe, 4)
                    def _(i):
                        score(i, 0)
                        for s in range(N):
                            if s + 1 < N:
                                score(i, s + 1)
                            turns(i, s)
                            if s >= 1:
                                sums(i, s - 1)
                        sums(i, N - 1)


CHUNKS = 4
TILES_CHUNK = 16
HT = HEADS * DEC_SEQ


def attend_latent(nc, t, ident):
    with ExitStack() as ctx:
        def sb(name, shape, dt=F32):
            return ctx.enter_context(nc.sbuf_tensor(f"lat_{name}", shape, dt))

        def sem(name):
            return phase_semaphore(nc, t["phase_sems"], f"lat_{name}")

        page_rows, page_part = sb("page_rows", [P, 4 * DEC_BATCH], I32), sb("page_part", [P, 1])
        gather_rows = sb("gather_rows", [P, 4 * DEC_BATCH], I32)
        rows_now = sb("rows_now", [P, CHUNKS], I32)
        kv = [sb(f"kv{c}", [P, TILES_CHUNK * KV_LORA]) for c in range(CHUNKS)]
        kr = [sb(f"kr{c}", [P, TILES_CHUNK * ROPE]) for c in range(CHUNKS)]
        kv_t = [sb(f"kv_t{n}", [P, TILES_CHUNK, P]) for n in range(2)]
        kr_t = [sb(f"kr_t{n}", [P, 4, P]) for n in range(2)]
        q_nope, q_rope = sb("q_nope", [NOPE, HEADS, N_SAMPLE]), sb("q_rope", [P, HEADS, N_SAMPLE])
        w_uk_t, w_uv = sb("w_uk_t", [NOPE, HEADS, KV_LORA]), sb("w_uv", [P, 512])
        q_lat = sb("q_lat", [P, DEC_BATCH, HT])
        q_pad = sb("q_pad", [P, DEC_BATCH, 4, HT])
        new_rows, new_t, new_kr_t = sb("new_rows", [N_SAMPLE, KV_LORA]), sb("new_t", [P, N_SAMPLE]), sb("new_kr_t", [ROPE, N_SAMPLE])
        new_kv, new_kv_now = sb("new_kv", [DEC_SEQ, DEC_BATCH, KV_LORA]), sb("new_kv_now", [DEC_SEQ, KV_LORA])
        new_mask, new_scores = sb("new_mask", [DEC_SEQ, HT]), sb("new_scores", [DEC_SEQ, DEC_BATCH, HT])
        scores = sb("scores", [P, CHUNKS * TILES_CHUNK + 1, HT])
        part_max, part_sum = sb("part_max", [P, CHUNKS + 1, HT]), sb("part_sum", [P, CHUNKS + 1, HT])
        all_max, all_sum = sb("all_max", [P, P]), sb("all_sum", [P, HT])
        carrier = sb("carrier", [P, 1])
        top, top_wide = sb("top", [HT, 1]), sb("top_wide", [HT, P])
        ones, inverse = sb("ones", [P, P]), sb("inverse", [P, HT])
        o_lat = sb("o_lat", [P, HEADS, DEC_BATCH, DEC_SEQ])
        out = sb("out", [N_SAMPLE, 512])

        def bank(name):
            return ctx.enter_context(nc.psum_tensor(f"lat_{name}", [P, 512], F32))

        turn, turn_kr = [bank("turn0"), bank("turn1")], bank("turn_kr")
        score_bank = [bank("score0"), bank("score1")]
        misc, out_bank = bank("misc"), bank("out_bank")
        max_t_bank, max_t, spread, total = misc[:, 0:P], misc[0:HT, 0:P], misc[:, P:P + HT], misc[:, P + HT:P + 2 * HT]

        inputs_in, rows_ready, rows_copied = sem("inputs_in"), sem("rows_ready"), sem("rows_copied")
        gathered_kv, gathered_kr = [sem(f"gathered_kv{c}") for c in range(CHUNKS)], [sem(f"gathered_kr{c}") for c in range(CHUNKS)]
        kr_turned, kr_copied = sem("kr_turned"), sem("kr_copied")
        even_turned, odd_turned, even_copied, odd_copied = sem("even_turned"), sem("odd_turned"), sem("even_copied"), sem("odd_copied")
        scored, score_copied = sem("scored"), sem("score_copied")
        maxed, max_turned, topped, top_spread = sem("maxed"), sem("max_turned"), sem("topped"), sem("top_spread")
        lowered, exped, summed_parts, totalled = sem("lowered"), sem("exped"), sem("summed_parts"), sem("totalled")
        used, weighted, normed = [sem(f"used{c}") for c in range(CHUNKS)], sem("weighted"), sem("normed")
        dve_link, new_placed, inverted = sem("dve_link"), sem("new_placed"), sem("inverted")
        q_lat_done, q_lat_copied, new_turned, new_t_copied, new_scored, q_padded = (
            sem("q_lat_done"), sem("q_lat_copied"), sem("new_turned"), sem("new_t_copied"), sem("new_scored"), sem("q_padded"))
        ones_set, out_done, out_copied, stored = sem("ones_set"), sem("out_done"), sem("out_copied"), sem("stored")
        sample = slice(SEQ, SEQ + N_SAMPLE)
        LINKS = 5
        N_IN = 13

        with nc.Block() as block:
            @block.sync
            def _(sp):
                def load(dst, src):
                    sp.dma_start(dst, src).then_inc(inputs_in, 16)

                load(page_rows[:, :], t["page_rows"])
                load(page_part[:, :], t["c_page_part"])
                load(q_nope[:, :, :], t["q_t"][:, 0:NOPE, sample].rearrange("h e n -> e h n"))
                load(w_uk_t[:, :, :], t["w_uk_t"])
                for u in range(4):
                    load(q_rope[u * ROPE:(u + 1) * ROPE, :, :], t["q_t"][:, NOPE:QK, sample].rearrange("h e n -> e h n"))
                load(new_rows[:, :], t["kv_all"][sample, :])
                load(new_kr_t[:, :], t["kr_t"][:, sample])
                load(new_kv[:, :, :], t["kv_all"][sample, :].rearrange("(b t) c -> t b c", t=DEC_SEQ))
                load(new_mask[:, :], t["c_new_mask"])
                load(w_uv[:, :], t["w_uv"])
                sp.wait_ge(out_copied, 1)
                sp.dma_start(t["o_cat"][sample, 0:512], out[:, :]).then_inc(stored, 16)
                sp.wait_ge(stored, 16)

            @block.gpsimd
            def _(gp):
                gp.wait_ge(rows_ready, 1)

                @stepped(gp, DEC_BATCH)
                def _(n):
                    for c in range(CHUNKS):
                        after(gp, used[c], n)
                        nc.gpsimd.tensor_copy(rows_now[:, c:c + 1], gather_rows[:, bass.ds(n * CHUNKS + c, 1)]).then_inc(rows_copied, 1)
                        gp.wait_ge(rows_copied, n * CHUNKS + (c + 1))
                        nc.gpsimd.tensor_tensor(carrier[:, 0:1], page_part[:, 0:1], page_part[:, 0:1], ALU.add)
                        offset = bass.IndirectOffsetOnAxis(ap=rows_now[:, c:c + 1], axis=0)
                        gp.indirect_dma_start(out=kv[c][:, :], out_offset=None, in_=t["cache_kv"], in_offset=offset).then_inc(gathered_kv[c], 16)
                        gp.indirect_dma_start(out=kr[c][:, :], out_offset=None, in_=t["cache_kr"], in_offset=offset).then_inc(gathered_kr[c], 16)

            @block.tensor
            def _(pe):
                mm, transpose = nc.tensor.matmul, nc.tensor.transpose
                pe.wait_ge(inputs_in, 16 * N_IN)
                for h in range(HEADS):
                    last = mm(score_bank[0][:, h * 64:(h + 1) * 64], w_uk_t[:, h, :], q_nope[:, h, :], start=True, stop=True)
                last.then_inc(q_lat_done, 1)
                transpose(score_bank[1][:, 0:N_SAMPLE], new_rows[:, :], ident[0:N_SAMPLE, 0:N_SAMPLE]).then_inc(new_turned, 1)
                pe.wait_ge(q_lat_copied, 1)
                pe.wait_ge(new_t_copied, 1)
                for b in range(DEC_BATCH):
                    at = slice(b * DEC_SEQ, (b + 1) * DEC_SEQ)
                    place = score_bank[1][0:DEC_SEQ, b * HT:(b + 1) * HT]
                    mm(place, new_t[:, at], q_lat[:, b, :], start=True, stop=False)
                    last = mm(place.rearrange("p (h t) -> p h t", h=HEADS), new_kr_t[:, at], q_rope[0:ROPE, :, at], start=False, stop=True)
                last.then_inc(new_scored, 1)
                pe.wait_ge(new_placed, 1)
                pe.wait_ge(q_padded, 1)
                pe.wait_ge(ones_set, 1)

                def turns(n, c):
                    pe.wait_ge(gathered_kr[c], 16 * n + 16)
                    after(pe, kr_copied, CHUNKS * n + c)
                    for g in range(4):
                        last = transpose(turn_kr[:, g * P:(g + 1) * P], kr[c][:, g * P:(g + 1) * P], ident[:, :])
                    last.then_inc(kr_turned, 1)
                    pe.wait_ge(gathered_kv[c], 16 * n + 16)
                    for g in range(4):
                        copied, turned = ((even_copied, even_turned), (odd_copied, odd_turned))[g % 2]
                        after(pe, copied, 2 * CHUNKS * n + (2 * c + g // 2))
                        for a in range(4):
                            u = 4 * g + a
                            last = transpose(turn[g % 2][:, a * P:(a + 1) * P], kv[c][:, u * P:(u + 1) * P], ident[:, :])
                        last.then_inc(turned, 1)

                def score(n, c):
                    pe.wait_ge(kr_copied, CHUNKS * n + (c + 1))
                    pe.wait_ge(even_copied, 2 * CHUNKS * n + (2 * c + 2))
                    pe.wait_ge(odd_copied, 2 * CHUNKS * n + (2 * c + 2))
                    for half in range(2):
                        after(pe, score_copied, 2 * CHUNKS * n + max(2 * c + half - 1, 0))
                        for g in (2 * half, 2 * half + 1):
                            place = score_bank[half][:, (g % 2) * 4 * HT:(g % 2 + 1) * 4 * HT]
                            mm(place, kr_t[c % 2][:, g, :], q_pad[:, bass.ds(n, 1), :, :].rearrange("p a u q -> p (a u q)"), start=True, stop=False,
                               skip_group_check=True)
                            for a in range(4):
                                last = mm(place[:, a * HT:(a + 1) * HT], kv_t[c % 2][:, 4 * g + a, :],
                                          q_lat[:, bass.ds(n, 1), :].rearrange("p a q -> p (a q)"), start=False, stop=(a == 3), skip_group_check=True)
                        last.then_inc(scored, 1)

                @stepped(pe, DEC_BATCH)
                def _(n):
                    turns(n, 0)
                    for c in range(CHUNKS):
                        if c + 1 < CHUNKS:
                            turns(n, c + 1)
                        score(n, c)
                    pe.wait_ge(maxed, n + 1)
                    transpose(max_t_bank, all_max[:, :], ident[:, :]).then_inc(max_turned, 1)
                    pe.wait_ge(topped, n + 1)
                    mm(spread, top_wide[:, :], ident[0:HT, 0:HT], start=True, stop=True).then_inc(top_spread, 1)
                    after(pe, normed, n)
                    for c in range(CHUNKS):
                        pe.wait_ge(exped, (CHUNKS + 1) * n + (c + 1))
                        for u in range(TILES_CHUNK):
                            last = mm(out_bank[:, 0:HT], kv[c][:, u * P:(u + 1) * P], scores[:, c * TILES_CHUNK + u, :],
                                      start=(c == 0 and u == 0), stop=False)
                        last.then_inc(used[c], 1)
                    pe.wait_ge(exped, (CHUNKS + 1) * n + (CHUNKS + 1))
                    mm(out_bank[:, 0:HT], new_kv_now[:, :], scores[0:DEC_SEQ, CHUNKS * TILES_CHUNK, :], start=False, stop=True).then_inc(weighted, 1)
                    pe.wait_ge(summed_parts, n + 1)
                    mm(total, ones[:, :], all_sum[:, :], start=True, stop=True).then_inc(totalled, 1)

                pe.wait_ge(normed, DEC_BATCH)
                for h in range(HEADS):
                    last = mm(score_bank[0][0:N_SAMPLE, h * 64:(h + 1) * 64], o_lat[:, h, :, :].rearrange("p b t -> p (b t)"),
                              w_uv[:, h * 64:(h + 1) * 64], start=True, stop=True)
                last.then_inc(out_done, 1)

            @block.scalar
            def _(act):
                copy = ACT.Copy

                def evacuate(n, c):
                    act.wait_ge(kr_turned, CHUNKS * n + (c + 1))
                    after(act, scored, 2 * CHUNKS * n + max(2 * c - 2, 0))
                    nc.scalar.activation(kr_t[c % 2][:, :, :], turn_kr[:, :].rearrange("p (g k) -> p g k", g=4), copy).then_inc(kr_copied, 1)
                    for g in (1, 3):
                        act.wait_ge(odd_turned, 2 * CHUNKS * n + (2 * c + g // 2 + 1))
                        nc.scalar.activation(kv_t[c % 2][:, 4 * g:4 * g + 4, :], turn[1][:, :].rearrange("p (g k) -> p g k", g=4), copy).then_inc(odd_copied, 1)

                @stepped(act, DEC_BATCH)
                def _(n):
                    evacuate(n, 0)
                    for c in range(CHUNKS):
                        if c + 1 < CHUNKS:
                            evacuate(n, c + 1)
                        if c == 0:
                            after(act, weighted, n)
                            after(act, summed_parts, n)
                        for half in range(2):
                            act.wait_ge(scored, 2 * CHUNKS * n + (2 * c + half + 1))
                            at = c * TILES_CHUNK + 8 * half
                            nc.scalar.activation(scores[:, at:at + 8, :], score_bank[half][:, :].rearrange("p (u q) -> p u q", u=8), copy).then_inc(score_copied, 1)
                    for c in range(CHUNKS + 1):
                        act.wait_ge(lowered, (CHUNKS + 1) * n + (c + 1))
                        at = slice(c * TILES_CHUNK, min((c + 1) * TILES_CHUNK, CHUNKS * TILES_CHUNK + 1))
                        nc.scalar.activation(scores[:, at, :], scores[:, at, :], ACT.Exp).then_inc(exped, 1)

            @block.vector
            def _(dve):
                v_ = nc.vector
                dve.wait_ge(inputs_in, 16 * N_IN)
                v_.tensor_scalar(gather_rows[:, :], page_rows[:, :], float(PAGE // TILES_CHUNK), page_part[:, 0:1], ALU.mult, ALU.add).then_inc(rows_ready, 1)
                v_.memset(ones[:, :], 1.0).then_inc(ones_set, 1)
                setup = Chain(dve, sem("setup_link"))
                setup.link(v_.memset(all_max[:, :], 0.0))
                setup.link(v_.memset(q_pad[:, :, :, :], 0.0))
                for u in range(4):
                    rows = slice(u * ROPE, (u + 1) * ROPE)
                    last = v_.tensor_copy(q_pad[rows, :, u, :].rearrange("p b (h t) -> p b h t", h=HEADS),
                                          q_rope[rows, :, :].rearrange("p h (b t) -> p b h t", b=DEC_BATCH))
                last.then_inc(q_padded, 1)
                dve.wait_ge(q_lat_done, 1)
                v_.tensor_copy(q_lat[:, :, :].rearrange("p b (h t) -> p b h t", h=HEADS),
                               score_bank[0][:, :].rearrange("p (h b t) -> p b h t", h=HEADS, b=DEC_BATCH)).then_inc(q_lat_copied, 1)
                dve.wait_ge(new_turned, 1)
                v_.tensor_copy(new_t[:, :], score_bank[1][:, 0:N_SAMPLE]).then_inc(new_t_copied, 1)
                dve.wait_ge(new_scored, 1)
                v_.tensor_tensor(new_scores[:, :, :], score_bank[1][0:DEC_SEQ, :].rearrange("p (b q) -> p b q", b=DEC_BATCH),
                                 new_mask[:, :].unsqueeze(1).broadcast_to([DEC_SEQ, DEC_BATCH, HT]), ALU.add).then_inc(new_placed, 1)
                dve.wait_ge(new_placed, 1)
                NEW = CHUNKS * TILES_CHUNK

                def evacuate(n, c):
                    after(dve, scored, 2 * CHUNKS * n + max(2 * c - 2, 0))
                    for g in (0, 2):
                        dve.wait_ge(even_turned, 2 * CHUNKS * n + (2 * c + g // 2 + 1))
                        v_.tensor_copy(kv_t[c % 2][:, 4 * g:4 * g + 4, :], turn[0][:, :].rearrange("p (g k) -> p g k", g=4)).then_inc(even_copied, 1)

                def chunk(c):
                    return scores[:, c * TILES_CHUNK:(c + 1) * TILES_CHUNK, :]

                def by_column(ap):
                    return ap.rearrange("p u q -> p q u")

                @stepped(dve, DEC_BATCH)
                def _(n):
                    link = Chain(dve, dve_link, LINKS * n).link
                    after(dve, weighted, n)
                    after(dve, totalled, n)
                    v_.tensor_copy(new_kv_now[:, :], new_kv[:, bass.ds(n, 1), :].rearrange("p a c -> p (a c)"))
                    link(v_.memset(scores[:, NEW, :], MASK))
                    link(v_.tensor_copy(scores[0:DEC_SEQ, NEW, :], new_scores[:, bass.ds(n, 1), :].rearrange("p a q -> p (a q)")))
                    v_.tensor_copy(part_max[:, CHUNKS, :], scores[:, NEW, :])
                    evacuate(n, 0)
                    for c in range(CHUNKS):
                        if c + 1 < CHUNKS:
                            evacuate(n, c + 1)
                        dve.wait_ge(score_copied, 2 * CHUNKS * n + (2 * c + 2))
                        last = v_.tensor_reduce(part_max[:, c, :], by_column(chunk(c)), AX.X, ALU.max)
                    link(last)
                    v_.tensor_reduce(all_max[:, 0:HT], by_column(part_max[:, :, :]), AX.X, ALU.max).then_inc(maxed, 1)
                    dve.wait_ge(max_turned, n + 1)
                    link(v_.tensor_reduce(top[:, :], max_t, AX.X, ALU.max))
                    v_.tensor_copy(top_wide[:, :], top[:, 0:1].broadcast_to([HT, P])).then_inc(topped, 1)
                    dve.wait_ge(top_spread, n + 1)
                    for c in range(CHUNKS):
                        v_.tensor_tensor(chunk(c), chunk(c), spread.unsqueeze(1).broadcast_to([P, TILES_CHUNK, HT]), ALU.subtract).then_inc(lowered, 1)
                    v_.tensor_tensor(scores[:, NEW, :], scores[:, NEW, :], spread, ALU.subtract).then_inc(lowered, 1)
                    for c in range(CHUNKS):
                        dve.wait_ge(exped, (CHUNKS + 1) * n + (c + 1))
                        v_.tensor_reduce(part_sum[:, c, :], by_column(chunk(c)), AX.X, ALU.add)
                    dve.wait_ge(exped, (CHUNKS + 1) * n + (CHUNKS + 1))
                    link(v_.tensor_copy(part_sum[:, CHUNKS, :], scores[:, NEW, :]))
                    v_.tensor_reduce(all_sum[:, :], by_column(part_sum[:, :, :]), AX.X, ALU.add).then_inc(summed_parts, 1)
                    dve.wait_ge(totalled, n + 1)
                    v_.reciprocal(inverse[:, :], total).then_inc(inverted, 1)
                    dve.wait_ge(inverted, n + 1)
                    v_.tensor_tensor(o_lat[:, :, bass.ds(n, 1), :].rearrange("p h a t -> p h (a t)"), out_bank[:, 0:HT].rearrange("p (h t) -> p h t", h=HEADS),
                                     inverse[:, :].rearrange("p (h t) -> p h t", h=HEADS), ALU.mult).then_inc(normed, 1)

                dve.wait_ge(out_done, 1)
                v_.tensor_copy(out[:, :], score_bank[0][0:N_SAMPLE, :]).then_inc(out_copied, 1)


def attend_window(nc, t, ident):
    with ExitStack() as ctx:
        def sb(name, shape, dt=F32):
            return ctx.enter_context(nc.sbuf_tensor(f"win_{name}", shape, dt))

        def sem(name):
            return phase_semaphore(nc, t["phase_sems"], f"win_{name}")

        bias, own_head = sb("bias", [HT, WIN_ALL]), sb("own_head", [HT, 512])
        q_heads = sb("q_heads", [P, 4, N_SAMPLE])
        q_all = sb("q_all", [P, DEC_BATCH, 4, HT])
        q_now = sb("q_now", [P, 4, HT])
        k_t = sb("k_t", [P, 4, WIN_ALL])
        v_old, v_near, v_new = sb("v_old", [OLD_J, DEC_SEQ, 512]), sb("v_near", [P, NEAR_TILES, 512]), sb("v_new", [DEC_SEQ, 512])
        scores = sb("scores", [P, WIN_ALL])
        top, low, total, inverse = sb("top", [HT, 1]), sb("low", [HT, 1]), sb("total", [HT, 1]), sb("inverse", [HT, 1])
        OLD, NEAR = DEC_SEQ, NEAR_TILES
        probs_t = sb("probs_t", [P, OLD + NEAR + 1, HT])
        own, out = sb("own", [HT, HEADS, 64]), sb("out", [HT, 64])
        carrier = sb("carrier", [1, 1])
        score_bank = ctx.enter_context(nc.psum_tensor("win_score_bank", [P, 1536], F32))
        turn_old = ctx.enter_context(nc.psum_tensor("win_turn_old", [P, 512], F32))
        turn_near = ctx.enter_context(nc.psum_tensor("win_turn_near", [P, 512], F32))
        sum_bank = ctx.enter_context(nc.psum_tensor("win_sum_bank", [P, 512], F32))

        inputs_in, keys_in, values_in = sem("inputs_in"), sem("keys_in"), sem("values_in")
        q_placed, q_copied = sem("q_placed"), sem("q_copied")
        scored, maxed, lowered, exped = sem("scored"), sem("maxed"), sem("lowered"), sem("exped")
        turned_old, turned_near, copied_old, copied_near = sem("turned_old"), sem("turned_near"), sem("copied_old"), sem("copied_near")
        summed, masked, normed, stored, dve_link = sem("summed"), sem("masked"), sem("normed"), sem("stored"), sem("dve_link")
        sample = slice(SEQ, SEQ + N_SAMPLE)
        N_IN, K_IN, V_IN, LINKS = 3, 2, 3, 2
        PIECES = [(0, 512), (512, 512), (1024, WIN_ALL - 1024)]
        OLD_END = OLD_KEYS

        with nc.Block() as block:
            @block.sync
            def _(sp):
                sp.dma_start(bias[:, :], t["c_window_sample"]).then_inc(inputs_in, 16)
                sp.dma_start(own_head[:, :], t["c_own_head"]).then_inc(inputs_in, 16)
                sp.dma_start(q_heads[:, :, :], t["q_sw_t"][:, sample].rearrange("(c p) n -> p c n", p=P)).then_inc(inputs_in, 16)
                old_rows = t["state_sw_v"].rearrange("b (j r) f -> b j r f", r=16)
                near_rows = t["state_sw_v"].rearrange("b (a p) f -> b p a f", p=P)
                new_k = t["k_sw_t"].rearrange("(c p) n -> p c n", p=P)

                @stepped(sp, DEC_BATCH)
                def _(n):
                    if not isinstance(n, int):
                        wait_apart(sp, t, scored, n)
                    one = bass.ds(n, 1)
                    sp.dma_start(k_t[:, :, 0:WIN_KEYS], t["window_k_t"][one, :, :, :].rearrange("b p c n -> p (b c) n")).then_inc(keys_in, 16)
                    sp.dma_start(k_t[:, :, WIN_KEYS:WIN_ALL], new_k[:, :, bass.ds(n * DEC_SEQ + SEQ, DEC_SEQ)]).then_inc(keys_in, 16)
                    if not isinstance(n, int):
                        wait_apart(sp, t, summed, n)
                    sp.dma_start(v_old[:, :, :], old_rows[one, 0:OLD_J, 0:DEC_SEQ, :].rearrange("b j r f -> (b j) r f")).then_inc(values_in, 16)
                    sp.dma_start(v_near[:, :, :], near_rows[one, :, WINDOW // P - NEAR_TILES:WINDOW // P, :].rearrange("b p a f -> (b p) a f")).then_inc(values_in, 16)
                    sp.dma_start(v_new[:, :], t["swv_all"][bass.ds(n * DEC_SEQ + SEQ, DEC_SEQ), :]).then_inc(values_in, 16)

            @block.tensor
            def _(pe):
                mm, transpose = nc.tensor.matmul, nc.tensor.transpose

                @stepped(pe, DEC_BATCH)
                def _(n):
                    pe.wait_ge(keys_in, 16 * K_IN * n + 16 * K_IN)
                    pe.wait_ge(q_copied, n + 1)
                    after(pe, maxed, n)
                    for c0, width in PIECES:
                        for c in range(4):
                            last = mm(score_bank[0:HT, c0:c0 + width], q_now[:, c, :], k_t[:, c, c0:c0 + width], start=(c == 0), stop=(c == 3))
                    last.then_inc(scored, 1)
                    pe.wait_ge(exped, n + 1)
                    after(pe, copied_near, n)
                    after(pe, copied_old, n)
                    transpose(turn_near[:, 0:P], scores[:, OLD_END:OLD_END + P], ident[:, :])
                    for r in range(1, NEAR):
                        at = OLD_END + r * P
                        transpose(turn_near[:, r * HT:(r + 1) * HT], scores[0:HT, at:at + P], ident[0:HT, 0:HT])
                    transpose(turn_near[0:DEC_SEQ, NEAR * HT:(NEAR + 1) * HT], scores[0:HT, WIN_KEYS:WIN_ALL], ident[0:HT, 0:HT]).then_inc(turned_near, 1)
                    for r in range(OLD):
                        last = transpose(turn_old[0:OLD_J, r * HT:(r + 1) * HT], scores[0:HT, r * OLD_J:(r + 1) * OLD_J], ident[0:HT, 0:HT])
                    last.then_inc(turned_old, 1)
                    pe.wait_ge(copied_old, n + 1)
                    pe.wait_ge(values_in, 16 * V_IN * n + 16 * V_IN)
                    after(pe, masked, n)
                    for r in range(OLD):
                        mm(sum_bank[0:HT, :], probs_t[0:OLD_J, r, :], v_old[:, r, :], start=(r == 0), stop=False)
                    pe.wait_ge(copied_near, n + 1)
                    for r in range(NEAR):
                        mm(sum_bank[0:HT, :], probs_t[:, OLD + r, :], v_near[:, r, :], start=False, stop=False)
                    mm(sum_bank[0:HT, :], probs_t[0:DEC_SEQ, OLD + NEAR, :], v_new[:, :], start=False, stop=True).then_inc(summed, 1)

            @block.scalar
            def _(act):
                @stepped(act, DEC_BATCH)
                def _(n):
                    act.wait_ge(lowered, n + 1)
                    nc.scalar.activation(scores[0:HT, :], scores[0:HT, :], ACT.Exp, bias=low[:, 0:1], accum_out=total[:, 0:1]).then_inc(exped, 1)
                    act.wait_ge(turned_near, n + 1)
                    after(act, summed, n)
                    nc.scalar.activation(probs_t[:, OLD:OLD + NEAR, :], turn_near[:, 0:NEAR * HT].rearrange("p (r q) -> p r q", r=NEAR), ACT.Copy)
                    nc.scalar.activation(probs_t[0:DEC_SEQ, OLD + NEAR, :], turn_near[0:DEC_SEQ, NEAR * HT:(NEAR + 1) * HT], ACT.Copy).then_inc(copied_near, 1)
                    act.wait_ge(normed, n + 1)
                    act.dma_start(t["o_window"][bass.ds(n, 1), :, :].rearrange("b q d -> (b q) d"), out[:, :]).then_inc(stored, 16)

                act.wait_ge(stored, 16 * DEC_BATCH)

            @block.vector
            def _(dve):
                v_ = nc.vector
                dve.wait_ge(inputs_in, 16 * N_IN)
                setup = Chain(dve, sem("setup_link"))
                v_.memset(scores[:, :], 0.0)
                setup.link(v_.memset(q_all[:, :, :, :], 0.0))
                for h in range(HEADS):
                    rows = slice((h % 2) * 64, (h % 2) * 64 + 64)
                    last = v_.tensor_copy(q_all[rows, :, h // 2, h * DEC_SEQ:(h + 1) * DEC_SEQ],
                                          q_heads[rows, h // 2, :].rearrange("p (b t) -> p b t", b=DEC_BATCH))
                last.then_inc(q_placed, 1)
                dve.wait_ge(q_placed, 1)

                @stepped(dve, DEC_BATCH)
                def _(n):
                    link = Chain(dve, dve_link, LINKS * n).link
                    after(dve, scored, n)
                    v_.tensor_copy(q_now[:, :, :], q_all[:, bass.ds(n, 1), :, :].rearrange("p b c q -> p (b c) q")).then_inc(q_copied, 1)
                    after(dve, turned_near, n)
                    dve.wait_ge(scored, n + 1)
                    v_.memset(carrier[:, :], 0.0)
                    v_.tensor_tensor_reduce(scores[0:HT, :], score_bank[0:HT, 0:WIN_ALL], bias[:, :], 1.0, -3e38, ALU.add, ALU.max,
                                            top[:, :]).then_inc(maxed, 1)
                    dve.wait_ge(maxed, n + 1)
                    v_.tensor_scalar(low[:, :], top[:, :], -1.0, None, ALU.mult).then_inc(lowered, 1)
                    dve.wait_ge(turned_old, n + 1)
                    after(dve, summed, n)
                    v_.tensor_copy(probs_t[0:OLD_J, 0:OLD, :], turn_old[0:OLD_J, :].rearrange("p (r q) -> p r q", r=OLD)).then_inc(copied_old, 1)
                    link(v_.reciprocal(inverse[:, :], total[:, :]))
                    dve.wait_ge(summed, n + 1)
                    v_.tensor_tensor(own[:, :, :], sum_bank[0:HT, :].rearrange("p (h d) -> p h d", h=HEADS),
                                     own_head[:, :].rearrange("p (h d) -> p h d", h=HEADS), ALU.mult).then_inc(masked, 1)
                    dve.wait_ge(masked, n + 1)
                    after(dve, stored, 16 * n)
                    link(v_.tensor_reduce(out[:, :], own[:, :, :].rearrange("p h d -> p d h"), AX.X, ALU.add))
                    v_.tensor_scalar(out[:, :], out[:, :], inverse[:, 0:1], None, ALU.mult).then_inc(normed, 1)


def mix_and_route(nc, t, ident):
    with ExitStack() as ctx:
        def sb(name, shape, dt=F32):
            return ctx.enter_context(nc.sbuf_tensor(f"mix_{name}", shape, dt))

        def sem(name):
            return phase_semaphore(nc, t["phase_sems"], f"mix_{name}")

        w_out, w_router = sb("w_out", [P, KC, D_MODEL]), sb("w_router", [P, KC, GROUPS + EXPERTS])
        g_out, g_ffn, b_router = sb("g_out", [P, D_MODEL]), sb("g_ffn", [P, D_MODEL]), sb("b_router", [P, GROUPS + EXPERTS])
        before, ones, iota = sb("before", [P, P]), sb("ones", [P, P]), sb("iota", [P, 64])
        ticket = sb("ticket", [P, TILES * TOP_K, 2], I32)
        real = sb("real", [P, TILES])
        o, o_n, o_t = sb("o", [P, D_MODEL]), sb("o_n", [P, D_MODEL]), sb("o_t", [P, KC, P])
        x, x_mid = sb("x", [P, D_MODEL]), sb("x_mid", [P, D_MODEL])
        h, h_t = sb("h", [P, D_MODEL]), sb("h_t", [P, KC, P])
        squares, o_stat, h_stat = sb("squares", [P, D_MODEL]), sb("o_stat", [P, 6]), sb("h_stat", [P, 3])
        logits = sb("logits", [P, 8 + EXPERTS])
        group_top, group_at = sb("group_top", [P, 8]), sb("group_at", [P, 8], U32)
        group, neg_top, group_hot = sb("group", [P, 2]), sb("neg_top", [P, 2]), sb("group_hot", [P, GROUPS])
        of_group, chosen = sb("of_group", [P, GROUPS, PER_GROUP]), sb("chosen", [P, PER_GROUP])
        best, best_at, best_f = sb("best", [P, 8]), sb("best_at", [P, 8], U32), sb("best_f", [P, 2])
        group_exp, pair_exp, sums, scale = sb("group_exp", [P, GROUPS]), sb("pair_exp", [P, 2]), sb("sums", [P, 2]), sb("scale", [P, 2])
        pair, hot, hot_sum, hot_total = sb("pair", [P, 2]), sb("hot", [P, 2, EXPERTS]), sb("hot_sum", [P, EXPERTS]), sb("hot_total", [P, EXPERTS])
        ranked, real_now = sb("ranked", [P, 2, EXPERTS]), sb("real_now", [P, 1])
        start_128, per_tile, blocks_of, block_end = sb("start_128", [P, EXPERTS]), sb("per_tile", [P, TILES]), sb("blocks_of", [P, EXPERTS]), sb("block_end", [P, EXPERTS])
        fills, upto = sb("fills", [P, EXPERTS, TILES]), sb("upto", [P, EXPERTS, EXPERTS])
        starts, slot = sb("starts", [P, TILES * 2, EXPERTS]), sb("slot", [P, TILES * 2])
        spill, scatter = sb("spill", [P, TILES * 2]), sb("scatter", [P, TILES * 2], I32)
        passed, block_f = sb("passed", [1, MAX_BLOCKS, EXPERTS]), sb("block_f", [1, MAX_BLOCKS])
        carrier = sb("carrier", [1, 1])
        all_hot, all_rank = sb("all_hot", [P, TILES * 2, EXPERTS]), sb("all_rank", [P, TILES * 2])
        turn = ctx.enter_context(nc.psum_tensor("mix_turn", [P, D_MODEL], F32))
        turn_h = ctx.enter_context(nc.psum_tensor("mix_turn_h", [P, D_MODEL], F32))
        mixed_bank = ctx.enter_context(nc.psum_tensor("mix_bank", [P, D_MODEL], F32))
        router_bank = ctx.enter_context(nc.psum_tensor("mix_router_bank", [P, 512], F32))
        rank_bank = ctx.enter_context(nc.psum_tensor("mix_rank_bank", [P, 512], F32))

        weights_in, o_in, x_in = sem("weights_in"), sem("o_in"), sem("x_in")
        o_squared, o_root, o_normed, o_cleared = sem("o_squared"), sem("o_root"), sem("o_normed"), sem("o_cleared")
        o_turned, o_t_lo, o_t_hi, mixed = sem("o_turned"), sem("o_t_lo"), sem("o_t_hi"), sem("mixed")
        x_added, x_squared, x_root, h_normed = sem("x_added"), sem("x_squared"), sem("x_root"), sem("h_normed")
        h_turned, h_t_lo, h_t_hi, routed = sem("h_turned"), sem("h_t_lo"), sem("h_t_hi"), sem("routed")
        logits_done, group_topped, group_exped = sem("logits_done"), sem("group_topped"), sem("group_exped")
        pair_topped, pair_exped = sem("pair_topped"), sem("pair_exped")
        hot_done, rank_done, total_added = sem("hot_done"), sem("rank_done"), sem("total_added")
        gates_scaled, rank_picked = sem("gates_scaled"), sem("rank_picked")
        x_stored, h_stored = sem("x_stored"), sem("h_stored")
        counted, planned, cleared, scattered = sem("counted"), sem("planned"), sem("cleared"), sem("scattered")
        head_link, body_link, tail_link = sem("head_link"), sem("body_link"), sem("tail_link")
        HEAD_LINKS, BODY_LINKS, TAIL_LINKS = 2, 2, 13
        N_W = 10
        LAST = TILES - 1
        HALF_D = D_MODEL // 2

        def tiled(eng, step):
            step(0)
            with eng.Fori(1, LAST - 1) as i:
                step(i)
            step(LAST - 1)
            step(LAST)

        def is_step(i, n):
            return isinstance(i, int) and i == n

        def quarters(ap):
            return ap.rearrange("p (a c) -> p a c", a=4)

        with nc.Block() as block:
            @block.sync
            def _(sp):
                def wait(sem, value):
                    wait_apart(sp, t, sem, value)

                def load(dst, src):
                    sp.dma_start(dst, src).then_inc(weights_in, 16)

                sp.dma_start(o[:, :], t["o_cat"][0:P, :]).then_inc(o_in, 16)
                sp.dma_start(x[:, :], t["x_all"][0:P, :]).then_inc(x_in, 16)
                load(g_out[:, :], row_broadcast(t["norm_out"]))
                load(w_out[:, :, :], t["w_out"].rearrange("(k p) n -> p k n", p=P))
                load(g_ffn[:, :], row_broadcast(t["norm_ffn"]))
                load(w_router[:, :, :], t["w_router"].rearrange("(k p) n -> p k n", p=P))
                load(b_router[:, :], row_broadcast(t["b_router"]))
                load(before[:, :], t["c_before"])
                load(iota[:, :], t["c_iota"])
                load(ticket[:, :, :], t["c_ticket"])
                load(real[:, :], t["c_real"])
                load(spill[:, :], t["c_spill"])

                def finish(i):
                    at = bass.ds(i * P, P)
                    wait(x_added, i + 1)
                    sp.dma_start(t["x_mid"][at, :], x_mid[:, :]).then_inc(x_stored, 16)
                    if not is_step(i, LAST):
                        sp.dma_start(x[:, :], t["x_all"][bass.ds(i * P + P, P), :]).then_inc(x_in, 16)
                    wait(h_normed, i + 1)
                    sp.dma_start(t["h_ffn"][at, :], h[:, :]).then_inc(h_stored, 16)

                @stepped(sp, LAST - 1)
                def _(i):
                    wait(o_normed, i + 1)
                    sp.dma_start(o[:, :], t["o_cat"][bass.ds(i * P + P, P), :]).then_inc(o_in, 16)
                    finish(i)

                sp.wait_ge(o_normed, LAST)
                sp.dma_start(o[0:N_SAMPLE, 0:HALF_D], t["o_cat"][SEQ:SEQ + N_SAMPLE, 0:HALF_D]).then_inc(o_in, 16)
                for b in range(DEC_BATCH):
                    sp.dma_start(o[b * DEC_SEQ:(b + 1) * DEC_SEQ, HALF_D:D_MODEL].rearrange("t (h d) -> t h d", h=HEADS),
                                 t["o_window"][b].rearrange("(h t) d -> t h d", h=HEADS)).then_inc(o_in, 16)
                finish(LAST - 1)
                finish(LAST)
                sp.wait_ge(x_stored, 16 * TILES)
                sp.wait_ge(h_stored, 16 * TILES)

            @block.tensor
            def _(pe):
                mm, transpose = nc.tensor.matmul, nc.tensor.transpose

                def turn_tile(to, of, done):
                    for k in range(KC):
                        last = transpose(to[:, k * P:(k + 1) * P], of[:, k * P:(k + 1) * P], ident[:, :])
                        if k % 4 == 3:
                            last.then_inc(done, 1)

                def turn_and_route(j):
                    pe.wait_ge(h_normed, j + 1)
                    after(pe, h_t_lo, j)
                    after(pe, h_t_hi, j)
                    turn_tile(turn_h, h, h_turned)
                    pe.wait_ge(h_t_lo, j + 1)
                    pe.wait_ge(h_t_hi, j + 1)
                    for k in range(KC):
                        last = mm(router_bank[:, 0:GROUPS + EXPERTS], h_t[:, k, :], w_router[:, k, :], start=(k == 0), stop=(k == KC - 1))
                    last.then_inc(routed, 1)

                def rank(j):
                    pe.wait_ge(hot_done, j + 1)
                    mm(rank_bank[:, 0:EXPERTS], before[:, :], hot_sum[:, :], start=True, stop=False)
                    mm(rank_bank[:, 0:EXPERTS], ones[:, :], hot_total[:, :], start=False, stop=True).then_inc(rank_done, 1)

                def step(i):
                    pe.wait_ge(o_normed, i + 1)
                    turn_tile(turn, o_n, o_turned)
                    if not is_step(i, 0):
                        turn_and_route(i - 1)
                    pe.wait_ge(o_t_lo, i + 1)
                    pe.wait_ge(o_t_hi, i + 1)
                    after(pe, x_added, i)
                    for k in range(KC):
                        for half in range(2):
                            cols = slice(half * HALF_D, (half + 1) * HALF_D)
                            last = mm(mixed_bank[:, cols], o_t[:, k, :], w_out[:, k, cols], start=(k == 0), stop=(k == KC - 1))
                    last.then_inc(mixed, 1)
                    if not is_step(i, 0):
                        rank(i - 1)

                pe.wait_ge(weights_in, 16 * N_W)
                tiled(pe, step)
                turn_and_route(LAST)
                rank(LAST)
                pe.wait_ge(total_added, TILES)
                pe.wait_ge(rank_picked, TILES)
                mm(rank_bank[:, 0:EXPERTS], ones[:, :], hot_total[:, :], start=True, stop=True).then_inc(counted, 1)

            @block.scalar
            def _(act):
                def norm_o(i):
                    if is_step(i, LAST):
                        act.wait_ge(o_cleared, 1)
                        act.wait_ge(o_in, 16 * LAST + 16 * (1 + DEC_BATCH))
                    else:
                        act.wait_ge(o_in, 16 * i + 16)
                    for half in range(2):
                        cols = slice(half * HALF_D, (half + 1) * HALF_D)
                        nc.scalar.activation(squares[:, cols], o[:, cols], ACT.Square, accum_out=o_stat[:, half:half + 1]).then_inc(o_squared, 1)
                    act.wait_ge(head_link, HEAD_LINKS * i + 1)
                    nc.scalar.activation(o_stat[:, 4:6], o_stat[:, 2:4], ACT.Sqrt).then_inc(o_root, 1)

                def route(j):
                    act.wait_ge(h_turned, 2 * j + 2)
                    after(act, routed, j)
                    nc.scalar.activation(h_t[:, 4:8, :], quarters(turn_h[:, HALF_D:D_MODEL]), ACT.Copy).then_inc(h_t_hi, 1)
                    act.wait_ge(group_topped, j + 1)
                    nc.scalar.activation(group_exp[:, :], logits[:, 0:GROUPS], ACT.Exp, bias=neg_top[:, 0:1], accum_out=sums[:, 0:1]).then_inc(group_exped, 1)
                    act.wait_ge(pair_topped, j + 1)
                    nc.scalar.activation(pair_exp[:, :], best[:, 0:2], ACT.Exp, bias=neg_top[:, 1:2], accum_out=sums[:, 1:2]).then_inc(pair_exped, 1)

                def step(i):
                    act.wait_ge(o_turned, 2 * i + 2)
                    after(act, mixed, i)
                    nc.scalar.activation(o_t[:, 4:8, :], quarters(turn[:, HALF_D:D_MODEL]), ACT.Copy).then_inc(o_t_hi, 1)
                    if not is_step(i, 0):
                        route(i - 1)
                    if not is_step(i, LAST):
                        norm_o(i + 1)
                    act.wait_ge(x_added, i + 1)
                    nc.scalar.activation(squares[:, :], x_mid[:, :], ACT.Square, accum_out=h_stat[:, 0:1]).then_inc(x_squared, 1)
                    act.wait_ge(body_link, BODY_LINKS * i + 1)
                    nc.scalar.activation(h_stat[:, 2:3], h_stat[:, 1:2], ACT.Sqrt).then_inc(x_root, 1)

                norm_o(0)
                tiled(act, step)
                route(LAST)

            @block.vector
            def _(dve):
                v_ = nc.vector

                def norm_o(i):
                    if is_step(i, LAST):
                        dve.wait_ge(o_normed, LAST)
                        v_.memset(o[N_SAMPLE:P, :], 0.0).then_inc(o_cleared, 1)
                    link = Chain(dve, head_link, HEAD_LINKS * i).link
                    dve.wait_ge(o_squared, 2 * i + 2)
                    link(v_.tensor_scalar(o_stat[:, 2:4], o_stat[:, 0:2], 1.0 / HALF_D, EPS, ALU.mult, ALU.add))
                    dve.wait_ge(o_root, i + 1)
                    link(v_.reciprocal(o_stat[:, 0:2], o_stat[:, 4:6]))
                    after(dve, o_turned, 2 * i)
                    for half in range(2):
                        cols = slice(half * HALF_D, (half + 1) * HALF_D)
                        last = v_.scalar_tensor_tensor(o_n[:, cols], o[:, cols], o_stat[:, half:half + 1], g_out[:, cols], ALU.mult, ALU.mult)
                    last.then_inc(o_normed, 1)

                def route(j):
                    chain = Chain(dve, tail_link, TAIL_LINKS * j)
                    link = chain.link
                    dve.wait_ge(h_turned, 2 * j + 1)
                    after(dve, routed, j)
                    v_.tensor_copy(h_t[:, 0:4, :], quarters(turn_h[:, 0:HALF_D])).then_inc(h_t_lo, 1)
                    dve.wait_ge(routed, j + 1)
                    v_.tensor_copy(real_now[:, :], real[:, bass.ds(j, 1)])
                    v_.tensor_tensor(logits[:, 0:GROUPS], router_bank[:, 0:GROUPS], b_router[:, 0:GROUPS], ALU.add)
                    link(v_.tensor_tensor(logits[:, 8:8 + EXPERTS], router_bank[:, GROUPS:GROUPS + EXPERTS], b_router[:, GROUPS:GROUPS + EXPERTS], ALU.add))
                    v_.memset(carrier[:, :], 0.0)
                    link(v_.max(group_top[:, :], logits[:, 0:8]))
                    v_.tensor_scalar(neg_top[:, 0:1], group_top[:, 0:1], -1.0, None, ALU.mult).then_inc(group_topped, 1)
                    v_.memset(carrier[:, :], 0.0)
                    link(v_.max_index(group_at[:, :], group_top[:, :], logits[:, 0:8]))
                    link(v_.tensor_copy(group[:, 0:1], group_at[:, 0:1]))
                    v_.tensor_scalar(group[:, 1:2], group[:, 0:1], float(PER_GROUP), None, ALU.mult)
                    link(v_.tensor_scalar(group_hot[:, :], iota[:, 0:GROUPS], group[:, 0:1], None, ALU.is_equal))
                    link(v_.tensor_tensor(of_group[:, :, :], logits[:, 8:8 + EXPERTS].rearrange("p (g j) -> p g j", g=GROUPS),
                                          group_hot[:, :].unsqueeze(2).broadcast_to([P, GROUPS, PER_GROUP]), ALU.mult))
                    link(v_.tensor_reduce(chosen[:, :], of_group[:, :, :].rearrange("p g j -> p j g"), AX.X, ALU.add))
                    v_.memset(carrier[:, :], 0.0)
                    link(v_.max(best[:, :], chosen[:, :]))
                    v_.tensor_scalar(neg_top[:, 1:2], best[:, 0:1], -1.0, None, ALU.mult).then_inc(pair_topped, 1)
                    v_.memset(carrier[:, :], 0.0)
                    link(v_.max_index(best_at[:, :], best[:, :], chosen[:, :]))
                    link(v_.tensor_copy(best_f[:, :], best_at[:, 0:2]))
                    link(v_.tensor_scalar(pair[:, :], best_f[:, :], group[:, 1:2], None, ALU.add))
                    link(v_.tensor_tensor(ranked[:, :, :], iota[:, 0:EXPERTS].unsqueeze(1).broadcast_to([P, 2, EXPERTS]),
                                          pair[:, :].unsqueeze(2).broadcast_to([P, 2, EXPERTS]), ALU.is_equal))
                    rows = bass.ds(2 * j, 2)
                    v_.tensor_scalar(hot[:, :, :], ranked[:, :, :], real_now[:, 0:1], None, ALU.mult)
                    link(v_.tensor_copy(all_hot[:, rows, :], ranked[:, :, :]))
                    v_.tensor_tensor(hot_sum[:, :], hot[:, 0, :], hot[:, 1, :], ALU.add).then_inc(hot_done, 1)
                    dve.wait_ge(group_exped, j + 1)
                    dve.wait_ge(pair_exped, j + 1)
                    v_.tensor_tensor(scale[:, 0:1], sums[:, 0:1], sums[:, 1:2], ALU.mult).then_inc(gates_scaled, 1)
                    dve.wait_ge(gates_scaled, 2 * j + 1)
                    v_.reciprocal(scale[:, 1:2], scale[:, 0:1]).then_inc(gates_scaled, 1)
                    dve.wait_ge(gates_scaled, 2 * j + 2)
                    v_.tensor_scalar(t["gates"][:, rows], pair_exp[:, :], scale[:, 1:2], None, ALU.mult)

                def keep_rank(j):
                    rows = bass.ds(2 * j, 2)
                    dve.wait_ge(rank_done, j + 1)
                    v_.tensor_tensor(hot_total[:, :], hot_total[:, :], hot_sum[:, :], ALU.add).then_inc(total_added, 1)
                    v_.tensor_tensor(ranked[:, :, :], hot[:, :, :], rank_bank[:, 0:EXPERTS].unsqueeze(1).broadcast_to([P, 2, EXPERTS]), ALU.mult).then_inc(rank_picked, 1)
                    dve.wait_ge(rank_picked, j + 1)
                    v_.tensor_reduce(all_rank[:, rows], ranked[:, :, :], AX.X, ALU.add)

                def step(i):
                    dve.wait_ge(o_turned, 2 * i + 1)
                    after(dve, mixed, i)
                    v_.tensor_copy(o_t[:, 0:4, :], quarters(turn[:, 0:HALF_D])).then_inc(o_t_lo, 1)
                    if not is_step(i, 0):
                        route(i - 1)
                    if not is_step(i, LAST):
                        norm_o(i + 1)
                    link = Chain(dve, body_link, BODY_LINKS * i).link
                    dve.wait_ge(mixed, i + 1)
                    dve.wait_ge(x_in, 16 * i + 16)
                    after(dve, x_stored, 16 * i)
                    v_.tensor_tensor(x_mid[:, :], mixed_bank[:, :], x[:, :], ALU.add).then_inc(x_added, 1)
                    dve.wait_ge(x_squared, i + 1)
                    link(v_.tensor_scalar(h_stat[:, 1:2], h_stat[:, 0:1], 1.0 / D_MODEL, EPS, ALU.mult, ALU.add))
                    dve.wait_ge(x_root, i + 1)
                    link(v_.reciprocal(h_stat[:, 0:1], h_stat[:, 2:3]))
                    after(dve, h_turned, 2 * i)
                    after(dve, h_stored, 16 * i)
                    v_.scalar_tensor_tensor(h[:, :], x_mid[:, :], h_stat[:, 0:1], g_ffn[:, :], ALU.mult, ALU.mult).then_inc(h_normed, 1)
                    if not is_step(i, 0):
                        keep_rank(i - 1)


                dve.wait_ge(weights_in, 16 * N_W)
                setup = Chain(dve, sem("setup_link"))
                v_.memset(logits[:, :], -3e38)
                setup.link(v_.memset(hot_total[:, :], 0.0))
                setup.link(v_.memset(ones[:, :], 1.0))
                norm_o(0)
                tiled(dve, step)
                route(LAST)
                keep_rank(LAST)

                dve.wait_ge(counted, 1)
                plan = Chain(dve, sem("plan_link")).link
                plan(v_.tensor_scalar(per_tile[:, :], iota[:, 0:TILES], float(P), None, ALU.mult))
                plan(v_.tensor_tensor(fills[:, :, :], rank_bank[:, 0:EXPERTS].unsqueeze(2).broadcast_to([P, EXPERTS, TILES]),
                                      per_tile[:, :].unsqueeze(1).broadcast_to([P, EXPERTS, TILES]), ALU.is_gt))
                plan(v_.tensor_reduce(blocks_of[:, :], fills[:, :, :], AX.X, ALU.add))
                plan(v_.tensor_tensor(upto[:, :, :], iota[:, 0:EXPERTS].unsqueeze(1).broadcast_to([P, EXPERTS, EXPERTS]),
                                      iota[:, 0:EXPERTS].unsqueeze(2).broadcast_to([P, EXPERTS, EXPERTS]), ALU.is_le))
                plan(v_.tensor_tensor(upto[:, :, :], upto[:, :, :], blocks_of[:, :].unsqueeze(1).broadcast_to([P, EXPERTS, EXPERTS]), ALU.mult))
                plan(v_.tensor_reduce(block_end[:, :], upto[:, :, :], AX.X, ALU.add))
                plan(v_.tensor_tensor(start_128[:, :], block_end[:, :], blocks_of[:, :], ALU.subtract))
                plan(v_.tensor_scalar(start_128[:, :], start_128[:, :], float(P), None, ALU.mult))
                plan(v_.tensor_tensor(starts[:, :, :], all_hot[:, :, :], start_128[:, :].unsqueeze(1).broadcast_to([P, TILES * 2, EXPERTS]), ALU.mult))
                plan(v_.tensor_reduce(slot[:, :], starts[:, :, :], AX.X, ALU.add))
                plan(v_.tensor_tensor(slot[:, :], slot[:, :], all_rank[:, :], ALU.add))
                plan(v_.tensor_tensor(slot[:, :].rearrange("p (i c) -> p i c", c=2), slot[:, :].rearrange("p (i c) -> p i c", c=2),
                                      real[:, :].unsqueeze(2).broadcast_to([P, TILES, 2]), ALU.mult))
                v_.tensor_tensor(scatter[:, :], slot[:, :], spill[:, :], ALU.add).then_inc(planned, 1)
                plan(v_.tensor_tensor(passed[:, :, :], block_end[0:1, :].unsqueeze(1).broadcast_to([1, MAX_BLOCKS, EXPERTS]),
                                      iota[0:1, 0:MAX_BLOCKS].unsqueeze(2).broadcast_to([1, MAX_BLOCKS, EXPERTS]), ALU.is_le))
                plan(v_.tensor_reduce(block_f[:, :], passed[:, :, :], AX.X, ALU.add))
                v_.tensor_scalar(t["block_expert"][:, 0:MAX_BLOCKS], block_f[:, :], float(EXPERTS - 1), None, ALU.min)
                plan(v_.tensor_copy(t["block_expert"][:, MAX_BLOCKS:MAX_BLOCKS + 1], block_end[0:1, EXPERTS - 1:EXPERTS]))

            @block.gpsimd
            def _(gp):
                gp.dma_start(t["slot_ticket"], t["c_empty_tickets"]).then_inc(cleared, 16)
                gp.wait_ge(cleared, 16)
                gp.wait_ge(weights_in, 16 * N_W)
                gp.wait_ge(planned, 1)
                for c in range(TILES * TOP_K):
                    gp.indirect_dma_start(out=t["slot_ticket"], out_offset=bass.IndirectOffsetOnAxis(ap=scatter[:, c:c + 1], axis=0),
                                          in_=ticket[:, c, :], in_offset=None).then_inc(scattered, 16)
                gp.wait_ge(scattered, 16 * TILES * TOP_K)


def experts(nc, t, ident):
    with ExitStack() as ctx:
        def sb(name, shape, dt=F32):
            return ctx.enter_context(nc.sbuf_tensor(f"ex_{name}", shape, dt))

        def sem(name):
            return phase_semaphore(nc, t["phase_sems"], f"ex_{name}")

        w_gate, w_up, w_down = sb("w_gate", [P, KC, D_EXPERT]), sb("w_up", [P, KC, D_EXPERT]), sb("w_down", [P, FC, D_MODEL])
        tickets, goal = sb("tickets", [P, 2], I32), sb("goal", [P, 1], I32)
        x, x_t = sb("x", [P, D_MODEL]), sb("x_t", [P, KC, P])
        gated, hidden, hidden_t = sb("gated", [P, D_EXPERT]), sb("hidden", [P, D_EXPERT]), sb("hidden_t", [P, FC, P])
        y = sb("y", [P, D_MODEL])
        carrier, carrier2, carrier3, carrier4 = sb("carrier", [P, 1]), sb("carrier2", [P, 1]), sb("carrier3", [P, 1]), sb("carrier4", [P, 1])
        turn_x = ctx.enter_context(nc.psum_tensor("ex_turn_x", [P, D_MODEL], F32))
        gate_bank = ctx.enter_context(nc.psum_tensor("ex_gate_bank", [P, 512], F32))
        up_bank = ctx.enter_context(nc.psum_tensor("ex_up_bank", [P, 512], F32))
        turn_h = ctx.enter_context(nc.psum_tensor("ex_turn_h", [P, 512], F32))
        down_bank = ctx.enter_context(nc.psum_tensor("ex_down_bank", [P, D_MODEL], F32))

        gate_in, up_in, down_in, tickets_in, gathered = sem("gate_in"), sem("up_in"), sem("down_in"), sem("tickets_in"), sem("gathered")
        x_turned, x_t_lo, x_t_hi = sem("x_turned"), sem("x_t_lo"), sem("x_t_hi")
        gate_done, up_done, gated_done, hidden_done = sem("gate_done"), sem("up_done"), sem("gated_done"), sem("hidden_done")
        h_turned, h_t_copied, down_done = sem("h_turned"), sem("h_t_copied"), sem("down_done")
        y_lo, y_hi, stored = sem("y_lo"), sem("y_hi"), sem("stored")
        carried, carried2, carried3, goal_copied = sem("carried"), sem("carried2"), sem("carried3"), sem("goal_copied")
        HALF_D = D_MODEL // 2

        def block_count(eng):
            return eng.value_load(t["block_expert"][0:1, MAX_BLOCKS:MAX_BLOCKS + 1], min_val=N_TOKENS * TOP_K // P, max_val=MAX_BLOCKS)

        def over_blocks(eng, count, step):
            step(0)
            with eng.Fori(1, count) as b:
                step(b)

        def quarters(ap):
            return ap.rearrange("p (a c) -> p a c", a=4)

        with nc.Block() as block:
            @block.sync
            def _(sp):
                count = block_count(sp)

                def step(b):
                    e = sp.value_load(t["block_expert"][0:1, bass.ds(b, 1)], min_val=0, max_val=EXPERTS - 1)
                    one = bass.ds(e, 1)
                    for w, name, used, ready in ((w_gate, "w_gate", gate_done, gate_in), (w_up, "w_up", up_done, up_in), (w_down, "w_down", down_done, down_in)):
                        k = w.shape[1]
                        if not isinstance(b, int):
                            wait_apart(sp, t, used, b)
                        sp.dma_start(w[:, :, :], t[name][one, :, :].rearrange("e (p k) n -> p (e k) n", k=k)).then_inc(ready, 16)

                over_blocks(sp, count, step)

            @block.gpsimd
            def _(gp):
                count = block_count(gp)

                def carry(tile, done=None):
                    tiny = nc.gpsimd.tensor_tensor(tile[:, 0:1], ident[:, 0:1], ident[:, 0:1], ALU.add)
                    if done is not None:
                        tiny.then_inc(done, 1)

                def gather(b):
                    after(gp, x_turned, 2 * b)
                    after(gp, goal_copied, b)
                    carry(carrier, carried)
                    gp.dma_start(tickets[:, :], t["slot_ticket"][bass.ds(b * P, P), :]).then_inc(tickets_in, 16)
                    gp.wait_ge(carried, b + 1)
                    gp.wait_ge(tickets_in, 16 * b + 16)
                    carry(carrier2, carried2)
                    gp.indirect_dma_start(out=x[:, :], out_offset=None, in_=t["h_ffn"],
                                          in_offset=bass.IndirectOffsetOnAxis(ap=tickets[:, 0:1], axis=0)).then_inc(gathered, 16)

                def scatter(b):
                    gp.wait_ge(carried2, b + 1)
                    gp.wait_ge(y_lo, b)
                    gp.wait_ge(y_hi, b)
                    carry(carrier3, carried3)
                    gp.indirect_dma_start(out=t["expert_rows"], out_offset=bass.IndirectOffsetOnAxis(ap=goal[:, 0:1], axis=0),
                                          in_=y[:, :], in_offset=None).then_inc(stored, 16)

                def keep_goal(b):
                    if not isinstance(b, int):
                        gp.wait_ge(stored, 16 * b)
                        gp.wait_ge(carried3, b)
                        carry(carrier4)
                    nc.gpsimd.tensor_copy(goal[:, :], tickets[:, 1:2]).then_inc(goal_copied, 1)

                gather(0)
                keep_goal(0)
                with gp.Fori(1, count) as b:
                    gather(b)
                    scatter(b)
                    keep_goal(b)
                gather(count)
                scatter(count)
                gp.wait_ge(carried3, count)
                gp.wait_ge(gathered, count * 16 + 16)
                gp.wait_ge(stored, count * 16)

            @block.tensor
            def _(pe):
                mm, transpose = nc.tensor.matmul, nc.tensor.transpose
                count = block_count(pe)

                def turn(half):
                    of = x[:, :].rearrange("p (c k) -> p k c", k=KC)
                    for k in range(4 * half, 4 * half + 4):
                        last = transpose(turn_x[:, k * P:(k + 1) * P], of[:, k, :], ident[:, :])
                    last.then_inc(x_turned, 1)

                def step(b):
                    pe.wait_ge(x_t_lo, b + 1)
                    pe.wait_ge(x_t_hi, b + 1)
                    pe.wait_ge(gate_in, 16 * b + 16)
                    after(pe, gated_done, b)
                    for k in range(KC):
                        last = mm(gate_bank[:, :], x_t[:, k, :], w_gate[:, k, :], start=(k == 0), stop=(k == KC - 1))
                    last.then_inc(gate_done, 1)
                    pe.wait_ge(up_in, 16 * b + 16)
                    after(pe, hidden_done, b)
                    for k in range(KC):
                        last = mm(up_bank[:, :], x_t[:, k, :], w_up[:, k, :], start=(k == 0), stop=(k == KC - 1))
                    last.then_inc(up_done, 1)
                    pe.wait_ge(gathered, 16 * b + 32)
                    turn(0)
                    pe.wait_ge(hidden_done, b + 1)
                    after(pe, h_t_copied, b)
                    of = hidden[:, :].rearrange("p (c k) -> p k c", k=FC)
                    for k in range(FC):
                        last = transpose(turn_h[:, k * P:(k + 1) * P], of[:, k, :], ident[:, :])
                    last.then_inc(h_turned, 1)
                    turn(1)
                    pe.wait_ge(down_in, 16 * b + 16)
                    pe.wait_ge(h_t_copied, b + 1)
                    after(pe, y_lo, b)
                    after(pe, y_hi, b)
                    for k in range(FC):
                        for half in range(2):
                            cols = slice(half * HALF_D, (half + 1) * HALF_D)
                            last = mm(down_bank[:, cols], hidden_t[:, k, :], w_down[:, k, cols], start=(k == 0), stop=(k == FC - 1))
                    last.then_inc(down_done, 1)

                pe.wait_ge(gathered, 16)
                turn(0)
                turn(1)
                over_blocks(pe, count, step)

            @block.scalar
            def _(act):
                count = block_count(act)

                def copy_x(b):
                    act.wait_ge(x_turned, 2 * b + 2)
                    nc.scalar.activation(x_t[:, 4:8, :], quarters(turn_x[:, HALF_D:D_MODEL]), ACT.Copy).then_inc(x_t_hi, 1)

                def step(b):
                    act.wait_ge(gate_done, b + 1)
                    after(act, hidden_done, b)
                    nc.scalar.activation(gated[:, :], gate_bank[:, :], ACT.Silu).then_inc(gated_done, 1)
                    act.wait_ge(up_done, b + 1)
                    copy_x(b + 1)
                    act.wait_ge(down_done, b + 1)
                    after(act, stored, 16 * b)
                    nc.scalar.activation(y[:, HALF_D:D_MODEL], down_bank[:, HALF_D:D_MODEL], ACT.Copy).then_inc(y_hi, 1)

                copy_x(0)
                over_blocks(act, count, step)

            @block.vector
            def _(dve):
                v_ = nc.vector
                count = block_count(dve)

                def copy_x(b):
                    dve.wait_ge(x_turned, 2 * b + 1)
                    v_.tensor_copy(x_t[:, 0:4, :], quarters(turn_x[:, 0:HALF_D])).then_inc(x_t_lo, 1)

                def step(b):
                    dve.wait_ge(up_done, b + 1)
                    dve.wait_ge(gated_done, b + 1)
                    v_.tensor_tensor(hidden[:, :], gated[:, :], up_bank[:, :], ALU.mult).then_inc(hidden_done, 1)
                    copy_x(b + 1)
                    dve.wait_ge(h_turned, b + 1)
                    v_.tensor_copy(hidden_t[:, :, :], quarters(turn_h[:, :])).then_inc(h_t_copied, 1)
                    dve.wait_ge(down_done, b + 1)
                    after(dve, stored, 16 * b)
                    v_.tensor_copy(y[:, 0:HALF_D], down_bank[:, 0:HALF_D]).then_inc(y_lo, 1)

                copy_x(0)
                over_blocks(dve, count, step)


def combine(nc, t, ident):
    with ExitStack() as ctx:
        def sb(name, shape, dt=F32):
            return ctx.enter_context(nc.sbuf_tensor(f"com_{name}", shape, dt))

        def sem(name):
            return phase_semaphore(nc, t["phase_sems"], f"com_{name}")

        g_final = sb("g_final", [P, D_MODEL])
        gates_now = [sb(f"gates_now{u}", [P, 2]) for u in range(2)]
        x, y = [sb(f"x{u}", [P, D_MODEL]) for u in range(2)], [sb(f"y{u}", [P, 2, D_MODEL]) for u in range(2)]
        one, both, out = [[sb(f"{n}{u}", [P, D_MODEL]) for u in range(2)] for n in ("one", "both", "out")]
        stat = [sb(f"stat{u}", [P, 4]) for u in range(2)]
        squares = sb("squares", [P, D_MODEL])

        def pair(name):
            return [sem(f"{name}{u}") for u in range(2)]

        gain_in, x_in, y_in, gates_copied = sem("gain_in"), pair("x_in"), pair("y_in"), sem("gates_copied")
        added, summed, squared, rooted, normed, stored = pair("added"), pair("summed"), pair("squared"), pair("rooted"), pair("normed"), pair("stored")
        tails_in, dve_link = sem("tails_in"), pair("dve_link")
        LINKS = 2
        PAIRS = PROMPT_TILES // 2

        def rows_of(i):
            return N_TOKENS - i * P if isinstance(i, int) and i == TILES - 1 else P

        def by_pairs(eng, step):
            for u in range(2):
                step(u, u, 0)
            with eng.Fori(1, PAIRS) as r:
                for u in range(2):
                    step(2 * r + u, u, r)
            step(TILES - 1, 0, PAIRS)

        with nc.Block() as block:
            @block.sync
            def _(sp):
                sp.dma_start(g_final[:, :], row_broadcast(t["norm_final"])).then_inc(gain_in, 16)
                new = slice(WINDOW - DEC_SEQ, WINDOW)
                for out_name, rows in (("sw_k_new", "swk_all"), ("sw_v_new", "swv_all")):
                    sp.dma_start(t[out_name][:, new, :], t[rows][SEQ:N_TOKENS, :].rearrange("(b t) f -> b t f", t=DEC_SEQ)).then_inc(tails_in, 16)

                def step(i, u, r):
                    if not isinstance(r, int):
                        wait_apart(sp, t, added[u], r)
                    elif r > 0:
                        sp.wait_ge(added[u], r)
                    n = rows_of(i)
                    sp.dma_start(x[u][0:n, :], t["x_mid"][bass.ds(i * P, n), :]).then_inc(x_in[u], 16)
                    if not isinstance(r, int):
                        wait_apart(sp, t, summed[u], r)
                    elif r > 0:
                        sp.wait_ge(summed[u], r)
                    for c in range(TOP_K):
                        sp.dma_start(y[u][0:n, c, :], t["expert_rows"][bass.ds(i * P + c * ROWS, n), :]).then_inc(y_in[u], 16)

                by_pairs(sp, step)
                sp.wait_ge(tails_in, 32)
                sp.wait_ge(t["shifted"], 16 * 2 * DEC_BATCH)

            @block.vector
            def _(dve):
                v_ = nc.vector
                dve.wait_ge(gain_in, 16)

                def step(i, u, r):
                    n = rows_of(i)
                    link = Chain(dve, dve_link[u], LINKS * r).link
                    dve.wait_ge(x_in[u], 16 * r + 16)
                    dve.wait_ge(y_in[u], 32 * r + 32)
                    v_.tensor_copy(gates_now[u][:, :], t["gates"][:, bass.ds(2 * i, 2)]).then_inc(gates_copied, 1)
                    dve.wait_ge(gates_copied, i + 1)
                    v_.scalar_tensor_tensor(one[u][0:n, :], y[u][0:n, 0, :], gates_now[u][0:n, 0:1], x[u][0:n, :], ALU.mult, ALU.add).then_inc(added[u], 1)
                    dve.wait_ge(added[u], r + 1)
                    v_.scalar_tensor_tensor(both[u][0:n, :], y[u][0:n, 1, :], gates_now[u][0:n, 1:2], one[u][0:n, :], ALU.mult, ALU.add).then_inc(summed[u], 1)
                    dve.wait_ge(squared[u], r + 1)
                    link(v_.tensor_scalar(stat[u][0:n, 1:2], stat[u][0:n, 0:1], 1.0 / D_MODEL, EPS, ALU.mult, ALU.add))
                    dve.wait_ge(rooted[u], r + 1)
                    link(v_.reciprocal(stat[u][0:n, 3:4], stat[u][0:n, 2:3]))
                    after(dve, stored[u], 16 * r)
                    v_.scalar_tensor_tensor(out[u][0:n, :], both[u][0:n, :], stat[u][0:n, 3:4], g_final[0:n, :], ALU.mult, ALU.mult).then_inc(normed[u], 1)

                by_pairs(dve, step)

            @block.scalar
            def _(act):
                def step(i, u, r):
                    n = rows_of(i)
                    act.wait_ge(summed[u], r + 1)
                    nc.scalar.activation(squares[0:n, :], both[u][0:n, :], ACT.Square, accum_out=stat[u][0:n, 0:1]).then_inc(squared[u], 1)
                    act.wait_ge(dve_link[u], LINKS * r + 1)
                    nc.scalar.activation(stat[u][0:n, 2:3], stat[u][0:n, 1:2], ACT.Sqrt).then_inc(rooted[u], 1)
                    act.wait_ge(normed[u], r + 1)
                    act.dma_start(t["y_all"][bass.ds(i * P, n), :], out[u][0:n, :]).then_inc(stored[u], 16)

                by_pairs(act, step)
                act.wait_ge(stored[0], 16 * (PAIRS + 1))
                act.wait_ge(stored[1], 16 * PAIRS)


OUTPUTS = {
    "y_all": (N_TOKENS, D_MODEL), "kv_all": (ROWS, KV_LORA), "kr_all": (ROWS, ROPE), "swk_all": (ROWS, SW_WIDTH),
    "swv_all": (ROWS, SW_WIDTH), "sw_k_new": (DEC_BATCH, WINDOW, SW_WIDTH), "sw_v_new": (DEC_BATCH, WINDOW, SW_WIDTH),
}
SCRATCH = {
    "q_t": ((HEADS, QK, ROWS), F32), "kn_t": ((HEADS * NOPE, ROWS), F32), "kr_t": ((ROPE, ROWS), F32),
    "v_mla": ((ROWS, 512), F32), "q_sw_t": ((512, ROWS), F32), "k_sw_t": ((512, ROWS), F32),
    "o_cat": ((ROWS, D_MODEL), F32), "o_window": ((DEC_BATCH, HEADS * DEC_SEQ, 64), F32),
    "x_mid": ((ROWS, D_MODEL), F32), "h_ffn": ((ROWS, D_MODEL), F32),
    "slot_ticket": (((MAX_BLOCKS + 1) * P, 2), I32),
    "expert_rows": ((TOP_K * ROWS + P, D_MODEL), F32),
}
SCRATCH_KIND = {}


def host_tables(np, a):
    f = np.float32
    slope = 2.0 ** (-8.0 * np.arange(1, HEADS + 1) / HEADS)

    def window_bias(dist):
        times = sum(((dist >= 0) & (dist <= w) & (dist % d == 0)).astype(np.int64) for w, d in PATTERNS)
        log_times = np.log(np.maximum(times, 1).astype(np.float64))
        shaped = slope.reshape([HEADS] + [1] * dist.ndim)
        return np.where(times > 0, log_times - shaped * dist, MASK).astype(f)

    dist = (SEQ - P) + np.arange(P)[:, None] - np.arange(SEQ)[None, :]
    a["c_causal"] = np.where(dist >= 0, 0.0, MASK).astype(f)[None].repeat(1, 0)
    a["c_window"] = window_bias(dist)
    row = np.concatenate([(16 * np.arange(OLD_J)[None, :] + np.arange(DEC_SEQ)[:, None]).ravel(),
                          np.arange(WINDOW - 512, WINDOW), WINDOW + np.arange(DEC_SEQ)])
    dist = WINDOW + np.arange(DEC_SEQ)[:, None] - row[None, :]
    a["c_window_sample"] = window_bias(dist).reshape(HEADS * DEC_SEQ, WIN_ALL)
    h = np.arange(HEADS * DEC_SEQ) // DEC_SEQ
    a["c_own_head"] = (h[:, None] == (np.arange(512) // 64)[None, :]).astype(f)
    new = np.where(np.arange(DEC_SEQ)[:, None] <= (np.arange(64) % DEC_SEQ)[None, :], 0.0, MASK).astype(f)
    a["c_new_mask"] = new
    a["c_page_part"] = (np.arange(P) % 8).astype(f)[:, None]
    a["c_before"] = (np.arange(P)[:, None] < np.arange(P)[None, :]).astype(f)
    row = np.arange(TILES)[None, :] * P + np.arange(P)[:, None]
    real = row < N_TOKENS
    choice = np.arange(TOP_K)
    a["c_ticket"] = np.stack(np.broadcast_arrays(row[:, :, None], row[:, :, None] + choice * ROWS), -1).reshape(P, TILES * TOP_K, 2).astype(np.int32)
    slots = np.arange((MAX_BLOCKS + 1) * P)
    a["c_empty_tickets"] = np.stack([0 * slots, TOP_K * ROWS + slots % P], 1).astype(np.int32)
    a["c_real"] = real.astype(f)
    behind = MAX_BLOCKS * P + (np.arange(P)[:, None, None] + np.arange(TOP_K) * N_SAMPLE) % P
    a["c_spill"] = np.where(real[:, :, None], 0, behind).reshape(P, TILES * TOP_K).astype(f)
    a["c_iota"] = np.broadcast_to(np.arange(64, dtype=f)[None, :], (P, 64)).copy()


def host_layout(np, a, x):
    k = x["state_sw_k"][0].reshape(DEC_BATCH, WINDOW, 4, P)
    old = (16 * np.arange(OLD_J)[None, :] + np.arange(DEC_SEQ)[:, None]).ravel()
    order = np.concatenate([old, np.arange(WINDOW - 512, WINDOW)])
    a["window_k_t"] = k[:, order].transpose(0, 3, 2, 1)
    a["w_uk_t"] = x["w_uk"][0].transpose(2, 1, 0)
    a["cache_kv"] = x["cache_kv_latent"][0].reshape(-1, 16 * KV_LORA)
    a["cache_kr"] = x["cache_k_rope"][0].reshape(-1, 16 * ROPE)
    pages = x["page_table"].astype(np.int32).reshape(DEC_BATCH, 4, 16)
    a["page_rows"] = pages.transpose(2, 0, 1).reshape(16, 32).repeat(8, 0)
    a["norm_out"] = np.concatenate([x["norm_out_mla"][0], x["norm_out_sw"][0]])
    a["w_out"], a["norm_ffn"], a["norm_final"] = x["w_out"][0], x["norm_ffn"][0], x["norm_final"]
    a["w_router"] = np.concatenate([x["w_router_group"][0], x["w_router_expert"][0]], 1)
    a["b_router"] = np.concatenate([x["b_router_group"][0], x["b_router_expert"][0]])
    a["w_gate"], a["w_up"], a["w_down"] = x["w_expert_gate"][0], x["w_expert_up"][0], x["w_expert_down"][0]


def program(nc, t, phases):
    t["shifted"] = nc.alloc_semaphore("window_shifted")
    t["ident_in"] = nc.alloc_semaphore("ident_in")
    with (nc.sbuf_tensor("ident", [P, P], F32) as ident,
          nc.sbuf_tensor("gates", [P, TILES * TOP_K], F32) as gates, nc.sbuf_tensor("block_expert", [1, MAX_BLOCKS + 1], I32) as block_expert):
        t.update(gates=gates, block_expert=block_expert)
        with nc.Block() as block:
            @block.sync
            def _(sp):
                sp.dma_start(ident[:, :], t["c_ident"]).then_inc(t["ident_in"], 16)
                sp.wait_ge(t["ident_in"], 16)
        for phase in phases:
            t["phase_sems"] = []
            phase(nc, t, ident)
            nc.clear_and_free_semaphores(t["phase_sems"])
            nc.all_engine_barrier()


PHASES = [project, attend_prompt, attend_latent, attend_window, mix_and_route, experts, combine]


def kernel(**inputs):
    import numpy as np
    import concourse.bacc as bacc
    from concourse.bass_utils import run_bass_kernel_spmd as run

    x = {n: np.asarray(a) for n, a in inputs.items()}
    f = np.float32
    a = {
        "x_all": np.concatenate([x["x_prompt"].reshape(SEQ, D_MODEL), x["x_sample"].reshape(N_SAMPLE, D_MODEL),
                                 np.zeros((ROWS - SEQ - N_SAMPLE, D_MODEL), f)]),
        "w_in": x["w_in"][0], "norm_mix": x["norm_mix"][0], "norm_q_latent": x["norm_q_latent"][0],
        "norm_kv_latent": x["norm_kv_latent"][0], "w_uq": x["w_uq"][0].reshape(Q_LORA, HEADS * QK),
        "w_uk": x["w_uk"][0].reshape(KV_LORA, 512), "w_uv": x["w_uv"][0].reshape(KV_LORA, 512),
        "state_sw_k": x["state_sw_k"][0].reshape(DEC_BATCH, WINDOW, SW_WIDTH),
        "state_sw_v": x["state_sw_v"][0].reshape(DEC_BATCH, WINDOW, SW_WIDTH),
    }
    pos = np.zeros(ROWS, f)
    pos[:SEQ] = np.arange(SEQ)
    pos[SEQ:SEQ + N_SAMPLE] = PAST_LEN + np.tile(np.arange(DEC_SEQ), DEC_BATCH)
    angle = (pos[:, None] * (f(10000.0) ** (-np.arange(HALF, dtype=f) / f(HALF)))[None, :]).astype(np.float64)
    a["c_angles"] = np.concatenate([np.cos(angle), np.sin(angle)], 1).astype(f)
    a["c_ident"] = np.eye(P, dtype=f)
    host_tables(np, a)
    host_layout(np, a, x)

    nc = bacc.Bacc("TRN2", target_bir_lowering=False, num_devices=1)
    t, arrays = {}, {}
    for name, v in a.items():
        v = np.ascontiguousarray(v)
        arrays[name] = v
        t[name] = nc.dram_tensor(name, v.shape, mybir.dt.from_np(v.dtype), kind="ExternalInput").ap()
    for name, shape in OUTPUTS.items():
        t[name] = nc.dram_tensor(name, shape, F32, kind="ExternalOutput").ap()
    for name, (shape, dt) in SCRATCH.items():
        t[name] = nc.dram_tensor(name, shape, dt, **SCRATCH_KIND).ap()
    program(nc, t, PHASES)
    o = run(nc, [arrays], core_ids=[0]).results[0]
    sample = slice(SEQ, SEQ + N_SAMPLE)
    return (o["y_all"][:SEQ].reshape(1, SEQ, D_MODEL), o["y_all"][sample].reshape(DEC_BATCH, DEC_SEQ, D_MODEL),
            o["kv_all"][:SEQ].reshape(1, 1, SEQ, KV_LORA), o["kr_all"][:SEQ].reshape(1, 1, SEQ, ROPE),
            o["swk_all"][:SEQ].reshape(1, 1, SEQ, HEADS, 64), o["swv_all"][:SEQ].reshape(1, 1, SEQ, HEADS, 64),
            o["kv_all"][sample].reshape(1, DEC_BATCH, DEC_SEQ, KV_LORA),
            o["kr_all"][sample].reshape(1, DEC_BATCH, DEC_SEQ, ROPE),
            o["sw_k_new"].reshape(1, DEC_BATCH, WINDOW, HEADS, 64),
            o["sw_v_new"].reshape(1, DEC_BATCH, WINDOW, HEADS, 64))
```

```python
from contextlib import ExitStack
import math

import concourse.bass as bass
from concourse import mybir

F32 = mybir.dt.float32
I32 = mybir.dt.int32
U32 = mybir.dt.uint32
ALU = mybir.AluOpType
ACT = mybir.ActivationFunctionType
AX = mybir.AxisListType

P = 128
D_MODEL = 1024
SEQ = 1024
DEC_BATCH, DEC_SEQ = 8, 8
N_SAMPLE = DEC_BATCH * DEC_SEQ
PROMPT_TILES = SEQ // P
TILES = PROMPT_TILES + 1
ROWS = TILES * P
PAST_LEN = 8192
PAGE = 128
N_PAGES = PAST_LEN // PAGE
HEADS = 8
Q_LORA, KV_LORA, NOPE, ROPE = 192, 128, 64, 32
QK = NOPE + ROPE
V_DIM = 64
HALF = ROPE // 2
MLA_SCALE = QK ** -0.5
SW_SCALE = 64 ** -0.5
SW_WIDTH = 512
LATENTS = Q_LORA + KV_LORA + ROPE
IN_WIDTH = LATENTS + 3 * SW_WIDTH
WINDOW = 2048
PATTERNS = ((128, 1), (512, 4), (2048, 16))
EPS = 1e-6
MASK = -1e30
KC = D_MODEL // P
GROUPS, PER_GROUP, EXPERTS, TOP_K = 4, 8, 32, 2
D_EXPERT = 512
FC = D_EXPERT // P
N_TOKENS = SEQ + N_SAMPLE
MAX_BLOCKS = -(-N_TOKENS * TOP_K // P) + EXPERTS
OLD_J = (WINDOW - 512) // 16
OLD_KEYS = OLD_J * DEC_SEQ
NEAR_TILES = 512 // P
WIN_KEYS = OLD_KEYS + 512
WIN_ALL = WIN_KEYS + DEC_SEQ


class Chain:

    def __init__(self, eng, sem, base=0):
        self.eng, self.sem, self.base, self.n = eng, sem, base, 0

    def link(self, ins):
        self.n += 1
        ins.then_inc(self.sem, 1)
        self.eng.wait_ge(self.sem, self.base + self.n)


def after(eng, sem, value):
    if not isinstance(value, int) or value > 0:
        eng.wait_ge(sem, value)


def wait_apart(eng, t, sem, value):
    eng.wait_ge(t["ident_in"], 16)
    eng.wait_ge(sem, value)


def stepped(eng, n):
    def run(step):
        step(0)
        with eng.Fori(1, n) as i:
            step(i)
    return run


def stepped_to_last(eng, n):
    def run(step):
        step(0, False)
        with eng.Fori(1, n - 1) as i:
            step(i, False)
        step(n - 1, True)
    return run


def phase_semaphore(nc, sems, name):
    s = nc.alloc_semaphore(name)
    sems.append(s)
    return s


def row_broadcast(vector):
    return vector.partition_broadcast(P)


def project(nc, t, ident):
    with ExitStack() as ctx:
        def sb(name, shape, dt=F32):
            return ctx.enter_context(nc.sbuf_tensor(f"a_{name}", shape, dt))

        def sem(name):
            return phase_semaphore(nc, t["phase_sems"], f"a_{name}")

        w_in = sb("w_in", [P, KC, IN_WIDTH])
        w_uq0, w_uq1 = sb("w_uq0", [P, HEADS * QK]), sb("w_uq1", [Q_LORA - P, HEADS * QK])
        w_uk, w_uv = sb("w_uk", [P, 512]), sb("w_uv", [P, 512])
        g_mix, g_q, g_kv = sb("g_mix", [P, D_MODEL]), sb("g_q", [P, Q_LORA]), sb("g_kv", [P, KV_LORA])
        x, squares, xn = sb("x", [P, D_MODEL]), sb("squares", [P, D_MODEL]), sb("xn", [P, D_MODEL])
        x_t = sb("x_t", [P, KC, P])
        angles = sb("angles", [P, ROPE])
        stat, stat2 = sb("stat", [P, 3]), sb("stat2", [P, 6])
        cq, ckv, kr = sb("cq", [P, Q_LORA]), sb("ckv", [P, KV_LORA]), sb("kr", [P, ROPE])
        rot = sb("rot", [P, 4, HEADS, HALF])
        rot_k = sb("rot_k", [P, 4, HALF])
        cq_t0, cq_t1 = sb("cq_t0", [P, P]), sb("cq_t1", [Q_LORA - P, P])
        ckv_t, kr_t = sb("ckv_t", [P, P]), sb("kr_t", [ROPE, P])
        q = sb("q", [P, HEADS, QK])
        q_t, kn_t, v = sb("q_t", [QK, HEADS, P]), sb("kn_t", [P, 4, P]), sb("v", [P, 512])
        q_sw, k_sw, v_sw = sb("q_sw", [P, 512]), sb("k_sw", [P, 512]), sb("v_sw", [P, 512])
        q_sw_t, k_sw_t = sb("q_sw_t", [P, 4, P]), sb("k_sw_t", [P, 4, P])
        bank = [ctx.enter_context(nc.psum_tensor(f"a_bank{n}", [P, 512], F32)) for n in range(8)]
        proj = bank[0:4]
        turn0, turn1, up0, up1 = bank[4:8]

        def quarters(b, rows=P):
            return b[0:rows, :].rearrange("p (a c) -> p a c", a=4)

        gain_in, weights_in, columns_in = sem("gain_in"), sem("weights_in"), [sem(f"columns_in{n}") for n in range(4)]
        COLUMNS = [(0, LATENTS)] + [(LATENTS + n * 512, 512) for n in range(3)]
        x_in, angles_in = sem("x_in"), sem("angles_in")
        x_squared, x_root, xn_done = sem("x_squared"), sem("x_root"), sem("xn_done")
        dve_link, x_link = sem("dve_link"), sem("x_link")
        x_turned, x_t_lo, x_t_hi = sem("x_turned"), sem("x_t_lo"), sem("x_t_hi")
        projected = sem("projected")
        lat_squared, lat_root, lat_normed, k_rotated = sem("lat_squared"), sem("lat_root"), sem("lat_normed"), sem("k_rotated")
        lat_turned, lat_t = sem("lat_turned"), sem("lat_t")
        q_up, kn_up, v_up = sem("q_up"), sem("kn_up"), sem("v_up")
        q_copied, q_rotated, kn_copied, v_copied = sem("q_copied"), sem("q_rotated"), sem("kn_copied"), sem("v_copied")
        q_sw_copied, k_sw_copied, v_sw_copied = sem("q_sw_copied"), sem("k_sw_copied"), sem("v_sw_copied")
        q_sw_turned, k_sw_turned, q_turned = sem("q_sw_turned"), sem("k_sw_turned"), sem("q_turned")
        q_sw_t_copied, k_sw_t_copied, q_t_lo, q_t_hi = sem("q_sw_t_copied"), sem("k_sw_t_copied"), sem("q_t_lo"), sem("q_t_hi")
        st = {n: sem(f"stored_{n}") for n in ("ckv", "kr", "k_sw", "v_sw", "q_t", "kn_t", "kr_t", "v", "q_sw_t", "k_sw_t")}
        N_W, LINKS = 4, 5
        block = ctx.enter_context(nc.Block())

        @block.sync
        def _(sp):
            def wait(sem, value):
                wait_apart(sp, t, sem, value)

            def load_x(row):
                sp.dma_start(x[:, :], t["x_all"][bass.ds(row, P), :]).then_inc(x_in, 16)

            def load_angles(row):
                sp.dma_start(angles[:, :], t["c_angles"][bass.ds(row, P), :]).then_inc(angles_in, 16)

            def store(done, row):
                at = bass.ds(row, P)
                wait(lat_normed, done)
                sp.dma_start(t["kv_all"][at, :], ckv[:, :]).then_inc(st["ckv"], 16)
                wait(k_rotated, done)
                sp.dma_start(t["kr_all"][at, :], kr[:, :]).then_inc(st["kr"], 16)
                wait(k_sw_copied, done)
                sp.dma_start(t["swk_all"][at, :], k_sw[:, :]).then_inc(st["k_sw"], 16)
                wait(v_sw_copied, done)
                sp.dma_start(t["swv_all"][at, :], v_sw[:, :]).then_inc(st["v_sw"], 16)
                wait(lat_t, done)
                sp.dma_start(t["kr_t"][:, at], kr_t[:, :]).then_inc(st["kr_t"], 16)
                wait(kn_copied, done)
                sp.dma_start(t["kn_t"].rearrange("(c p) n -> p c n", p=P)[:, :, at], kn_t[:, :, :]).then_inc(st["kn_t"], 16)
                wait(v_copied, done)
                sp.dma_start(t["v_mla"][at, :], v[:, :]).then_inc(st["v"], 16)
                wait(q_sw_t_copied, done)
                sp.dma_start(t["q_sw_t"].rearrange("(c p) n -> p c n", p=P)[:, :, at], q_sw_t[:, :, :]).then_inc(st["q_sw_t"], 16)
                wait(k_sw_t_copied, done)
                sp.dma_start(t["k_sw_t"].rearrange("(c p) n -> p c n", p=P)[:, :, at], k_sw_t[:, :, :]).then_inc(st["k_sw_t"], 16)
                wait(q_t_lo, done)
                wait(q_t_hi, done)
                sp.dma_start(t["q_t"].rearrange("h e n -> e h n")[:, :, at], q_t[:, :, :]).then_inc(st["q_t"], 16)

            load_x(0)
            load_angles(0)
            sp.dma_start(g_mix[:, :], row_broadcast(t["norm_mix"])).then_inc(gain_in, 16)
            for n, (c0, width) in enumerate(COLUMNS):
                sp.dma_start(w_in[:, :, c0:c0 + width], t["w_in"].rearrange("(k p) n -> p k n", p=P)[:, :, c0:c0 + width]).then_inc(columns_in[n], 16)
                if n == 0:
                    sp.dma_start(g_q[:, :], row_broadcast(t["norm_q_latent"])).then_inc(gain_in, 16)
                    sp.dma_start(g_kv[:, :], row_broadcast(t["norm_kv_latent"])).then_inc(gain_in, 16)
            sp.dma_start(w_uq0[:, :], t["w_uq"][0:P, :]).then_inc(weights_in, 16)
            sp.dma_start(w_uq1[:, :], t["w_uq"][P:Q_LORA, :]).then_inc(weights_in, 16)
            sp.dma_start(w_uk[:, :], t["w_uk"]).then_inc(weights_in, 16)
            sp.dma_start(w_uv[:, :], t["w_uv"]).then_inc(weights_in, 16)

            @stepped(sp, TILES - 1)
            def _(i):
                wait(xn_done, i + 1)
                load_x(i * P + P)
                store(i + 1, i * P)
                wait(q_rotated, i + 1)
                load_angles(i * P + P)
            store(TILES, (TILES - 1) * P)
            for s in st.values():
                sp.wait_ge(s, 16 * TILES)

        @block.scalar
        def _(act):
            def norm_x(i):
                act.wait_ge(x_in, 16 * i + 16)
                nc.scalar.activation(squares[:, :], x[:, :], ACT.Square, accum_out=stat[:, 0:1]).then_inc(x_squared, 1)
                act.wait_ge(x_link, 2 * i + 1)
                nc.scalar.activation(stat[:, 2:3], stat[:, 1:2], ACT.Sqrt).then_inc(x_root, 1)

            norm_x(0)

            @stepped_to_last(act, TILES)
            def _(i, is_last):
                act.wait_ge(x_turned, 2 * i + 2)
                nc.scalar.activation(x_t[:, 4:8, :], quarters(turn1), ACT.Copy).then_inc(x_t_hi, 1)
                act.wait_ge(projected, 4 * i + 1)
                nc.scalar.activation(squares[:, 0:Q_LORA], proj[0][:, 0:Q_LORA], ACT.Square, accum_out=stat2[:, 0:1]).then_inc(lat_squared, 1)
                nc.scalar.activation(squares[:, Q_LORA:Q_LORA + KV_LORA], proj[0][:, Q_LORA:Q_LORA + KV_LORA], ACT.Square,
                                     accum_out=stat2[:, 1:2]).then_inc(lat_squared, 1)
                act.wait_ge(dve_link, LINKS * i + 2)
                nc.scalar.activation(stat2[:, 4:6], stat2[:, 2:4], ACT.Sqrt).then_inc(lat_root, 1)
                if not is_last:
                    norm_x(i + 1)
                act.wait_ge(projected, 4 * i + 2)
                nc.scalar.activation(q_sw[:, :], proj[1][:, :], ACT.Copy, scale=SW_SCALE).then_inc(q_sw_copied, 1)
                act.wait_ge(projected, 4 * i + 4)
                after(act, st["v_sw"], 16 * i)
                nc.scalar.activation(v_sw[:, :], proj[3][:, :], ACT.Copy).then_inc(v_sw_copied, 1)
                act.wait_ge(q_up, i + 1)
                nc.scalar.activation(q[:, 0:4, :], up0[:, 0:4 * QK].rearrange("p (h e) -> p h e", h=4), ACT.Copy,
                                     scale=MLA_SCALE).then_inc(q_copied, 1)
                nc.scalar.activation(q[:, 4:8, :], up1[:, 0:4 * QK].rearrange("p (h e) -> p h e", h=4), ACT.Copy,
                                     scale=MLA_SCALE).then_inc(q_copied, 1)
                act.wait_ge(v_up, i + 1)
                after(act, st["v"], 16 * i)
                nc.scalar.activation(v[:, :], proj[0][:, :], ACT.Copy).then_inc(v_copied, 1)
                act.wait_ge(k_sw_turned, i + 1)
                after(act, st["k_sw_t"], 16 * i)
                nc.scalar.activation(k_sw_t[:, :, :], quarters(turn1), ACT.Copy).then_inc(k_sw_t_copied, 1)
                act.wait_ge(q_turned, 2 * i + 2)
                after(act, st["q_t"], 16 * i)
                nc.scalar.activation(q_t[:, 4:8, :], quarters(up1, QK), ACT.Copy).then_inc(q_t_hi, 1)

        @block.vector
        def _(dve):
            v_ = nc.vector

            def rotate(link, out_lo, out_hi, lo, hi, cos, sin, tmp, final):
                v_.tensor_tensor(tmp[0], lo, cos, ALU.mult)
                v_.tensor_tensor(tmp[1], hi, sin, ALU.mult)
                v_.tensor_tensor(tmp[2], lo, sin, ALU.mult)
                link(v_.tensor_tensor(tmp[3], hi, cos, ALU.mult))
                v_.tensor_tensor(out_lo, tmp[0], tmp[1], ALU.subtract)
                v_.tensor_tensor(out_hi, tmp[2], tmp[3], ALU.add).then_inc(final, 1)

            def norm_x(i):
                link = Chain(dve, x_link, 2 * i).link
                dve.wait_ge(x_squared, i + 1)
                link(v_.tensor_scalar(stat[:, 1:2], stat[:, 0:1], 1.0 / D_MODEL, EPS, ALU.mult, ALU.add))
                dve.wait_ge(x_root, i + 1)
                link(v_.reciprocal(stat[:, 0:1], stat[:, 2:3]))
                dve.wait_ge(gain_in, 16 * 3)
                after(dve, x_turned, 2 * i)
                v_.scalar_tensor_tensor(xn[:, :], x[:, :], stat[:, 0:1], g_mix[:, :], ALU.mult, ALU.mult).then_inc(xn_done, 1)

            norm_x(0)

            @stepped_to_last(dve, TILES)
            def _(i, is_last):
                chain = Chain(dve, dve_link, LINKS * i)
                link = chain.link
                dve.wait_ge(x_turned, 2 * i + 1)
                v_.tensor_copy(x_t[:, 0:4, :], quarters(turn0)).then_inc(x_t_lo, 1)
                dve.wait_ge(lat_squared, 2 * i + 2)
                link(v_.tensor_scalar(stat2[:, 2:3], stat2[:, 0:1], 1.0 / Q_LORA, EPS, ALU.mult, ALU.add))
                link(v_.tensor_scalar(stat2[:, 3:4], stat2[:, 1:2], 1.0 / KV_LORA, EPS, ALU.mult, ALU.add))
                dve.wait_ge(lat_root, i + 1)
                link(v_.reciprocal(stat2[:, 0:2], stat2[:, 4:6]))
                after(dve, st["ckv"], 16 * i)
                after(dve, lat_turned, i)
                v_.scalar_tensor_tensor(cq[:, :], proj[0][:, 0:Q_LORA], stat2[:, 0:1], g_q[:, :], ALU.mult, ALU.mult)
                v_.scalar_tensor_tensor(ckv[:, :], proj[0][:, Q_LORA:Q_LORA + KV_LORA], stat2[:, 1:2], g_kv[:, :],
                                        ALU.mult, ALU.mult).then_inc(lat_normed, 1)
                dve.wait_ge(angles_in, 16 * i + 16)
                after(dve, st["kr"], 16 * i)
                k0 = Q_LORA + KV_LORA
                rotate(link, kr[:, 0:HALF], kr[:, HALF:ROPE], proj[0][:, k0:k0 + HALF], proj[0][:, k0 + HALF:k0 + ROPE],
                       angles[:, 0:HALF], angles[:, HALF:ROPE], [rot_k[:, n, :] for n in range(4)], k_rotated)
                if not is_last:
                    norm_x(i + 1)
                dve.wait_ge(projected, 4 * i + 3)
                after(dve, st["k_sw"], 16 * i)
                after(dve, k_sw_turned, i)
                v_.tensor_copy(k_sw[:, :], proj[2][:, :]).then_inc(k_sw_copied, 1)
                dve.wait_ge(lat_turned, i + 1)
                after(dve, st["kr_t"], 16 * i)
                v_.tensor_copy(cq_t0[:, :], turn0[:, 0:P])
                v_.tensor_copy(cq_t1[:, :], turn0[0:Q_LORA - P, P:2 * P])
                v_.tensor_copy(ckv_t[:, :], turn0[:, 2 * P:3 * P])
                v_.tensor_copy(kr_t[:, :], turn0[0:ROPE, 3 * P:4 * P]).then_inc(lat_t, 1)
                dve.wait_ge(kn_up, i + 1)
                after(dve, st["kn_t"], 16 * i)
                v_.tensor_copy(kn_t[:, :, :], quarters(turn1)).then_inc(kn_copied, 1)
                dve.wait_ge(q_copied, 2 * i + 2)
                cos = angles[:, 0:HALF].unsqueeze(1).broadcast_to([P, HEADS, HALF])
                sin = angles[:, HALF:ROPE].unsqueeze(1).broadcast_to([P, HEADS, HALF])
                rotate(link, q[:, :, NOPE:NOPE + HALF], q[:, :, NOPE + HALF:QK], q[:, :, NOPE:NOPE + HALF],
                       q[:, :, NOPE + HALF:QK], cos, sin, [rot[:, n, :, :] for n in range(4)], q_rotated)
                dve.wait_ge(q_sw_turned, i + 1)
                after(dve, st["q_sw_t"], 16 * i)
                v_.tensor_copy(q_sw_t[:, :, :], quarters(turn0)).then_inc(q_sw_t_copied, 1)
                dve.wait_ge(q_turned, 2 * i + 1)
                after(dve, st["q_t"], 16 * i)
                v_.tensor_copy(q_t[:, 0:4, :], quarters(up0, QK)).then_inc(q_t_lo, 1)
                assert chain.n == LINKS

        @block.tensor
        def _(pe):
            mm, turn = nc.tensor.matmul, nc.tensor.transpose

            def turns(out_bank, src, step=P, rows=P):
                for a in range(4):
                    last = turn(quarters(out_bank, rows)[:, a, :], src(a), ident[:, :])
                return last

            @stepped(pe, TILES)
            def _(i):
                pe.wait_ge(xn_done, i + 1)
                after(pe, q_sw_t_copied, i)
                turns(turn0, lambda a: xn[:, a * P:(a + 1) * P]).then_inc(x_turned, 1)
                after(pe, k_sw_t_copied, i)
                turns(turn1, lambda a: xn[:, (4 + a) * P:(5 + a) * P]).then_inc(x_turned, 1)
                pe.wait_ge(x_t_lo, i + 1)
                pe.wait_ge(x_t_hi, i + 1)
                for n, free in enumerate((v_copied, q_sw_copied, k_sw_copied, v_sw_copied)):
                    after(pe, free, i)
                    pe.wait_ge(columns_in[n], 16)
                    c0, width = COLUMNS[n]
                    for k in range(KC):
                        last = mm(proj[n][:, 0:width], x_t[:, k, :], w_in[:, k, c0:c0 + width], start=(k == 0), stop=(k == KC - 1))
                    last.then_inc(projected, 1)
                pe.wait_ge(lat_normed, i + 1)
                pe.wait_ge(k_rotated, i + 1)
                turn(turn0[:, 0:P], cq[:, 0:P], ident[:, :])
                turn(turn0[0:Q_LORA - P, P:2 * P], cq[:, P:Q_LORA], ident[:, :])
                turn(turn0[:, 2 * P:3 * P], ckv[:, :], ident[:, :])
                turn(turn0[0:ROPE, 3 * P:4 * P], kr[:, :], ident[:, :]).then_inc(lat_turned, 1)
                pe.wait_ge(lat_t, i + 1)
                pe.wait_ge(weights_in, 16 * N_W)
                after(pe, q_t_lo, i)
                after(pe, q_t_hi, i)
                for n, out in enumerate((up0, up1)):
                    at = slice(n * 4 * QK, (n + 1) * 4 * QK)
                    mm(out[:, 0:4 * QK], cq_t0[:, :], w_uq0[:, at], start=True, stop=False)
                    last = mm(out[:, 0:4 * QK], cq_t1[:, :], w_uq1[:, at], start=False, stop=True)
                last.then_inc(q_up, 1)
                for a in range(4):
                    last = mm(turn1[:, a * P:(a + 1) * P], w_uk[:, a * P:(a + 1) * P], ckv_t[:, :], start=True, stop=True)
                last.then_inc(kn_up, 1)
                mm(proj[0][:, :], ckv_t[:, :], w_uv[:, :], start=True, stop=True).then_inc(v_up, 1)
                pe.wait_ge(q_sw_copied, i + 1)
                turns(turn0, lambda a: q_sw[:, a * P:(a + 1) * P]).then_inc(q_sw_turned, 1)
                pe.wait_ge(k_sw_copied, i + 1)
                pe.wait_ge(kn_copied, i + 1)
                turns(turn1, lambda a: k_sw[:, a * P:(a + 1) * P]).then_inc(k_sw_turned, 1)
                pe.wait_ge(q_rotated, i + 1)
                turns(up0, lambda a: q[:, a, :], rows=QK).then_inc(q_turned, 1)
                turns(up1, lambda a: q[:, 4 + a, :], rows=QK).then_inc(q_turned, 1)


def attend_prompt(nc, t, ident):
    with ExitStack() as ctx:
        def sb(name, shape, dt=F32):
            return ctx.enter_context(nc.sbuf_tensor(f"b_{name}", shape, dt))

        def pair(name, shape):
            return [sb(f"{name}{n}", shape) for n in range(2)]

        q_t, k_t = pair("q_t", [QK, SEQ]), pair("k_t", [QK, SEQ])
        v = pair("v", [P, PROMPT_TILES, 64])
        bias = pair("bias", [P, SEQ])
        scores, probs_t = pair("scores", [P, SEQ]), pair("probs_t", [P, PROMPT_TILES, P])
        out = pair("out", [P, PROMPT_TILES, 64])
        top, low = sb("top", [P, 16]), sb("low", [P, 16])
        total, inverse = sb("total", [P, 16]), sb("inverse", [P, 16])
        carrier = sb("carrier", [1, 1])
        score_bank = [ctx.enter_context(nc.psum_tensor(f"b_scorebank{n}", [P, SEQ], F32)) for n in range(2)]
        turn = [ctx.enter_context(nc.psum_tensor(f"b_turn{n}", [P, 4, P], F32)) for n in range(2)]
        out_bank = [ctx.enter_context(nc.psum_tensor(f"b_sum{n}", [P, 512], F32)) for n in range(2)]

        STEPS = [(u, tile) for u in range(2) for tile in range(PROMPT_TILES)]
        N = len(STEPS)
        WIDE = [s for s, (_, tile) in enumerate(STEPS) if tile >= 4]

        for kind in ("latent", "window"):
            latent = kind == "latent"
            dim = QK if latent else 64

            def sem(name):
                return nc.alloc_semaphore(f"b_{kind}_{name}")

            shared_in = sem("shared_in")
            head_in = [sem("head0_in"), sem("head1_in")]
            scored, maxed, lowered, exped, inverted = sem("scored"), sem("maxed"), sem("lowered"), sem("exped"), sem("inverted")
            turned0, turned1, copied0, copied1 = sem("turned0"), sem("turned1"), sem("copied0"), sem("copied1")
            summed, normed = sem("summed"), sem("normed")
            stored = [sem("stored0"), sem("stored1")]
            LOADS = 3 if latent else 4

            def wide_before(s):
                return sum(1 for w in WIDE if w < s)

            with nc.Block() as block:
                @block.sync
                def _(sp):
                    if latent:
                        for u in range(2):
                            sp.dma_start(k_t[u][NOPE:QK, :], t["kr_t"][:, 0:SEQ]).then_inc(shared_in, 16)
                            sp.dma_start(bias[u][:, :], t["c_causal"][0]).then_inc(shared_in, 16)
                    values = (t["v_mla"] if latent else t["swv_all"]).rearrange("(a p) n -> p a n", p=P)

                    @stepped(sp, 4)
                    def _(i):
                        for u in range(2):
                            if not isinstance(i, int):
                                wait_apart(sp, t, summed, N * i - (N // 2) * (1 - u))
                            h = i * 2 + u
                            if latent:
                                sp.dma_start(q_t[u][:, :], t["q_t"][bass.ds(h, 1), :, 0:SEQ].rearrange("a e n -> e (a n)")).then_inc(head_in[u], 16)
                                sp.dma_start(k_t[u][0:NOPE, :], t["kn_t"][bass.ds(h * NOPE, NOPE), 0:SEQ]).then_inc(head_in[u], 16)
                            else:
                                sp.dma_start(q_t[u][0:64, :], t["q_sw_t"][bass.ds(h * 64, 64), 0:SEQ]).then_inc(head_in[u], 16)
                                sp.dma_start(k_t[u][0:64, :], t["k_sw_t"][bass.ds(h * 64, 64), 0:SEQ]).then_inc(head_in[u], 16)
                                sp.dma_start(bias[u][:, :], t["c_window"][bass.ds(h, 1), :, :].rearrange("a e n -> e (a n)")).then_inc(head_in[u], 16)
                            sp.dma_start(v[u][:, :, :], values[:, 0:PROMPT_TILES, bass.ds(h * 64, 64)]).then_inc(head_in[u], 16)

                @block.scalar
                def _(act):
                    o_cat = t["o_cat"].rearrange("(a p) n -> p a n", p=P)
                    new, old = ("sw_k_new", "state_sw_k") if latent else ("sw_v_new", "state_sw_v")

                    def copy_wide(act, i, s):
                        w = len(WIDE) * i + wide_before(s)
                        n = STEPS[s][1] - 3
                        act.wait_ge(turned1, w + 1)
                        after(act, summed, N * i + max(s - 1, 0))
                        nc.scalar.activation(probs_t[s % 2][:, 4:4 + n, :], turn[1][:, 0:n, :], ACT.Copy).then_inc(copied1, 1)

                    def store(act, i, u):
                        act.wait_ge(normed, N * i + PROMPT_TILES * (u + 1))
                        at = i * 128 + (u * 64 + (0 if latent else 512))
                        act.dma_start(o_cat[:, 0:PROMPT_TILES, bass.ds(at, 64)], out[u][:, :, :]).then_inc(stored[u], 16)

                    @stepped(act, 4)
                    def _(i):
                        for s, (u, tile) in enumerate(STEPS):
                            b, width = s % 2, P * (tile + 1)
                            act.wait_ge(lowered, N * i + s + 1)
                            nc.scalar.activation(scores[b][:, 0:width], scores[b][:, 0:width], ACT.Exp, bias=low[:, s:s + 1],
                                                 accum_out=total[:, s:s + 1]).then_inc(exped, 1)
                            if s >= 1 and STEPS[s - 1][1] >= 4:
                                copy_wide(act, i, s - 1)
                            if s == 9:
                                store(act, i, 0)
                            if s % PROMPT_TILES == 1:
                                act.dma_start(t[new][bass.ds(2 * i + u, 1), 0:WINDOW - DEC_SEQ, :].rearrange("b (a n) f -> (b a) (n f)", a=120),
                                              t[old][bass.ds(2 * i + u, 1), DEC_SEQ:WINDOW, :].rearrange("b (a n) f -> (b a) (n f)", a=120)).then_inc(t["shifted"], 16)
                        copy_wide(act, i, N - 1)
                        store(act, i, 1)

                    for u in range(2):
                        act.wait_ge(stored[u], 16 * 4)

                @block.vector
                def _(dve):
                    v_ = nc.vector

                    def copy_first(i, s):
                        n = min(STEPS[s][1] + 1, 4)
                        dve.wait_ge(turned0, N * i + s + 1)
                        after(dve, summed, N * i + max(s - 1, 0))
                        v_.tensor_copy(probs_t[s % 2][:, 0:n, :], turn[0][:, 0:n, :]).then_inc(copied0, 1)

                    def norm(i, s):
                        u, tile = STEPS[s]
                        dve.wait_ge(exped, N * i + s + 1)
                        v_.reciprocal(inverse[:, s:s + 1], total[:, s:s + 1]).then_inc(inverted, 1)
                        dve.wait_ge(inverted, N * i + s + 1)
                        dve.wait_ge(summed, N * i + s + 1)
                        if tile == 0:
                            after(dve, stored[u], 16 * i)
                        v_.tensor_scalar(out[u][:, tile, :], out_bank[s % 2][:, 0:64], inverse[:, s:s + 1], None, ALU.mult).then_inc(normed, 1)

                    @stepped(dve, 4)
                    def _(i):
                        dve.wait_ge(head_in[0], 16 * LOADS * i + 16 * LOADS)
                        if latent:
                            dve.wait_ge(shared_in, 16 * 4)
                        for s, (u, tile) in enumerate(STEPS):
                            b, width = s % 2, P * (tile + 1)
                            if s == PROMPT_TILES:
                                dve.wait_ge(head_in[1], 16 * LOADS * i + 16 * LOADS)
                            if s >= 2:
                                dve.wait_ge(turned0, N * i + s - 1)
                                if STEPS[s - 2][1] >= 4:
                                    dve.wait_ge(turned1, len(WIDE) * i + wide_before(s - 1))
                            dve.wait_ge(scored, N * i + s + 1)
                            v_.memset(carrier[:, :], 0.0)
                            v_.tensor_tensor_reduce(scores[b][:, 0:width], score_bank[b][:, 0:width], bias[u][:, SEQ - width:SEQ], 1.0, -3e38,
                                                    ALU.add, ALU.max, top[:, s:s + 1]).then_inc(maxed, 1)
                            dve.wait_ge(maxed, N * i + s + 1)
                            v_.tensor_scalar(low[:, s:s + 1], top[:, s:s + 1], -1.0, None, ALU.mult).then_inc(lowered, 1)
                            if s >= 1:
                                copy_first(i, s - 1)
                            if s >= 2:
                                norm(i, s - 2)
                        copy_first(i, N - 1)
                        norm(i, N - 2)
                        norm(i, N - 1)

                @block.tensor
                def _(pe):
                    mm, transpose = nc.tensor.matmul, nc.tensor.transpose

                    def score(i, s):
                        u, tile = STEPS[s]
                        if tile == 0:
                            pe.wait_ge(head_in[u], 16 * LOADS * i + 16 * LOADS)
                            if latent:
                                pe.wait_ge(shared_in, 16 * 4)
                        after(pe, maxed, N * i + max(s - 1, 0))
                        width = P * (tile + 1)
                        for c in range(0, width, 512):
                            w = min(512, width - c)
                            last = mm(score_bank[s % 2][:, c:c + w], q_t[u][0:dim, tile * P:(tile + 1) * P], k_t[u][0:dim, c:c + w],
                                      start=True, stop=True)
                        last.then_inc(scored, 1)

                    def turns(i, s):
                        tile = STEPS[s][1]
                        pe.wait_ge(exped, N * i + s + 1)
                        after(pe, copied0, N * i + s)
                        for k in range(min(tile + 1, 4)):
                            last = transpose(turn[0][:, k, :], scores[s % 2][:, k * P:(k + 1) * P], ident[:, :])
                        last.then_inc(turned0, 1)
                        if tile >= 4:
                            after(pe, copied1, len(WIDE) * i + wide_before(s))
                            for k in range(4, tile + 1):
                                last = transpose(turn[1][:, k - 4, :], scores[s % 2][:, k * P:(k + 1) * P], ident[:, :])
                            last.then_inc(turned1, 1)

                    def sums(i, s):
                        u, tile = STEPS[s]
                        pe.wait_ge(copied0, N * i + s + 1)
                        after(pe, normed, N * i + max(s - 1, 0))
                        for k in range(tile + 1):
                            if k == 4:
                                pe.wait_ge(copied1, len(WIDE) * i + wide_before(s) + 1)
                            last = mm(out_bank[s % 2][:, 0:64], probs_t[s % 2][:, k, :], v[u][:, k, :], start=(k == 0), stop=(k == tile))
                        last.then_inc(summed, 1)

                    @stepped(pe, 4)
                    def _(i):
                        score(i, 0)
                        for s in range(N):
                            if s + 1 < N:
                                score(i, s + 1)
                            turns(i, s)
                            if s >= 1:
                                sums(i, s - 1)
                        sums(i, N - 1)


CHUNKS = 4
TILES_CHUNK = 16
HT = HEADS * DEC_SEQ


def attend_latent(nc, t, ident):
    with ExitStack() as ctx:
        def sb(name, shape, dt=F32):
            return ctx.enter_context(nc.sbuf_tensor(f"lat_{name}", shape, dt))

        def sem(name):
            return phase_semaphore(nc, t["phase_sems"], f"lat_{name}")

        page_rows, page_part = sb("page_rows", [P, 4 * DEC_BATCH], I32), sb("page_part", [P, 1])
        gather_rows = sb("gather_rows", [P, 4 * DEC_BATCH], I32)
        rows_of = [sb(f"rows{u}", [P, CHUNKS], I32) for u in range(2)]
        kv_of = [[sb(f"kv{u}{c}", [P, TILES_CHUNK * KV_LORA]) for c in range(CHUNKS)] for u in range(2)]
        kr_of = [[sb(f"kr{u}{c}", [P, TILES_CHUNK * ROPE]) for c in range(CHUNKS)] for u in range(2)]
        kv_t = [sb(f"kv_t{n}", [P, TILES_CHUNK, P]) for n in range(2)]
        kr_t = [sb(f"kr_t{n}", [P, 4, P]) for n in range(2)]
        q_nope, q_rope = sb("q_nope", [NOPE, HEADS, N_SAMPLE]), sb("q_rope", [P, HEADS, N_SAMPLE])
        w_uk_t, w_uv = sb("w_uk_t", [NOPE, HEADS, KV_LORA]), sb("w_uv", [P, 512])
        q_lat = sb("q_lat", [P, DEC_BATCH, HT])
        q_pad = sb("q_pad", [P, DEC_BATCH, 4, HT])
        new_rows, new_t, new_kr_t = sb("new_rows", [N_SAMPLE, KV_LORA]), sb("new_t", [P, N_SAMPLE]), sb("new_kr_t", [ROPE, N_SAMPLE])
        new_kv, new_kv_of = sb("new_kv", [DEC_SEQ, DEC_BATCH, KV_LORA]), [sb(f"new_kv{u}", [DEC_SEQ, KV_LORA]) for u in range(2)]
        new_mask, new_scores = sb("new_mask", [DEC_SEQ, HT]), sb("new_scores", [DEC_SEQ, DEC_BATCH, HT])
        scores_of = [sb(f"scores{u}", [P, CHUNKS * TILES_CHUNK + 1, HT]) for u in range(2)]
        part_max, part_sum = sb("part_max", [P, CHUNKS + 1, HT]), sb("part_sum", [P, CHUNKS + 1, HT])
        all_max, all_sum = sb("all_max", [P, P]), sb("all_sum", [P, HT])
        carrier = sb("carrier", [P, 1])
        top, top_wide = sb("top", [HT, 1]), sb("top_wide", [HT, P])
        ones, inverse = sb("ones", [P, P]), sb("inverse", [P, HT])
        o_lat = sb("o_lat", [P, HEADS, DEC_BATCH, DEC_SEQ])
        out = sb("out", [N_SAMPLE, 512])

        def bank(name):
            return ctx.enter_context(nc.psum_tensor(f"lat_{name}", [P, 512], F32))

        turn, turn_kr = [bank("turn0"), bank("turn1")], bank("turn_kr")
        score_bank = [bank("score0"), bank("score1")]
        misc, out_bank = bank("misc"), bank("out_bank")
        max_t_bank, max_t, spread, total = misc[:, 0:P], misc[0:HT, 0:P], misc[:, P:P + HT], misc[:, P + HT:P + 2 * HT]

        inputs_in, rows_ready, rows_copied = sem("inputs_in"), sem("rows_ready"), sem("rows_copied")
        gathered_kv, gathered_kr = [[[sem(f"gathered_{k}{u}{c}") for c in range(CHUNKS)] for u in range(2)] for k in ("kv", "kr")]
        kr_turned, kr_copied = sem("kr_turned"), sem("kr_copied")
        even_turned, odd_turned, even_copied, odd_copied = sem("even_turned"), sem("odd_turned"), sem("even_copied"), sem("odd_copied")
        scored, score_copied = sem("scored"), sem("score_copied")
        maxed, max_turned, topped, top_spread = sem("maxed"), sem("max_turned"), sem("topped"), sem("top_spread")
        lowered, exped, summed_parts, totalled = sem("lowered"), sem("exped"), sem("summed_parts"), sem("totalled")
        used, weighted, normed = [sem(f"used{c}") for c in range(CHUNKS)], sem("weighted"), sem("normed")
        dve_link, new_placed, inverted = sem("dve_link"), sem("new_placed"), sem("inverted")
        top_found, parts_added = sem("top_found"), sem("parts_added")
        q_lat_done, q_lat_copied, new_turned, new_t_copied, new_scored, q_padded = (
            sem("q_lat_done"), sem("q_lat_copied"), sem("new_turned"), sem("new_t_copied"), sem("new_scored"), sem("q_padded"))
        ones_set, out_done, out_copied, stored = sem("ones_set"), sem("out_done"), sem("out_copied"), sem("stored")
        sample = slice(SEQ, SEQ + N_SAMPLE)
        LINKS = 3
        N_IN = 13
        C2, C5 = 2 * CHUNKS, CHUNKS + 1

        def by_requests(eng, step):
            @stepped(eng, DEC_BATCH // 2)
            def _(i):
                for u in range(2):
                    step(2 * i + u, u, i)

        def has_previous(n):
            return not (isinstance(n, int) and n == 0)

        with nc.Block() as block:
            @block.sync
            def _(sp):
                def load(dst, src):
                    sp.dma_start(dst, src).then_inc(inputs_in, 16)

                load(page_rows[:, :], t["page_rows"])
                load(page_part[:, :], t["c_page_part"])
                load(q_nope[:, :, :], t["q_t"][:, 0:NOPE, sample].rearrange("h e n -> e h n"))
                load(w_uk_t[:, :, :], t["w_uk_t"])
                for u in range(4):
                    load(q_rope[u * ROPE:(u + 1) * ROPE, :, :], t["q_t"][:, NOPE:QK, sample].rearrange("h e n -> e h n"))
                load(new_rows[:, :], t["kv_all"][sample, :])
                load(new_kr_t[:, :], t["kr_t"][:, sample])
                load(new_kv[:, :, :], t["kv_all"][sample, :].rearrange("(b t) c -> t b c", t=DEC_SEQ))
                load(new_mask[:, :], t["c_new_mask"])
                load(w_uv[:, :], t["w_uv"])
                sp.wait_ge(out_copied, 1)
                sp.dma_start(t["o_cat"][sample, 0:512], out[:, :]).then_inc(stored, 16)
                sp.wait_ge(stored, 16)

            @block.gpsimd
            def _(gp):
                gp.wait_ge(rows_ready, 1)

                def step(n, u, r):
                    for c in range(CHUNKS):
                        after(gp, used[c], n - 1)
                        nc.gpsimd.tensor_copy(rows_of[u][:, c:c + 1], gather_rows[:, bass.ds(n * CHUNKS + c, 1)]).then_inc(rows_copied, 1)
                        gp.wait_ge(rows_copied, n * CHUNKS + (c + 1))
                        nc.gpsimd.tensor_tensor(carrier[:, 0:1], page_part[:, 0:1], page_part[:, 0:1], ALU.add)
                        offset = bass.IndirectOffsetOnAxis(ap=rows_of[u][:, c:c + 1], axis=0)
                        gp.indirect_dma_start(out=kv_of[u][c][:, :], out_offset=None, in_=t["cache_kv"], in_offset=offset).then_inc(gathered_kv[u][c], 16)
                        gp.indirect_dma_start(out=kr_of[u][c][:, :], out_offset=None, in_=t["cache_kr"], in_offset=offset).then_inc(gathered_kr[u][c], 16)

                by_requests(gp, step)

            @block.tensor
            def _(pe):
                mm, transpose = nc.tensor.matmul, nc.tensor.transpose
                pe.wait_ge(inputs_in, 16 * N_IN)
                for h in range(HEADS):
                    last = mm(score_bank[0][:, h * 64:(h + 1) * 64], w_uk_t[:, h, :], q_nope[:, h, :], start=True, stop=True)
                last.then_inc(q_lat_done, 1)
                transpose(score_bank[1][:, 0:N_SAMPLE], new_rows[:, :], ident[0:N_SAMPLE, 0:N_SAMPLE]).then_inc(new_turned, 1)
                pe.wait_ge(q_lat_copied, 1)
                pe.wait_ge(new_t_copied, 1)
                for b in range(DEC_BATCH):
                    at = slice(b * DEC_SEQ, (b + 1) * DEC_SEQ)
                    place = score_bank[1][0:DEC_SEQ, b * HT:(b + 1) * HT]
                    mm(place, new_t[:, at], q_lat[:, b, :], start=True, stop=False)
                    last = mm(place.rearrange("p (h t) -> p h t", h=HEADS), new_kr_t[:, at], q_rope[0:ROPE, :, at], start=False, stop=True)
                last.then_inc(new_scored, 1)
                pe.wait_ge(new_placed, 1)
                pe.wait_ge(q_padded, 1)
                pe.wait_ge(ones_set, 1)

                def turn_rotary(n, u, r, c):
                    kr = kr_of[u]
                    pe.wait_ge(gathered_kr[u][c], 16 * r + 16)
                    after(pe, kr_copied, CHUNKS * n + c)
                    for g in range(4):
                        last = transpose(turn_kr[:, g * P:(g + 1) * P], kr[c][:, g * P:(g + 1) * P], ident[:, :])
                    last.then_inc(kr_turned, 1)
                    pe.wait_ge(gathered_kv[u][c], 16 * r + 16)

                def turns(n, u, c, half):
                    kv = kv_of[u]
                    for g in (2 * half, 2 * half + 1):
                        copied, turned = ((even_copied, even_turned), (odd_copied, odd_turned))[g % 2]
                        after(pe, copied, C2 * n + (2 * c + g // 2))
                        for a in range(4):
                            at = (4 * g + a) * P
                            last = transpose(turn[g % 2][:, a * P:(a + 1) * P], kv[c][:, at:at + P], ident[:, :])
                        last.then_inc(turned, 1)

                def score(n, c, half):
                    pe.wait_ge(kr_copied, CHUNKS * n + (c + 1))
                    pe.wait_ge(even_copied, C2 * n + (2 * c + half + 1))
                    pe.wait_ge(odd_copied, C2 * n + (2 * c + half + 1))
                    after(pe, score_copied, C2 * n + (2 * c + half - 1))
                    for g in (2 * half, 2 * half + 1):
                        place = score_bank[half][:, (g % 2) * 4 * HT:(g % 2 + 1) * 4 * HT]
                        mm(place, kr_t[c % 2][:, g, :], q_pad[:, bass.ds(n, 1), :, :].rearrange("p a u q -> p (a u q)"), start=True, stop=False,
                           skip_group_check=True)
                        for a in range(4):
                            last = mm(place[:, a * HT:(a + 1) * HT], kv_t[c % 2][:, 4 * g + a, :],
                                      q_lat[:, bass.ds(n, 1), :].rearrange("p a q -> p (a q)"), start=False, stop=(a == 3), skip_group_check=True)
                    last.then_inc(scored, 1)

                def spread_top(n):
                    pe.wait_ge(topped, n)
                    mm(spread, top_wide[:, :], ident[0:HT, 0:HT], start=True, stop=True).then_inc(top_spread, 1)

                def weigh(n, u):
                    kv, scores = kv_of[u], scores_of[u]
                    after(pe, normed, n - 1)
                    for c in range(CHUNKS):
                        pe.wait_ge(exped, C5 * n - (CHUNKS - c))
                        for k in range(TILES_CHUNK):
                            last = mm(out_bank[:, 0:HT], kv[c][:, k * P:(k + 1) * P], scores[:, c * TILES_CHUNK + k, :],
                                      start=(c == 0 and k == 0), stop=False)
                        last.then_inc(used[c], 1)
                    pe.wait_ge(exped, C5 * n)
                    mm(out_bank[:, 0:HT], new_kv_of[u][:, :], scores[0:DEC_SEQ, CHUNKS * TILES_CHUNK, :], start=False, stop=True).then_inc(weighted, 1)

                def total_up(n):
                    pe.wait_ge(summed_parts, n)
                    mm(total, ones[:, :], all_sum[:, :], start=True, stop=True).then_inc(totalled, 1)

                def step(n, u, r):
                    turn_rotary(n, u, r, 0)
                    turns(n, u, 0, 0)
                    turns(n, u, 0, 1)
                    if has_previous(n):
                        spread_top(n)
                    for c in range(CHUNKS):
                        if c + 1 < CHUNKS:
                            turn_rotary(n, u, r, c + 1)
                        for half in range(2):
                            if c + 1 < CHUNKS:
                                turns(n, u, c + 1, half)
                            score(n, c, half)
                    if has_previous(n):
                        weigh(n, 1 - u)
                    pe.wait_ge(maxed, n + 1)
                    transpose(max_t_bank, all_max[:, :], ident[:, :]).then_inc(max_turned, 1)
                    if has_previous(n):
                        total_up(n)

                by_requests(pe, step)
                spread_top(DEC_BATCH)
                weigh(DEC_BATCH, 1)
                total_up(DEC_BATCH)

                pe.wait_ge(normed, DEC_BATCH)
                for h in range(HEADS):
                    last = mm(score_bank[0][0:N_SAMPLE, h * 64:(h + 1) * 64], o_lat[:, h, :, :].rearrange("p b t -> p (b t)"),
                              w_uv[:, h * 64:(h + 1) * 64], start=True, stop=True)
                last.then_inc(out_done, 1)

            @block.scalar
            def _(act):
                copy = ACT.Copy

                def evacuate_rotary(n, c):
                    act.wait_ge(kr_turned, CHUNKS * n + (c + 1))
                    after(act, scored, C2 * n + (2 * c - 2))
                    nc.scalar.activation(kr_t[c % 2][:, :, :], turn_kr[:, :].rearrange("p (g k) -> p g k", g=4), copy).then_inc(kr_copied, 1)

                def evacuate(n, c, half):
                    g = 2 * half + 1
                    act.wait_ge(odd_turned, C2 * n + (2 * c + half + 1))
                    nc.scalar.activation(kv_t[c % 2][:, 4 * g:4 * g + 4, :], turn[1][:, :].rearrange("p (g k) -> p g k", g=4), copy).then_inc(odd_copied, 1)

                def exps(n, u, c):
                    scores = scores_of[u]
                    act.wait_ge(lowered, C5 * n - (CHUNKS - c))
                    at = slice(c * TILES_CHUNK, min((c + 1) * TILES_CHUNK, CHUNKS * TILES_CHUNK + 1))
                    nc.scalar.activation(scores[:, at, :], scores[:, at, :], ACT.Exp).then_inc(exped, 1)

                def step(n, u, r):
                    scores = scores_of[u]
                    evacuate_rotary(n, 0)
                    evacuate(n, 0, 0)
                    evacuate(n, 0, 1)
                    after(act, weighted, n - 1)
                    after(act, summed_parts, n - 1)
                    for c in range(CHUNKS):
                        if c + 1 < CHUNKS:
                            evacuate_rotary(n, c + 1)
                        for half in range(2):
                            if c + 1 < CHUNKS:
                                evacuate(n, c + 1, half)
                            act.wait_ge(scored, C2 * n + (2 * c + half + 1))
                            at = c * TILES_CHUNK + 8 * half
                            nc.scalar.activation(scores[:, at:at + 8, :], score_bank[half][:, :].rearrange("p (u q) -> p u q", u=8), copy).then_inc(score_copied, 1)
                        if has_previous(n):
                            exps(n, 1 - u, c)
                    if has_previous(n):
                        exps(n, 1 - u, CHUNKS)

                by_requests(act, step)
                for c in range(CHUNKS + 1):
                    exps(DEC_BATCH, 1, c)

            @block.vector
            def _(dve):
                v_ = nc.vector
                dve.wait_ge(inputs_in, 16 * N_IN)
                v_.tensor_scalar(gather_rows[:, :], page_rows[:, :], float(PAGE // TILES_CHUNK), page_part[:, 0:1], ALU.mult, ALU.add).then_inc(rows_ready, 1)
                v_.memset(ones[:, :], 1.0).then_inc(ones_set, 1)
                setup = Chain(dve, sem("setup_link"))
                setup.link(v_.memset(all_max[:, :], 0.0))
                setup.link(v_.memset(q_pad[:, :, :, :], 0.0))
                for u in range(4):
                    rows = slice(u * ROPE, (u + 1) * ROPE)
                    last = v_.tensor_copy(q_pad[rows, :, u, :].rearrange("p b (h t) -> p b h t", h=HEADS),
                                          q_rope[rows, :, :].rearrange("p h (b t) -> p b h t", b=DEC_BATCH))
                last.then_inc(q_padded, 1)
                dve.wait_ge(q_lat_done, 1)
                v_.tensor_copy(q_lat[:, :, :].rearrange("p b (h t) -> p b h t", h=HEADS),
                               score_bank[0][:, :].rearrange("p (h b t) -> p b h t", h=HEADS, b=DEC_BATCH)).then_inc(q_lat_copied, 1)
                dve.wait_ge(new_turned, 1)
                v_.tensor_copy(new_t[:, :], score_bank[1][:, 0:N_SAMPLE]).then_inc(new_t_copied, 1)
                dve.wait_ge(new_scored, 1)
                v_.tensor_tensor(new_scores[:, :, :], score_bank[1][0:DEC_SEQ, :].rearrange("p (b q) -> p b q", b=DEC_BATCH),
                                 new_mask[:, :].unsqueeze(1).broadcast_to([DEC_SEQ, DEC_BATCH, HT]), ALU.add).then_inc(new_placed, 1)
                dve.wait_ge(new_placed, 1)
                NEW = CHUNKS * TILES_CHUNK

                def evacuate(n, c, half):
                    g = 2 * half
                    after(dve, scored, C2 * n + (2 * c + half - 3))
                    dve.wait_ge(even_turned, C2 * n + (2 * c + half + 1))
                    v_.tensor_copy(kv_t[c % 2][:, 4 * g:4 * g + 4, :], turn[0][:, :].rearrange("p (g k) -> p g k", g=4)).then_inc(even_copied, 1)

                def chunk(u, c):
                    return scores_of[u][:, c * TILES_CHUNK:(c + 1) * TILES_CHUNK, :]

                def by_column(ap):
                    return ap.rearrange("p u q -> p q u")

                def find_top(n):
                    dve.wait_ge(max_turned, n)
                    v_.tensor_reduce(top[:, :], max_t, AX.X, ALU.max).then_inc(top_found, 1)
                    dve.wait_ge(top_found, n)
                    v_.tensor_copy(top_wide[:, :], top[:, 0:1].broadcast_to([HT, P])).then_inc(topped, 1)

                def lower(n, u, c):
                    if c < CHUNKS:
                        v_.tensor_tensor(chunk(u, c), chunk(u, c), spread.unsqueeze(1).broadcast_to([P, TILES_CHUNK, HT]), ALU.subtract).then_inc(lowered, 1)
                    else:
                        v_.tensor_tensor(scores_of[u][:, NEW, :], scores_of[u][:, NEW, :], spread, ALU.subtract).then_inc(lowered, 1)

                def add_up(n, u, c):
                    dve.wait_ge(exped, C5 * n - (CHUNKS - c))
                    if c < CHUNKS:
                        v_.tensor_reduce(part_sum[:, c, :], by_column(chunk(u, c)), AX.X, ALU.add)
                    else:
                        v_.tensor_copy(part_sum[:, CHUNKS, :], scores_of[u][:, NEW, :]).then_inc(parts_added, 1)
                        dve.wait_ge(parts_added, n)
                        v_.tensor_reduce(all_sum[:, :], by_column(part_sum[:, :, :]), AX.X, ALU.add).then_inc(summed_parts, 1)

                def normalise(n):
                    dve.wait_ge(totalled, n)
                    v_.reciprocal(inverse[:, :], total).then_inc(inverted, 1)
                    dve.wait_ge(inverted, n)
                    dve.wait_ge(weighted, n)
                    v_.tensor_tensor(o_lat[:, :, bass.ds(n - 1, 1), :].rearrange("p h a t -> p h (a t)"), out_bank[:, 0:HT].rearrange("p (h t) -> p h t", h=HEADS),
                                     inverse[:, :].rearrange("p (h t) -> p h t", h=HEADS), ALU.mult).then_inc(normed, 1)

                def step(n, u, r):
                    scores, link = scores_of[u], Chain(dve, dve_link, LINKS * n).link
                    if has_previous(n):
                        find_top(n)
                    v_.tensor_copy(new_kv_of[u][:, :], new_kv[:, bass.ds(n, 1), :].rearrange("p a c -> p (a c)"))
                    link(v_.memset(scores[:, NEW, :], MASK))
                    link(v_.tensor_copy(scores[0:DEC_SEQ, NEW, :], new_scores[:, bass.ds(n, 1), :].rearrange("p a q -> p (a q)")))
                    v_.tensor_copy(part_max[:, CHUNKS, :], scores[:, NEW, :])
                    evacuate(n, 0, 0)
                    evacuate(n, 0, 1)
                    if has_previous(n):
                        dve.wait_ge(top_spread, n)
                    for c in range(CHUNKS):
                        if c + 1 < CHUNKS:
                            evacuate(n, c + 1, 0)
                        if has_previous(n):
                            lower(n, 1 - u, c)
                        if c + 1 < CHUNKS:
                            evacuate(n, c + 1, 1)
                        if has_previous(n):
                            if c > 0:
                                add_up(n, 1 - u, c - 1)
                        dve.wait_ge(score_copied, C2 * n + (2 * c + 2))
                        last = v_.tensor_reduce(part_max[:, c, :], by_column(chunk(u, c)), AX.X, ALU.max)
                    link(last)
                    v_.tensor_reduce(all_max[:, 0:HT], by_column(part_max[:, :, :]), AX.X, ALU.max).then_inc(maxed, 1)
                    if has_previous(n):
                        lower(n, 1 - u, CHUNKS)
                        add_up(n, 1 - u, CHUNKS - 1)
                        add_up(n, 1 - u, CHUNKS)
                        normalise(n)

                by_requests(dve, step)
                find_top(DEC_BATCH)
                dve.wait_ge(top_spread, DEC_BATCH)
                for c in range(CHUNKS + 1):
                    lower(DEC_BATCH, 1, c)
                for c in range(CHUNKS + 1):
                    add_up(DEC_BATCH, 1, c)
                normalise(DEC_BATCH)

                dve.wait_ge(out_done, 1)
                v_.tensor_copy(out[:, :], score_bank[0][0:N_SAMPLE, :]).then_inc(out_copied, 1)


def attend_window(nc, t, ident):
    with ExitStack() as ctx:
        def sb(name, shape, dt=F32):
            return ctx.enter_context(nc.sbuf_tensor(f"win_{name}", shape, dt))

        def sem(name):
            return phase_semaphore(nc, t["phase_sems"], f"win_{name}")

        bias, own_head = sb("bias", [HT, WIN_ALL]), sb("own_head", [HT, 512])
        q_heads = sb("q_heads", [P, 4, N_SAMPLE])
        q_all = sb("q_all", [P, DEC_BATCH, 4, HT])
        q_now = sb("q_now", [P, 4, HT])
        k_t = sb("k_t", [P, 4, WIN_ALL])
        v_old, v_near, v_new = sb("v_old", [OLD_J, DEC_SEQ, 512]), sb("v_near", [P, NEAR_TILES, 512]), sb("v_new", [DEC_SEQ, 512])
        scores = sb("scores", [P, WIN_ALL])
        top, low, total, inverse = sb("top", [HT, 1]), sb("low", [HT, 1]), sb("total", [HT, 1]), sb("inverse", [HT, 1])
        OLD, NEAR = DEC_SEQ, NEAR_TILES
        probs_t = sb("probs_t", [P, OLD + NEAR + 1, HT])
        own, out = sb("own", [HT, HEADS, 64]), sb("out", [HT, 64])
        carrier = sb("carrier", [1, 1])
        score_bank = ctx.enter_context(nc.psum_tensor("win_score_bank", [P, 1536], F32))
        turn_old = ctx.enter_context(nc.psum_tensor("win_turn_old", [P, 512], F32))
        turn_near = ctx.enter_context(nc.psum_tensor("win_turn_near", [P, 512], F32))
        sum_bank = ctx.enter_context(nc.psum_tensor("win_sum_bank", [P, 512], F32))

        inputs_in, keys_in, values_in = sem("inputs_in"), sem("keys_in"), sem("values_in")
        q_placed, q_copied = sem("q_placed"), sem("q_copied")
        scored, maxed, lowered, exped = sem("scored"), sem("maxed"), sem("lowered"), sem("exped")
        turned_old, turned_near, copied_old, copied_near = sem("turned_old"), sem("turned_near"), sem("copied_old"), sem("copied_near")
        summed, masked, normed, stored, dve_link = sem("summed"), sem("masked"), sem("normed"), sem("stored"), sem("dve_link")
        sample = slice(SEQ, SEQ + N_SAMPLE)
        N_IN, K_IN, V_IN, LINKS = 3, 2, 3, 2
        PIECES = [(0, 512), (512, 512), (1024, WIN_ALL - 1024)]
        OLD_END = OLD_KEYS

        with nc.Block() as block:
            @block.sync
            def _(sp):
                sp.dma_start(bias[:, :], t["c_window_sample"]).then_inc(inputs_in, 16)
                sp.dma_start(own_head[:, :], t["c_own_head"]).then_inc(inputs_in, 16)
                sp.dma_start(q_heads[:, :, :], t["q_sw_t"][:, sample].rearrange("(c p) n -> p c n", p=P)).then_inc(inputs_in, 16)
                old_rows = t["state_sw_v"].rearrange("b (j r) f -> b j r f", r=16)
                near_rows = t["state_sw_v"].rearrange("b (a p) f -> b p a f", p=P)
                new_k = t["k_sw_t"].rearrange("(c p) n -> p c n", p=P)

                @stepped(sp, DEC_BATCH)
                def _(n):
                    if not isinstance(n, int):
                        wait_apart(sp, t, scored, n)
                    one = bass.ds(n, 1)
                    sp.dma_start(k_t[:, :, 0:WIN_KEYS], t["window_k_t"][one, :, :, :].rearrange("b p c n -> p (b c) n")).then_inc(keys_in, 16)
                    sp.dma_start(k_t[:, :, WIN_KEYS:WIN_ALL], new_k[:, :, bass.ds(n * DEC_SEQ + SEQ, DEC_SEQ)]).then_inc(keys_in, 16)
                    if not isinstance(n, int):
                        wait_apart(sp, t, summed, n)
                    sp.dma_start(v_old[:, :, :], old_rows[one, 0:OLD_J, 0:DEC_SEQ, :].rearrange("b j r f -> (b j) r f")).then_inc(values_in, 16)
                    sp.dma_start(v_near[:, :, :], near_rows[one, :, WINDOW // P - NEAR_TILES:WINDOW // P, :].rearrange("b p a f -> (b p) a f")).then_inc(values_in, 16)
                    sp.dma_start(v_new[:, :], t["swv_all"][bass.ds(n * DEC_SEQ + SEQ, DEC_SEQ), :]).then_inc(values_in, 16)

            @block.tensor
            def _(pe):
                mm, transpose = nc.tensor.matmul, nc.tensor.transpose

                @stepped(pe, DEC_BATCH)
                def _(n):
                    pe.wait_ge(keys_in, 16 * K_IN * n + 16 * K_IN)
                    pe.wait_ge(q_copied, n + 1)
                    after(pe, maxed, n)
                    for c0, width in PIECES:
                        for c in range(4):
                            last = mm(score_bank[0:HT, c0:c0 + width], q_now[:, c, :], k_t[:, c, c0:c0 + width], start=(c == 0), stop=(c == 3))
                    last.then_inc(scored, 1)
                    pe.wait_ge(exped, n + 1)
                    after(pe, copied_near, n)
                    after(pe, copied_old, n)
                    transpose(turn_near[:, 0:P], scores[:, OLD_END:OLD_END + P], ident[:, :])
                    for r in range(1, NEAR):
                        at = OLD_END + r * P
                        transpose(turn_near[:, r * HT:(r + 1) * HT], scores[0:HT, at:at + P], ident[0:HT, 0:HT])
                    transpose(turn_near[0:DEC_SEQ, NEAR * HT:(NEAR + 1) * HT], scores[0:HT, WIN_KEYS:WIN_ALL], ident[0:HT, 0:HT]).then_inc(turned_near, 1)
                    for r in range(OLD):
                        last = transpose(turn_old[0:OLD_J, r * HT:(r + 1) * HT], scores[0:HT, r * OLD_J:(r + 1) * OLD_J], ident[0:HT, 0:HT])
                    last.then_inc(turned_old, 1)
                    pe.wait_ge(copied_old, n + 1)
                    pe.wait_ge(values_in, 16 * V_IN * n + 16 * V_IN)
                    after(pe, masked, n)
                    for r in range(OLD):
                        mm(sum_bank[0:HT, :], probs_t[0:OLD_J, r, :], v_old[:, r, :], start=(r == 0), stop=False)
                    pe.wait_ge(copied_near, n + 1)
                    for r in range(NEAR):
                        mm(sum_bank[0:HT, :], probs_t[:, OLD + r, :], v_near[:, r, :], start=False, stop=False)
                    mm(sum_bank[0:HT, :], probs_t[0:DEC_SEQ, OLD + NEAR, :], v_new[:, :], start=False, stop=True).then_inc(summed, 1)

            @block.scalar
            def _(act):
                @stepped(act, DEC_BATCH)
                def _(n):
                    act.wait_ge(lowered, n + 1)
                    nc.scalar.activation(scores[0:HT, :], scores[0:HT, :], ACT.Exp, bias=low[:, 0:1], accum_out=total[:, 0:1]).then_inc(exped, 1)
                    act.wait_ge(turned_near, n + 1)
                    after(act, summed, n)
                    nc.scalar.activation(probs_t[:, OLD:OLD + NEAR, :], turn_near[:, 0:NEAR * HT].rearrange("p (r q) -> p r q", r=NEAR), ACT.Copy)
                    nc.scalar.activation(probs_t[0:DEC_SEQ, OLD + NEAR, :], turn_near[0:DEC_SEQ, NEAR * HT:(NEAR + 1) * HT], ACT.Copy).then_inc(copied_near, 1)
                    act.wait_ge(normed, n + 1)
                    act.dma_start(t["o_window"][bass.ds(n, 1), :, :].rearrange("b q d -> (b q) d"), out[:, :]).then_inc(stored, 16)

                act.wait_ge(stored, 16 * DEC_BATCH)

            @block.vector
            def _(dve):
                v_ = nc.vector
                dve.wait_ge(inputs_in, 16 * N_IN)
                setup = Chain(dve, sem("setup_link"))
                v_.memset(scores[:, :], 0.0)
                setup.link(v_.memset(q_all[:, :, :, :], 0.0))
                for h in range(HEADS):
                    rows = slice((h % 2) * 64, (h % 2) * 64 + 64)
                    last = v_.tensor_copy(q_all[rows, :, h // 2, h * DEC_SEQ:(h + 1) * DEC_SEQ],
                                          q_heads[rows, h // 2, :].rearrange("p (b t) -> p b t", b=DEC_BATCH))
                last.then_inc(q_placed, 1)
                dve.wait_ge(q_placed, 1)

                @stepped(dve, DEC_BATCH)
                def _(n):
                    link = Chain(dve, dve_link, LINKS * n).link
                    after(dve, scored, n)
                    v_.tensor_copy(q_now[:, :, :], q_all[:, bass.ds(n, 1), :, :].rearrange("p b c q -> p (b c) q")).then_inc(q_copied, 1)
                    after(dve, turned_near, n)
                    dve.wait_ge(scored, n + 1)
                    v_.memset(carrier[:, :], 0.0)
                    v_.tensor_tensor_reduce(scores[0:HT, :], score_bank[0:HT, 0:WIN_ALL], bias[:, :], 1.0, -3e38, ALU.add, ALU.max,
                                            top[:, :]).then_inc(maxed, 1)
                    dve.wait_ge(maxed, n + 1)
                    v_.tensor_scalar(low[:, :], top[:, :], -1.0, None, ALU.mult).then_inc(lowered, 1)
                    dve.wait_ge(turned_old, n + 1)
                    after(dve, summed, n)
                    v_.tensor_copy(probs_t[0:OLD_J, 0:OLD, :], turn_old[0:OLD_J, :].rearrange("p (r q) -> p r q", r=OLD)).then_inc(copied_old, 1)
                    link(v_.reciprocal(inverse[:, :], total[:, :]))
                    dve.wait_ge(summed, n + 1)
                    v_.tensor_tensor(own[:, :, :], sum_bank[0:HT, :].rearrange("p (h d) -> p h d", h=HEADS),
                                     own_head[:, :].rearrange("p (h d) -> p h d", h=HEADS), ALU.mult).then_inc(masked, 1)
                    dve.wait_ge(masked, n + 1)
                    after(dve, stored, 16 * n)
                    link(v_.tensor_reduce(out[:, :], own[:, :, :].rearrange("p h d -> p d h"), AX.X, ALU.add))
                    v_.tensor_scalar(out[:, :], out[:, :], inverse[:, 0:1], None, ALU.mult).then_inc(normed, 1)


def mix_and_route(nc, t, ident):
    with ExitStack() as ctx:
        def sb(name, shape, dt=F32):
            return ctx.enter_context(nc.sbuf_tensor(f"mix_{name}", shape, dt))

        def sem(name):
            return phase_semaphore(nc, t["phase_sems"], f"mix_{name}")

        w_out, w_router = sb("w_out", [P, KC, D_MODEL]), sb("w_router", [P, KC, GROUPS + EXPERTS])
        g_out, g_ffn, b_router = sb("g_out", [P, D_MODEL]), sb("g_ffn", [P, D_MODEL]), sb("b_router", [P, GROUPS + EXPERTS])
        before, ones, iota = sb("before", [P, P]), sb("ones", [P, P]), sb("iota", [P, 64])
        ticket = sb("ticket", [P, TILES * TOP_K, 2], I32)
        real = sb("real", [P, TILES])
        o, o_n, o_t = sb("o", [P, D_MODEL]), sb("o_n", [P, D_MODEL]), sb("o_t", [P, KC, P])
        x, x_mid = sb("x", [P, D_MODEL]), sb("x_mid", [P, D_MODEL])
        h, h_t = sb("h", [P, D_MODEL]), sb("h_t", [P, KC, P])
        squares, o_stat, h_stat = sb("squares", [P, D_MODEL]), sb("o_stat", [P, 6]), sb("h_stat", [P, 3])
        logits = sb("logits", [P, 8 + EXPERTS])
        group_top, group_at = sb("group_top", [P, 8]), sb("group_at", [P, 8], U32)
        group, neg_top, group_hot = sb("group", [P, 2]), sb("neg_top", [P, 2]), sb("group_hot", [P, GROUPS])
        of_group, chosen = sb("of_group", [P, GROUPS, PER_GROUP]), sb("chosen", [P, PER_GROUP])
        best, best_at, best_f = sb("best", [P, 8]), sb("best_at", [P, 8], U32), sb("best_f", [P, 2])
        group_exp, pair_exp, sums, scale = sb("group_exp", [P, GROUPS]), sb("pair_exp", [P, 2]), sb("sums", [P, 2]), sb("scale", [P, 2])
        pair, hot, hot_sum, hot_total = sb("pair", [P, 2]), sb("hot", [P, 2, EXPERTS]), sb("hot_sum", [P, EXPERTS]), sb("hot_total", [P, EXPERTS])
        ranked, real_now = sb("ranked", [P, 2, EXPERTS]), sb("real_now", [P, 1])
        start_128, per_tile, blocks_of, block_end = sb("start_128", [P, EXPERTS]), sb("per_tile", [P, TILES]), sb("blocks_of", [P, EXPERTS]), sb("block_end", [P, EXPERTS])
        fills, upto = sb("fills", [P, EXPERTS, TILES]), sb("upto", [P, EXPERTS, EXPERTS])
        starts, slot = sb("starts", [P, TILES * 2, EXPERTS]), sb("slot", [P, TILES * 2])
        spill, scatter = sb("spill", [P, TILES * 2]), sb("scatter", [P, TILES * 2], I32)
        passed, block_f = sb("passed", [1, MAX_BLOCKS, EXPERTS]), sb("block_f", [1, MAX_BLOCKS])
        carrier = sb("carrier", [1, 1])
        all_hot, all_rank = sb("all_hot", [P, TILES * 2, EXPERTS]), sb("all_rank", [P, TILES * 2])
        turn = ctx.enter_context(nc.psum_tensor("mix_turn", [P, D_MODEL], F32))
        turn_h = ctx.enter_context(nc.psum_tensor("mix_turn_h", [P, D_MODEL], F32))
        mixed_bank = ctx.enter_context(nc.psum_tensor("mix_bank", [P, D_MODEL], F32))
        router_bank = ctx.enter_context(nc.psum_tensor("mix_router_bank", [P, 512], F32))
        rank_bank = ctx.enter_context(nc.psum_tensor("mix_rank_bank", [P, 512], F32))

        weights_in, o_in, x_in = sem("weights_in"), sem("o_in"), sem("x_in")
        o_squared, o_root, o_normed, o_cleared = sem("o_squared"), sem("o_root"), sem("o_normed"), sem("o_cleared")
        o_turned, o_t_lo, o_t_hi, mixed = sem("o_turned"), sem("o_t_lo"), sem("o_t_hi"), sem("mixed")
        x_added, x_squared, x_root, h_normed = sem("x_added"), sem("x_squared"), sem("x_root"), sem("h_normed")
        h_turned, h_t_lo, h_t_hi, routed = sem("h_turned"), sem("h_t_lo"), sem("h_t_hi"), sem("routed")
        logits_done, group_topped, group_exped = sem("logits_done"), sem("group_topped"), sem("group_exped")
        pair_topped, pair_exped = sem("pair_topped"), sem("pair_exped")
        hot_done, rank_done, total_added = sem("hot_done"), sem("rank_done"), sem("total_added")
        gates_scaled, rank_picked = sem("gates_scaled"), sem("rank_picked")
        x_stored, h_stored = sem("x_stored"), sem("h_stored")
        counted, planned, cleared, scattered = sem("counted"), sem("planned"), sem("cleared"), sem("scattered")
        head_link, body_link, tail_link = sem("head_link"), sem("body_link"), sem("tail_link")
        HEAD_LINKS, BODY_LINKS, TAIL_LINKS = 2, 2, 13
        N_W = 10
        LAST = TILES - 1
        HALF_D = D_MODEL // 2

        def tiled(eng, step):
            step(0)
            with eng.Fori(1, LAST - 1) as i:
                step(i)
            step(LAST - 1)
            step(LAST)

        def is_step(i, n):
            return isinstance(i, int) and i == n

        def quarters(ap):
            return ap.rearrange("p (a c) -> p a c", a=4)

        with nc.Block() as block:
            @block.sync
            def _(sp):
                def wait(sem, value):
                    wait_apart(sp, t, sem, value)

                def load(dst, src):
                    sp.dma_start(dst, src).then_inc(weights_in, 16)

                sp.dma_start(o[:, :], t["o_cat"][0:P, :]).then_inc(o_in, 16)
                sp.dma_start(x[:, :], t["x_all"][0:P, :]).then_inc(x_in, 16)
                load(g_out[:, :], row_broadcast(t["norm_out"]))
                load(w_out[:, :, :], t["w_out"].rearrange("(k p) n -> p k n", p=P))
                load(g_ffn[:, :], row_broadcast(t["norm_ffn"]))
                load(w_router[:, :, :], t["w_router"].rearrange("(k p) n -> p k n", p=P))
                load(b_router[:, :], row_broadcast(t["b_router"]))
                load(before[:, :], t["c_before"])
                load(iota[:, :], t["c_iota"])
                load(ticket[:, :, :], t["c_ticket"])
                load(real[:, :], t["c_real"])
                load(spill[:, :], t["c_spill"])

                def finish(i):
                    at = bass.ds(i * P, P)
                    wait(x_added, i + 1)
                    sp.dma_start(t["x_mid"][at, :], x_mid[:, :]).then_inc(x_stored, 16)
                    if not is_step(i, LAST):
                        sp.dma_start(x[:, :], t["x_all"][bass.ds(i * P + P, P), :]).then_inc(x_in, 16)
                    wait(h_normed, i + 1)
                    sp.dma_start(t["h_ffn"][at, :], h[:, :]).then_inc(h_stored, 16)

                @stepped(sp, LAST - 1)
                def _(i):
                    wait(o_normed, i + 1)
                    sp.dma_start(o[:, :], t["o_cat"][bass.ds(i * P + P, P), :]).then_inc(o_in, 16)
                    finish(i)

                sp.wait_ge(o_normed, LAST)
                sp.dma_start(o[0:N_SAMPLE, 0:HALF_D], t["o_cat"][SEQ:SEQ + N_SAMPLE, 0:HALF_D]).then_inc(o_in, 16)
                for b in range(DEC_BATCH):
                    sp.dma_start(o[b * DEC_SEQ:(b + 1) * DEC_SEQ, HALF_D:D_MODEL].rearrange("t (h d) -> t h d", h=HEADS),
                                 t["o_window"][b].rearrange("(h t) d -> t h d", h=HEADS)).then_inc(o_in, 16)
                finish(LAST - 1)
                finish(LAST)
                sp.wait_ge(x_stored, 16 * TILES)
                sp.wait_ge(h_stored, 16 * TILES)

            @block.tensor
            def _(pe):
                mm, transpose = nc.tensor.matmul, nc.tensor.transpose

                def turn_tile(to, of, done):
                    for k in range(KC):
                        last = transpose(to[:, k * P:(k + 1) * P], of[:, k * P:(k + 1) * P], ident[:, :])
                        if k % 4 == 3:
                            last.then_inc(done, 1)

                def turn_and_route(j):
                    pe.wait_ge(h_normed, j + 1)
                    after(pe, h_t_lo, j)
                    after(pe, h_t_hi, j)
                    turn_tile(turn_h, h, h_turned)
                    pe.wait_ge(h_t_lo, j + 1)
                    pe.wait_ge(h_t_hi, j + 1)
                    for k in range(KC):
                        last = mm(router_bank[:, 0:GROUPS + EXPERTS], h_t[:, k, :], w_router[:, k, :], start=(k == 0), stop=(k == KC - 1))
                    last.then_inc(routed, 1)

                def rank(j):
                    pe.wait_ge(hot_done, j + 1)
                    mm(rank_bank[:, 0:EXPERTS], before[:, :], hot_sum[:, :], start=True, stop=False)
                    mm(rank_bank[:, 0:EXPERTS], ones[:, :], hot_total[:, :], start=False, stop=True).then_inc(rank_done, 1)

                def step(i):
                    pe.wait_ge(o_normed, i + 1)
                    turn_tile(turn, o_n, o_turned)
                    if not is_step(i, 0):
                        turn_and_route(i - 1)
                    pe.wait_ge(o_t_lo, i + 1)
                    pe.wait_ge(o_t_hi, i + 1)
                    after(pe, x_added, i)
                    for k in range(KC):
                        for half in range(2):
                            cols = slice(half * HALF_D, (half + 1) * HALF_D)
                            last = mm(mixed_bank[:, cols], o_t[:, k, :], w_out[:, k, cols], start=(k == 0), stop=(k == KC - 1))
                    last.then_inc(mixed, 1)
                    if not is_step(i, 0):
                        rank(i - 1)

                pe.wait_ge(weights_in, 16 * N_W)
                tiled(pe, step)
                turn_and_route(LAST)
                rank(LAST)
                pe.wait_ge(total_added, TILES)
                pe.wait_ge(rank_picked, TILES)
                mm(rank_bank[:, 0:EXPERTS], ones[:, :], hot_total[:, :], start=True, stop=True).then_inc(counted, 1)

            @block.scalar
            def _(act):
                def norm_o(i):
                    if is_step(i, LAST):
                        act.wait_ge(o_cleared, 1)
                        act.wait_ge(o_in, 16 * LAST + 16 * (1 + DEC_BATCH))
                    else:
                        act.wait_ge(o_in, 16 * i + 16)
                    for half in range(2):
                        cols = slice(half * HALF_D, (half + 1) * HALF_D)
                        nc.scalar.activation(squares[:, cols], o[:, cols], ACT.Square, accum_out=o_stat[:, half:half + 1]).then_inc(o_squared, 1)
                    act.wait_ge(head_link, HEAD_LINKS * i + 1)
                    nc.scalar.activation(o_stat[:, 4:6], o_stat[:, 2:4], ACT.Sqrt).then_inc(o_root, 1)

                def route(j):
                    act.wait_ge(h_turned, 2 * j + 2)
                    after(act, routed, j)
                    nc.scalar.activation(h_t[:, 4:8, :], quarters(turn_h[:, HALF_D:D_MODEL]), ACT.Copy).then_inc(h_t_hi, 1)
                    act.wait_ge(group_topped, j + 1)
                    nc.scalar.activation(group_exp[:, :], logits[:, 0:GROUPS], ACT.Exp, bias=neg_top[:, 0:1], accum_out=sums[:, 0:1]).then_inc(group_exped, 1)
                    act.wait_ge(pair_topped, j + 1)
                    nc.scalar.activation(pair_exp[:, :], best[:, 0:2], ACT.Exp, bias=neg_top[:, 1:2], accum_out=sums[:, 1:2]).then_inc(pair_exped, 1)

                def step(i):
                    act.wait_ge(o_turned, 2 * i + 2)
                    after(act, mixed, i)
                    nc.scalar.activation(o_t[:, 4:8, :], quarters(turn[:, HALF_D:D_MODEL]), ACT.Copy).then_inc(o_t_hi, 1)
                    if not is_step(i, 0):
                        route(i - 1)
                    if not is_step(i, LAST):
                        norm_o(i + 1)
                    act.wait_ge(x_added, i + 1)
                    nc.scalar.activation(squares[:, :], x_mid[:, :], ACT.Square, accum_out=h_stat[:, 0:1]).then_inc(x_squared, 1)
                    act.wait_ge(body_link, BODY_LINKS * i + 1)
                    nc.scalar.activation(h_stat[:, 2:3], h_stat[:, 1:2], ACT.Sqrt).then_inc(x_root, 1)

                norm_o(0)
                tiled(act, step)
                route(LAST)

            @block.vector
            def _(dve):
                v_ = nc.vector

                def norm_o(i):
                    if is_step(i, LAST):
                        dve.wait_ge(o_normed, LAST)
                        v_.memset(o[N_SAMPLE:P, :], 0.0).then_inc(o_cleared, 1)
                    link = Chain(dve, head_link, HEAD_LINKS * i).link
                    dve.wait_ge(o_squared, 2 * i + 2)
                    link(v_.tensor_scalar(o_stat[:, 2:4], o_stat[:, 0:2], 1.0 / HALF_D, EPS, ALU.mult, ALU.add))
                    dve.wait_ge(o_root, i + 1)
                    link(v_.reciprocal(o_stat[:, 0:2], o_stat[:, 4:6]))
                    after(dve, o_turned, 2 * i)
                    for half in range(2):
                        cols = slice(half * HALF_D, (half + 1) * HALF_D)
                        last = v_.scalar_tensor_tensor(o_n[:, cols], o[:, cols], o_stat[:, half:half + 1], g_out[:, cols], ALU.mult, ALU.mult)
                    last.then_inc(o_normed, 1)

                def route(j):
                    chain = Chain(dve, tail_link, TAIL_LINKS * j)
                    link = chain.link
                    dve.wait_ge(h_turned, 2 * j + 1)
                    after(dve, routed, j)
                    v_.tensor_copy(h_t[:, 0:4, :], quarters(turn_h[:, 0:HALF_D])).then_inc(h_t_lo, 1)
                    dve.wait_ge(routed, j + 1)
                    v_.tensor_copy(real_now[:, :], real[:, bass.ds(j, 1)])
                    v_.tensor_tensor(logits[:, 0:GROUPS], router_bank[:, 0:GROUPS], b_router[:, 0:GROUPS], ALU.add)
                    link(v_.tensor_tensor(logits[:, 8:8 + EXPERTS], router_bank[:, GROUPS:GROUPS + EXPERTS], b_router[:, GROUPS:GROUPS + EXPERTS], ALU.add))
                    v_.memset(carrier[:, :], 0.0)
                    link(v_.max(group_top[:, :], logits[:, 0:8]))
                    v_.tensor_scalar(neg_top[:, 0:1], group_top[:, 0:1], -1.0, None, ALU.mult).then_inc(group_topped, 1)
                    v_.memset(carrier[:, :], 0.0)
                    link(v_.max_index(group_at[:, :], group_top[:, :], logits[:, 0:8]))
                    link(v_.tensor_copy(group[:, 0:1], group_at[:, 0:1]))
                    v_.tensor_scalar(group[:, 1:2], group[:, 0:1], float(PER_GROUP), None, ALU.mult)
                    link(v_.tensor_scalar(group_hot[:, :], iota[:, 0:GROUPS], group[:, 0:1], None, ALU.is_equal))
                    link(v_.tensor_tensor(of_group[:, :, :], logits[:, 8:8 + EXPERTS].rearrange("p (g j) -> p g j", g=GROUPS),
                                          group_hot[:, :].unsqueeze(2).broadcast_to([P, GROUPS, PER_GROUP]), ALU.mult))
                    link(v_.tensor_reduce(chosen[:, :], of_group[:, :, :].rearrange("p g j -> p j g"), AX.X, ALU.add))
                    v_.memset(carrier[:, :], 0.0)
                    link(v_.max(best[:, :], chosen[:, :]))
                    v_.tensor_scalar(neg_top[:, 1:2], best[:, 0:1], -1.0, None, ALU.mult).then_inc(pair_topped, 1)
                    v_.memset(carrier[:, :], 0.0)
                    link(v_.max_index(best_at[:, :], best[:, :], chosen[:, :]))
                    link(v_.tensor_copy(best_f[:, :], best_at[:, 0:2]))
                    link(v_.tensor_scalar(pair[:, :], best_f[:, :], group[:, 1:2], None, ALU.add))
                    link(v_.tensor_tensor(ranked[:, :, :], iota[:, 0:EXPERTS].unsqueeze(1).broadcast_to([P, 2, EXPERTS]),
                                          pair[:, :].unsqueeze(2).broadcast_to([P, 2, EXPERTS]), ALU.is_equal))
                    rows = bass.ds(2 * j, 2)
                    v_.tensor_scalar(hot[:, :, :], ranked[:, :, :], real_now[:, 0:1], None, ALU.mult)
                    link(v_.tensor_copy(all_hot[:, rows, :], ranked[:, :, :]))
                    v_.tensor_tensor(hot_sum[:, :], hot[:, 0, :], hot[:, 1, :], ALU.add).then_inc(hot_done, 1)
                    dve.wait_ge(group_exped, j + 1)
                    dve.wait_ge(pair_exped, j + 1)
                    v_.tensor_tensor(scale[:, 0:1], sums[:, 0:1], sums[:, 1:2], ALU.mult).then_inc(gates_scaled, 1)
                    dve.wait_ge(gates_scaled, 2 * j + 1)
                    v_.reciprocal(scale[:, 1:2], scale[:, 0:1]).then_inc(gates_scaled, 1)
                    dve.wait_ge(gates_scaled, 2 * j + 2)
                    v_.tensor_scalar(t["gates"][:, rows], pair_exp[:, :], scale[:, 1:2], None, ALU.mult)

                def keep_rank(j):
                    rows = bass.ds(2 * j, 2)
                    dve.wait_ge(rank_done, j + 1)
                    v_.tensor_tensor(hot_total[:, :], hot_total[:, :], hot_sum[:, :], ALU.add).then_inc(total_added, 1)
                    v_.tensor_tensor(ranked[:, :, :], hot[:, :, :], rank_bank[:, 0:EXPERTS].unsqueeze(1).broadcast_to([P, 2, EXPERTS]), ALU.mult).then_inc(rank_picked, 1)
                    dve.wait_ge(rank_picked, j + 1)
                    v_.tensor_reduce(all_rank[:, rows], ranked[:, :, :], AX.X, ALU.add)

                def step(i):
                    dve.wait_ge(o_turned, 2 * i + 1)
                    after(dve, mixed, i)
                    v_.tensor_copy(o_t[:, 0:4, :], quarters(turn[:, 0:HALF_D])).then_inc(o_t_lo, 1)
                    if not is_step(i, 0):
                        route(i - 1)
                    if not is_step(i, LAST):
                        norm_o(i + 1)
                    link = Chain(dve, body_link, BODY_LINKS * i).link
                    dve.wait_ge(mixed, i + 1)
                    dve.wait_ge(x_in, 16 * i + 16)
                    after(dve, x_stored, 16 * i)
                    v_.tensor_tensor(x_mid[:, :], mixed_bank[:, :], x[:, :], ALU.add).then_inc(x_added, 1)
                    dve.wait_ge(x_squared, i + 1)
                    link(v_.tensor_scalar(h_stat[:, 1:2], h_stat[:, 0:1], 1.0 / D_MODEL, EPS, ALU.mult, ALU.add))
                    dve.wait_ge(x_root, i + 1)
                    link(v_.reciprocal(h_stat[:, 0:1], h_stat[:, 2:3]))
                    after(dve, h_turned, 2 * i)
                    after(dve, h_stored, 16 * i)
                    v_.scalar_tensor_tensor(h[:, :], x_mid[:, :], h_stat[:, 0:1], g_ffn[:, :], ALU.mult, ALU.mult).then_inc(h_normed, 1)
                    if not is_step(i, 0):
                        keep_rank(i - 1)


                dve.wait_ge(weights_in, 16 * N_W)
                setup = Chain(dve, sem("setup_link"))
                v_.memset(logits[:, :], -3e38)
                setup.link(v_.memset(hot_total[:, :], 0.0))
                setup.link(v_.memset(ones[:, :], 1.0))
                norm_o(0)
                tiled(dve, step)
                route(LAST)
                keep_rank(LAST)

                dve.wait_ge(counted, 1)
                plan = Chain(dve, sem("plan_link")).link
                plan(v_.tensor_scalar(per_tile[:, :], iota[:, 0:TILES], float(P), None, ALU.mult))
                plan(v_.tensor_tensor(fills[:, :, :], rank_bank[:, 0:EXPERTS].unsqueeze(2).broadcast_to([P, EXPERTS, TILES]),
                                      per_tile[:, :].unsqueeze(1).broadcast_to([P, EXPERTS, TILES]), ALU.is_gt))
                plan(v_.tensor_reduce(blocks_of[:, :], fills[:, :, :], AX.X, ALU.add))
                plan(v_.tensor_tensor(upto[:, :, :], iota[:, 0:EXPERTS].unsqueeze(1).broadcast_to([P, EXPERTS, EXPERTS]),
                                      iota[:, 0:EXPERTS].unsqueeze(2).broadcast_to([P, EXPERTS, EXPERTS]), ALU.is_le))
                plan(v_.tensor_tensor(upto[:, :, :], upto[:, :, :], blocks_of[:, :].unsqueeze(1).broadcast_to([P, EXPERTS, EXPERTS]), ALU.mult))
                plan(v_.tensor_reduce(block_end[:, :], upto[:, :, :], AX.X, ALU.add))
                plan(v_.tensor_tensor(start_128[:, :], block_end[:, :], blocks_of[:, :], ALU.subtract))
                plan(v_.tensor_scalar(start_128[:, :], start_128[:, :], float(P), None, ALU.mult))
                plan(v_.tensor_tensor(starts[:, :, :], all_hot[:, :, :], start_128[:, :].unsqueeze(1).broadcast_to([P, TILES * 2, EXPERTS]), ALU.mult))
                plan(v_.tensor_reduce(slot[:, :], starts[:, :, :], AX.X, ALU.add))
                plan(v_.tensor_tensor(slot[:, :], slot[:, :], all_rank[:, :], ALU.add))
                plan(v_.tensor_tensor(slot[:, :].rearrange("p (i c) -> p i c", c=2), slot[:, :].rearrange("p (i c) -> p i c", c=2),
                                      real[:, :].unsqueeze(2).broadcast_to([P, TILES, 2]), ALU.mult))
                v_.tensor_tensor(scatter[:, :], slot[:, :], spill[:, :], ALU.add).then_inc(planned, 1)
                plan(v_.tensor_tensor(passed[:, :, :], block_end[0:1, :].unsqueeze(1).broadcast_to([1, MAX_BLOCKS, EXPERTS]),
                                      iota[0:1, 0:MAX_BLOCKS].unsqueeze(2).broadcast_to([1, MAX_BLOCKS, EXPERTS]), ALU.is_le))
                plan(v_.tensor_reduce(block_f[:, :], passed[:, :, :], AX.X, ALU.add))
                v_.tensor_scalar(t["block_expert"][:, 0:MAX_BLOCKS], block_f[:, :], float(EXPERTS - 1), None, ALU.min)
                plan(v_.tensor_copy(t["block_expert"][:, MAX_BLOCKS:MAX_BLOCKS + 1], block_end[0:1, EXPERTS - 1:EXPERTS]))

            @block.gpsimd
            def _(gp):
                gp.dma_start(t["slot_ticket"], t["c_empty_tickets"]).then_inc(cleared, 16)
                gp.wait_ge(cleared, 16)
                gp.wait_ge(weights_in, 16 * N_W)
                gp.wait_ge(planned, 1)
                for c in range(TILES * TOP_K):
                    gp.indirect_dma_start(out=t["slot_ticket"], out_offset=bass.IndirectOffsetOnAxis(ap=scatter[:, c:c + 1], axis=0),
                                          in_=ticket[:, c, :], in_offset=None).then_inc(scattered, 16)
                gp.wait_ge(scattered, 16 * TILES * TOP_K)


def experts(nc, t, ident):
    with ExitStack() as ctx:
        def sb(name, shape, dt=F32):
            return ctx.enter_context(nc.sbuf_tensor(f"ex_{name}", shape, dt))

        def sem(name):
            return phase_semaphore(nc, t["phase_sems"], f"ex_{name}")

        w_gate, w_up, w_down = sb("w_gate", [P, KC, D_EXPERT]), sb("w_up", [P, KC, D_EXPERT]), sb("w_down", [P, FC, D_MODEL])
        tickets = sb("tickets", [P, MAX_BLOCKS + 2, 2], I32)
        token, goal = sb("token", [P, 1], I32), sb("goal", [P, 1], I32)
        x, x_t = sb("x", [P, D_MODEL]), sb("x_t", [P, KC, P])
        gated, hidden, hidden_t = sb("gated", [P, D_EXPERT]), sb("hidden", [P, D_EXPERT]), sb("hidden_t", [P, FC, P])
        y = sb("y", [P, D_MODEL])
        carrier = [sb(f"carrier{n}", [P, 1]) for n in range(4)]
        turn_x = ctx.enter_context(nc.psum_tensor("ex_turn_x", [P, D_MODEL], F32))
        gate_bank = ctx.enter_context(nc.psum_tensor("ex_gate_bank", [P, 512], F32))
        up_bank = ctx.enter_context(nc.psum_tensor("ex_up_bank", [P, 512], F32))
        turn_h = ctx.enter_context(nc.psum_tensor("ex_turn_h", [P, 512], F32))
        down_bank = ctx.enter_context(nc.psum_tensor("ex_down_bank", [P, D_MODEL], F32))

        gate_in, up_in, down_in, tickets_in, gathered = sem("gate_in"), sem("up_in"), sem("down_in"), sem("tickets_in"), sem("gathered")
        x_turned, x_t_lo, x_t_hi = sem("x_turned"), sem("x_t_lo"), sem("x_t_hi")
        gate_done, up_done, gated_done, hidden_done = sem("gate_done"), sem("up_done"), sem("gated_done"), sem("hidden_done")
        h_turned, h_t_copied, down_done = sem("h_turned"), sem("h_t_copied"), sem("down_done")
        y_lo, y_hi, stored = sem("y_lo"), sem("y_hi"), sem("stored")
        token_copied, goal_copied = sem("token_copied"), sem("goal_copied")
        HALF_D = D_MODEL // 2

        def block_count(eng):
            return eng.value_load(t["block_expert"][0:1, MAX_BLOCKS:MAX_BLOCKS + 1], min_val=N_TOKENS * TOP_K // P, max_val=MAX_BLOCKS)

        def over_blocks(eng, count, step):
            step(0)
            with eng.Fori(1, count) as b:
                step(b)

        def quarters(ap):
            return ap.rearrange("p (a c) -> p a c", a=4)

        with nc.Block() as block:
            @block.sync
            def _(sp):
                count = block_count(sp)

                def step(b):
                    e = sp.value_load(t["block_expert"][0:1, bass.ds(b, 1)], min_val=0, max_val=EXPERTS - 1)
                    one = bass.ds(e, 1)
                    for w, name, used, ready in ((w_gate, "w_gate", gate_done, gate_in), (w_up, "w_up", up_done, up_in), (w_down, "w_down", down_done, down_in)):
                        k = w.shape[1]
                        if not isinstance(b, int):
                            wait_apart(sp, t, used, b)
                        sp.dma_start(w[:, :, :], t[name][one, :, :].rearrange("e (p k) n -> p (e k) n", k=k)).then_inc(ready, 16)

                over_blocks(sp, count, step)

            @block.gpsimd
            def _(gp):
                count = block_count(gp)

                def carry(n):
                    nc.gpsimd.tensor_tensor(carrier[n][:, 0:1], ident[:, 0:1], ident[:, 0:1], ALU.add)

                def gather(b):
                    if not (isinstance(b, int) and b == 0):
                        gp.wait_ge(x_turned, 2 * b)
                        carry(0)
                    nc.gpsimd.tensor_copy(token[:, :], tickets[:, bass.ds(b, 1), 0:1].rearrange("p a o -> p (a o)")).then_inc(token_copied, 1)
                    gp.wait_ge(token_copied, b + 1)
                    carry(1)
                    gp.indirect_dma_start(out=x[:, :], out_offset=None, in_=t["h_ffn"],
                                          in_offset=bass.IndirectOffsetOnAxis(ap=token[:, 0:1], axis=0)).then_inc(gathered, 16)

                def scatter(b, done):
                    if not (isinstance(done, int) and done == 1):
                        gp.wait_ge(stored, 16 * done - 16)
                        carry(2)
                    nc.gpsimd.tensor_copy(goal[:, :], tickets[:, bass.ds(b, 1), 1:2].rearrange("p a o -> p (a o)")).then_inc(goal_copied, 1)
                    gp.wait_ge(goal_copied, done)
                    gp.wait_ge(y_lo, done)
                    gp.wait_ge(y_hi, done)
                    carry(3)
                    gp.indirect_dma_start(out=t["expert_rows"], out_offset=bass.IndirectOffsetOnAxis(ap=goal[:, 0:1], axis=0),
                                          in_=y[:, :], in_offset=None).then_inc(stored, 16)

                gp.dma_start(tickets[:, :, :], t["slot_ticket"].rearrange("(b p) c -> p b c", p=P)).then_inc(tickets_in, 16)
                gp.wait_ge(tickets_in, 16)
                gather(0)
                gather(1)
                gather(2)
                scatter(0, 1)
                with gp.Fori(2, count + 1) as b:
                    gather(b + 1)
                    scatter(b - 1, b)
                gp.wait_ge(gathered, count * 16 + 32)
                gp.wait_ge(stored, count * 16)

            @block.tensor
            def _(pe):
                mm, transpose = nc.tensor.matmul, nc.tensor.transpose
                count = block_count(pe)

                def turn(half):
                    of = x[:, :].rearrange("p (c k) -> p k c", k=KC)
                    for k in range(4 * half, 4 * half + 4):
                        last = transpose(turn_x[:, k * P:(k + 1) * P], of[:, k, :], ident[:, :])
                    last.then_inc(x_turned, 1)

                def step(b):
                    pe.wait_ge(x_t_lo, b + 1)
                    pe.wait_ge(x_t_hi, b + 1)
                    pe.wait_ge(gate_in, 16 * b + 16)
                    after(pe, gated_done, b)
                    for k in range(KC):
                        last = mm(gate_bank[:, :], x_t[:, k, :], w_gate[:, k, :], start=(k == 0), stop=(k == KC - 1))
                    last.then_inc(gate_done, 1)
                    pe.wait_ge(up_in, 16 * b + 16)
                    after(pe, hidden_done, b)
                    for k in range(KC):
                        last = mm(up_bank[:, :], x_t[:, k, :], w_up[:, k, :], start=(k == 0), stop=(k == KC - 1))
                    last.then_inc(up_done, 1)
                    pe.wait_ge(gathered, 16 * b + 32)
                    turn(0)
                    pe.wait_ge(hidden_done, b + 1)
                    after(pe, h_t_copied, b)
                    of = hidden[:, :].rearrange("p (c k) -> p k c", k=FC)
                    for k in range(FC):
                        last = transpose(turn_h[:, k * P:(k + 1) * P], of[:, k, :], ident[:, :])
                    last.then_inc(h_turned, 1)
                    turn(1)
                    pe.wait_ge(down_in, 16 * b + 16)
                    pe.wait_ge(h_t_copied, b + 1)
                    after(pe, y_lo, b)
                    after(pe, y_hi, b)
                    for k in range(FC):
                        for half in range(2):
                            cols = slice(half * HALF_D, (half + 1) * HALF_D)
                            last = mm(down_bank[:, cols], hidden_t[:, k, :], w_down[:, k, cols], start=(k == 0), stop=(k == FC - 1))
                    last.then_inc(down_done, 1)

                pe.wait_ge(gathered, 16)
                turn(0)
                turn(1)
                over_blocks(pe, count, step)

            @block.scalar
            def _(act):
                count = block_count(act)

                def copy_x(b):
                    act.wait_ge(x_turned, 2 * b + 2)
                    nc.scalar.activation(x_t[:, 4:8, :], quarters(turn_x[:, HALF_D:D_MODEL]), ACT.Copy).then_inc(x_t_hi, 1)

                def step(b):
                    act.wait_ge(gate_done, b + 1)
                    after(act, hidden_done, b)
                    nc.scalar.activation(gated[:, :], gate_bank[:, :], ACT.Silu).then_inc(gated_done, 1)
                    act.wait_ge(up_done, b + 1)
                    copy_x(b + 1)
                    act.wait_ge(down_done, b + 1)
                    after(act, stored, 16 * b)
                    nc.scalar.activation(y[:, HALF_D:D_MODEL], down_bank[:, HALF_D:D_MODEL], ACT.Copy).then_inc(y_hi, 1)

                copy_x(0)
                over_blocks(act, count, step)

            @block.vector
            def _(dve):
                v_ = nc.vector
                count = block_count(dve)

                def copy_x(b):
                    dve.wait_ge(x_turned, 2 * b + 1)
                    v_.tensor_copy(x_t[:, 0:4, :], quarters(turn_x[:, 0:HALF_D])).then_inc(x_t_lo, 1)

                def step(b):
                    dve.wait_ge(up_done, b + 1)
                    dve.wait_ge(gated_done, b + 1)
                    v_.tensor_tensor(hidden[:, :], gated[:, :], up_bank[:, :], ALU.mult).then_inc(hidden_done, 1)
                    copy_x(b + 1)
                    dve.wait_ge(h_turned, b + 1)
                    v_.tensor_copy(hidden_t[:, :, :], quarters(turn_h[:, :])).then_inc(h_t_copied, 1)
                    dve.wait_ge(down_done, b + 1)
                    after(dve, stored, 16 * b)
                    v_.tensor_copy(y[:, 0:HALF_D], down_bank[:, 0:HALF_D]).then_inc(y_lo, 1)

                copy_x(0)
                over_blocks(dve, count, step)


def combine(nc, t, ident):
    with ExitStack() as ctx:
        def sb(name, shape, dt=F32):
            return ctx.enter_context(nc.sbuf_tensor(f"com_{name}", shape, dt))

        def sem(name):
            return phase_semaphore(nc, t["phase_sems"], f"com_{name}")

        g_final = sb("g_final", [P, D_MODEL])
        gates_now = [sb(f"gates_now{u}", [P, 2]) for u in range(2)]
        x, y = [sb(f"x{u}", [P, D_MODEL]) for u in range(2)], [sb(f"y{u}", [P, 2, D_MODEL]) for u in range(2)]
        one, both, out = [[sb(f"{n}{u}", [P, D_MODEL]) for u in range(2)] for n in ("one", "both", "out")]
        stat = [sb(f"stat{u}", [P, 4]) for u in range(2)]
        squares = sb("squares", [P, D_MODEL])

        def pair(name):
            return [sem(f"{name}{u}") for u in range(2)]

        gain_in, x_in, y_in, gates_copied = sem("gain_in"), pair("x_in"), pair("y_in"), sem("gates_copied")
        added, summed, squared, rooted, normed, stored = pair("added"), pair("summed"), pair("squared"), pair("rooted"), pair("normed"), pair("stored")
        tails_in, dve_link = sem("tails_in"), pair("dve_link")
        LINKS = 2
        PAIRS = PROMPT_TILES // 2

        def rows_of(i):
            return N_TOKENS - i * P if isinstance(i, int) and i == TILES - 1 else P

        def by_pairs(eng, step):
            for u in range(2):
                step(u, u, 0)
            with eng.Fori(1, PAIRS) as r:
                for u in range(2):
                    step(2 * r + u, u, r)
            step(TILES - 1, 0, PAIRS)

        with nc.Block() as block:
            @block.sync
            def _(sp):
                sp.dma_start(g_final[:, :], row_broadcast(t["norm_final"])).then_inc(gain_in, 16)
                new = slice(WINDOW - DEC_SEQ, WINDOW)
                for out_name, rows in (("sw_k_new", "swk_all"), ("sw_v_new", "swv_all")):
                    sp.dma_start(t[out_name][:, new, :], t[rows][SEQ:N_TOKENS, :].rearrange("(b t) f -> b t f", t=DEC_SEQ)).then_inc(tails_in, 16)

                def step(i, u, r):
                    if not isinstance(r, int):
                        wait_apart(sp, t, added[u], r)
                    elif r > 0:
                        sp.wait_ge(added[u], r)
                    n = rows_of(i)
                    sp.dma_start(x[u][0:n, :], t["x_mid"][bass.ds(i * P, n), :]).then_inc(x_in[u], 16)
                    if not isinstance(r, int):
                        wait_apart(sp, t, summed[u], r)
                    elif r > 0:
                        sp.wait_ge(summed[u], r)
                    for c in range(TOP_K):
                        sp.dma_start(y[u][0:n, c, :], t["expert_rows"][bass.ds(i * P + c * ROWS, n), :]).then_inc(y_in[u], 16)

                by_pairs(sp, step)
                sp.wait_ge(tails_in, 32)
                sp.wait_ge(t["shifted"], 16 * 2 * DEC_BATCH)

            @block.vector
            def _(dve):
                v_ = nc.vector
                dve.wait_ge(gain_in, 16)

                def step(i, u, r):
                    n = rows_of(i)
                    link = Chain(dve, dve_link[u], LINKS * r).link
                    dve.wait_ge(x_in[u], 16 * r + 16)
                    dve.wait_ge(y_in[u], 32 * r + 32)
                    v_.tensor_copy(gates_now[u][:, :], t["gates"][:, bass.ds(2 * i, 2)]).then_inc(gates_copied, 1)
                    dve.wait_ge(gates_copied, i + 1)
                    v_.scalar_tensor_tensor(one[u][0:n, :], y[u][0:n, 0, :], gates_now[u][0:n, 0:1], x[u][0:n, :], ALU.mult, ALU.add).then_inc(added[u], 1)
                    dve.wait_ge(added[u], r + 1)
                    v_.scalar_tensor_tensor(both[u][0:n, :], y[u][0:n, 1, :], gates_now[u][0:n, 1:2], one[u][0:n, :], ALU.mult, ALU.add).then_inc(summed[u], 1)
                    dve.wait_ge(squared[u], r + 1)
                    link(v_.tensor_scalar(stat[u][0:n, 1:2], stat[u][0:n, 0:1], 1.0 / D_MODEL, EPS, ALU.mult, ALU.add))
                    dve.wait_ge(rooted[u], r + 1)
                    link(v_.reciprocal(stat[u][0:n, 3:4], stat[u][0:n, 2:3]))
                    after(dve, stored[u], 16 * r)
                    v_.scalar_tensor_tensor(out[u][0:n, :], both[u][0:n, :], stat[u][0:n, 3:4], g_final[0:n, :], ALU.mult, ALU.mult).then_inc(normed[u], 1)

                by_pairs(dve, step)

            @block.scalar
            def _(act):
                def step(i, u, r):
                    n = rows_of(i)
                    act.wait_ge(summed[u], r + 1)
                    nc.scalar.activation(squares[0:n, :], both[u][0:n, :], ACT.Square, accum_out=stat[u][0:n, 0:1]).then_inc(squared[u], 1)
                    act.wait_ge(dve_link[u], LINKS * r + 1)
                    nc.scalar.activation(stat[u][0:n, 2:3], stat[u][0:n, 1:2], ACT.Sqrt).then_inc(rooted[u], 1)
                    act.wait_ge(normed[u], r + 1)
                    act.dma_start(t["y_all"][bass.ds(i * P, n), :], out[u][0:n, :]).then_inc(stored[u], 16)

                by_pairs(act, step)
                act.wait_ge(stored[0], 16 * (PAIRS + 1))
                act.wait_ge(stored[1], 16 * PAIRS)


OUTPUTS = {
    "y_all": (N_TOKENS, D_MODEL), "kv_all": (ROWS, KV_LORA), "kr_all": (ROWS, ROPE), "swk_all": (ROWS, SW_WIDTH),
    "swv_all": (ROWS, SW_WIDTH), "sw_k_new": (DEC_BATCH, WINDOW, SW_WIDTH), "sw_v_new": (DEC_BATCH, WINDOW, SW_WIDTH),
}
SCRATCH = {
    "q_t": ((HEADS, QK, ROWS), F32), "kn_t": ((HEADS * NOPE, ROWS), F32), "kr_t": ((ROPE, ROWS), F32),
    "v_mla": ((ROWS, 512), F32), "q_sw_t": ((512, ROWS), F32), "k_sw_t": ((512, ROWS), F32),
    "o_cat": ((ROWS, D_MODEL), F32), "o_window": ((DEC_BATCH, HEADS * DEC_SEQ, 64), F32),
    "x_mid": ((ROWS, D_MODEL), F32), "h_ffn": ((ROWS, D_MODEL), F32),
    "slot_ticket": (((MAX_BLOCKS + 2) * P, 2), I32),
    "expert_rows": ((TOP_K * ROWS + P, D_MODEL), F32),
}
SCRATCH_KIND = {}


def host_tables(np, a):
    f = np.float32
    slope = 2.0 ** (-8.0 * np.arange(1, HEADS + 1) / HEADS)

    def window_bias(dist):
        times = sum(((dist >= 0) & (dist <= w) & (dist % d == 0)).astype(np.int64) for w, d in PATTERNS)
        log_times = np.log(np.maximum(times, 1).astype(np.float64))
        shaped = slope.reshape([HEADS] + [1] * dist.ndim)
        return np.where(times > 0, log_times - shaped * dist, MASK).astype(f)

    dist = (SEQ - P) + np.arange(P)[:, None] - np.arange(SEQ)[None, :]
    a["c_causal"] = np.where(dist >= 0, 0.0, MASK).astype(f)[None].repeat(1, 0)
    a["c_window"] = window_bias(dist)
    row = np.concatenate([(16 * np.arange(OLD_J)[None, :] + np.arange(DEC_SEQ)[:, None]).ravel(),
                          np.arange(WINDOW - 512, WINDOW), WINDOW + np.arange(DEC_SEQ)])
    dist = WINDOW + np.arange(DEC_SEQ)[:, None] - row[None, :]
    a["c_window_sample"] = window_bias(dist).reshape(HEADS * DEC_SEQ, WIN_ALL)
    h = np.arange(HEADS * DEC_SEQ) // DEC_SEQ
    a["c_own_head"] = (h[:, None] == (np.arange(512) // 64)[None, :]).astype(f)
    new = np.where(np.arange(DEC_SEQ)[:, None] <= (np.arange(64) % DEC_SEQ)[None, :], 0.0, MASK).astype(f)
    a["c_new_mask"] = new
    a["c_page_part"] = (np.arange(P) % 8).astype(f)[:, None]
    a["c_before"] = (np.arange(P)[:, None] < np.arange(P)[None, :]).astype(f)
    row = np.arange(TILES)[None, :] * P + np.arange(P)[:, None]
    real = row < N_TOKENS
    choice = np.arange(TOP_K)
    a["c_ticket"] = np.stack(np.broadcast_arrays(row[:, :, None], row[:, :, None] + choice * ROWS), -1).reshape(P, TILES * TOP_K, 2).astype(np.int32)
    slots = np.arange((MAX_BLOCKS + 2) * P)
    a["c_empty_tickets"] = np.stack([0 * slots, TOP_K * ROWS + slots % P], 1).astype(np.int32)
    a["c_real"] = real.astype(f)
    behind = MAX_BLOCKS * P + (np.arange(P)[:, None, None] + np.arange(TOP_K) * N_SAMPLE) % P
    a["c_spill"] = np.where(real[:, :, None], 0, behind).reshape(P, TILES * TOP_K).astype(f)
    a["c_iota"] = np.broadcast_to(np.arange(64, dtype=f)[None, :], (P, 64)).copy()


def host_layout(np, a, x):
    k = x["state_sw_k"][0].reshape(DEC_BATCH, WINDOW, 4, P)
    old = (16 * np.arange(OLD_J)[None, :] + np.arange(DEC_SEQ)[:, None]).ravel()
    order = np.concatenate([old, np.arange(WINDOW - 512, WINDOW)])
    a["window_k_t"] = k[:, order].transpose(0, 3, 2, 1)
    a["w_uk_t"] = x["w_uk"][0].transpose(2, 1, 0)
    a["cache_kv"] = x["cache_kv_latent"][0].reshape(-1, 16 * KV_LORA)
    a["cache_kr"] = x["cache_k_rope"][0].reshape(-1, 16 * ROPE)
    pages = x["page_table"].astype(np.int32).reshape(DEC_BATCH, 4, 16)
    a["page_rows"] = pages.transpose(2, 0, 1).reshape(16, 32).repeat(8, 0)
    a["norm_out"] = np.concatenate([x["norm_out_mla"][0], x["norm_out_sw"][0]])
    a["w_out"], a["norm_ffn"], a["norm_final"] = x["w_out"][0], x["norm_ffn"][0], x["norm_final"]
    a["w_router"] = np.concatenate([x["w_router_group"][0], x["w_router_expert"][0]], 1)
    a["b_router"] = np.concatenate([x["b_router_group"][0], x["b_router_expert"][0]])
    a["w_gate"], a["w_up"], a["w_down"] = x["w_expert_gate"][0], x["w_expert_up"][0], x["w_expert_down"][0]


def program(nc, t, phases):
    t["shifted"] = nc.alloc_semaphore("window_shifted")
    t["ident_in"] = nc.alloc_semaphore("ident_in")
    with (nc.sbuf_tensor("ident", [P, P], F32) as ident,
          nc.sbuf_tensor("gates", [P, TILES * TOP_K], F32) as gates, nc.sbuf_tensor("block_expert", [1, MAX_BLOCKS + 1], I32) as block_expert):
        t.update(gates=gates, block_expert=block_expert)
        with nc.Block() as block:
            @block.sync
            def _(sp):
                sp.dma_start(ident[:, :], t["c_ident"]).then_inc(t["ident_in"], 16)
                sp.wait_ge(t["ident_in"], 16)
        for phase in phases:
            t["phase_sems"] = []
            phase(nc, t, ident)
            nc.clear_and_free_semaphores(t["phase_sems"])
            nc.all_engine_barrier()


PHASES = [project, attend_prompt, attend_latent, attend_window, mix_and_route, experts, combine]


def kernel(**inputs):
    import numpy as np
    import concourse.bacc as bacc
    from concourse.bass_utils import run_bass_kernel_spmd as run

    x = {n: np.asarray(a) for n, a in inputs.items()}
    f = np.float32
    a = {
        "x_all": np.concatenate([x["x_prompt"].reshape(SEQ, D_MODEL), x["x_sample"].reshape(N_SAMPLE, D_MODEL),
                                 np.zeros((ROWS - SEQ - N_SAMPLE, D_MODEL), f)]),
        "w_in": x["w_in"][0], "norm_mix": x["norm_mix"][0], "norm_q_latent": x["norm_q_latent"][0],
        "norm_kv_latent": x["norm_kv_latent"][0], "w_uq": x["w_uq"][0].reshape(Q_LORA, HEADS * QK),
        "w_uk": x["w_uk"][0].reshape(KV_LORA, 512), "w_uv": x["w_uv"][0].reshape(KV_LORA, 512),
        "state_sw_k": x["state_sw_k"][0].reshape(DEC_BATCH, WINDOW, SW_WIDTH),
        "state_sw_v": x["state_sw_v"][0].reshape(DEC_BATCH, WINDOW, SW_WIDTH),
    }
    pos = np.zeros(ROWS, f)
    pos[:SEQ] = np.arange(SEQ)
    pos[SEQ:SEQ + N_SAMPLE] = PAST_LEN + np.tile(np.arange(DEC_SEQ), DEC_BATCH)
    angle = (pos[:, None] * (f(10000.0) ** (-np.arange(HALF, dtype=f) / f(HALF)))[None, :]).astype(np.float64)
    a["c_angles"] = np.concatenate([np.cos(angle), np.sin(angle)], 1).astype(f)
    a["c_ident"] = np.eye(P, dtype=f)
    host_tables(np, a)
    host_layout(np, a, x)

    nc = bacc.Bacc("TRN2", target_bir_lowering=False, num_devices=1)
    t, arrays = {}, {}
    for name, v in a.items():
        v = np.ascontiguousarray(v)
        arrays[name] = v
        t[name] = nc.dram_tensor(name, v.shape, mybir.dt.from_np(v.dtype), kind="ExternalInput").ap()
    for name, shape in OUTPUTS.items():
        t[name] = nc.dram_tensor(name, shape, F32, kind="ExternalOutput").ap()
    for name, (shape, dt) in SCRATCH.items():
        t[name] = nc.dram_tensor(name, shape, dt, **SCRATCH_KIND).ap()
    program(nc, t, PHASES)
    o = run(nc, [arrays], core_ids=[0]).results[0]
    sample = slice(SEQ, SEQ + N_SAMPLE)
    return (o["y_all"][:SEQ].reshape(1, SEQ, D_MODEL), o["y_all"][sample].reshape(DEC_BATCH, DEC_SEQ, D_MODEL),
            o["kv_all"][:SEQ].reshape(1, 1, SEQ, KV_LORA), o["kr_all"][:SEQ].reshape(1, 1, SEQ, ROPE),
            o["swk_all"][:SEQ].reshape(1, 1, SEQ, HEADS, 64), o["swv_all"][:SEQ].reshape(1, 1, SEQ, HEADS, 64),
            o["kv_all"][sample].reshape(1, DEC_BATCH, DEC_SEQ, KV_LORA),
            o["kr_all"][sample].reshape(1, DEC_BATCH, DEC_SEQ, ROPE),
            o["sw_k_new"].reshape(1, DEC_BATCH, WINDOW, HEADS, 64),
            o["sw_v_new"].reshape(1, DEC_BATCH, WINDOW, HEADS, 64))
```

```python
from contextlib import ExitStack
import math

import concourse.bass as bass
from concourse import mybir

F32 = mybir.dt.float32
I32 = mybir.dt.int32
U32 = mybir.dt.uint32
ALU = mybir.AluOpType
ACT = mybir.ActivationFunctionType
AX = mybir.AxisListType

P = 128
D_MODEL = 1024
SEQ = 1024
DEC_BATCH, DEC_SEQ = 8, 8
N_SAMPLE = DEC_BATCH * DEC_SEQ
PROMPT_TILES = SEQ // P
TILES = PROMPT_TILES + 1
ROWS = TILES * P
PAST_LEN = 8192
PAGE = 128
N_PAGES = PAST_LEN // PAGE
HEADS = 8
Q_LORA, KV_LORA, NOPE, ROPE = 192, 128, 64, 32
QK = NOPE + ROPE
V_DIM = 64
HALF = ROPE // 2
MLA_SCALE = QK ** -0.5
SW_SCALE = 64 ** -0.5
SW_WIDTH = 512
LATENTS = Q_LORA + KV_LORA + ROPE
IN_WIDTH = LATENTS + 3 * SW_WIDTH
WINDOW = 2048
PATTERNS = ((128, 1), (512, 4), (2048, 16))
EPS = 1e-6
MASK = -1e30
KC = D_MODEL // P
GROUPS, PER_GROUP, EXPERTS, TOP_K = 4, 8, 32, 2
D_EXPERT = 512
FC = D_EXPERT // P
N_TOKENS = SEQ + N_SAMPLE
MAX_BLOCKS = -(-N_TOKENS * TOP_K // P) + EXPERTS
SLOT_BLOCKS = MAX_BLOCKS + 2
OLD_J = (WINDOW - 512) // 16
OLD_KEYS = OLD_J * DEC_SEQ
WIN_KEYS = OLD_KEYS + 512
WIN_TILES = WIN_KEYS // P
WIN_ALL = WIN_KEYS + DEC_SEQ


class Chain:

    def __init__(self, eng, sem, base=0):
        self.eng, self.sem, self.base, self.n = eng, sem, base, 0

    def link(self, ins):
        self.n += 1
        ins.then_inc(self.sem, 1)
        self.eng.wait_ge(self.sem, self.base + self.n)


def after(eng, sem, value):
    if not isinstance(value, int) or value > 0:
        eng.wait_ge(sem, value)


def wait_apart(eng, t, sem, value):
    if not isinstance(value, int):
        eng.wait_ge(t["ident_in"], 16)
    after(eng, sem, value)


def stepped(eng, n):
    def run(step):
        step(0)
        with eng.Fori(1, n) as i:
            step(i)
    return run


def stepped_to_last(eng, n):
    def run(step):
        step(0, False)
        with eng.Fori(1, n - 1) as i:
            step(i, False)
        step(n - 1, True)
    return run


def phase_semaphore(nc, sems, name):
    s = nc.alloc_semaphore(name)
    sems.append(s)
    return s


SHIFT_PARTS = 4


def shift_window(eng, t, what, b, part=0, parts=1):
    rows = (WINDOW - DEC_SEQ) // parts
    lines = 120 // parts

    def piece(name, first):
        return t[name][bass.ds(b, 1), first:first + rows, :].rearrange("b (a n) f -> (b a) (n f)", a=lines)

    eng.dma_start(piece(f"sw_{what}_new", part * rows), piece(f"state_sw_{what}", part * rows + DEC_SEQ)).then_inc(t["shifted"], 16)


def row_broadcast(vector):
    return vector.partition_broadcast(P)


def project(nc, t, ident):
    with ExitStack() as ctx:
        def sb(name, shape, dt=F32):
            return ctx.enter_context(nc.sbuf_tensor(f"a_{name}", shape, dt))

        def sem(name):
            return phase_semaphore(nc, t["phase_sems"], f"a_{name}")

        w_in = sb("w_in", [P, KC, IN_WIDTH])
        w_uq0, w_uq1 = sb("w_uq0", [P, HEADS * QK]), sb("w_uq1", [Q_LORA - P, HEADS * QK])
        w_uk, w_uv = sb("w_uk", [P, 512]), sb("w_uv", [P, 512])
        g_mix, g_q, g_kv = sb("g_mix", [P, D_MODEL]), sb("g_q", [P, Q_LORA]), sb("g_kv", [P, KV_LORA])
        x, squares, xn = sb("x", [P, D_MODEL]), sb("squares", [P, D_MODEL]), sb("xn", [P, D_MODEL])
        x_t = sb("x_t", [P, KC, P])
        angles = sb("angles", [P, ROPE])
        stat, stat2 = sb("stat", [P, 3]), sb("stat2", [P, 6])
        cq, ckv, kr = sb("cq", [P, Q_LORA]), sb("ckv", [P, KV_LORA]), sb("kr", [P, ROPE])
        rot = sb("rot", [P, 4, HEADS, HALF])
        rot_k = sb("rot_k", [P, 4, HALF])
        cq_t0, cq_t1 = sb("cq_t0", [P, P]), sb("cq_t1", [Q_LORA - P, P])
        ckv_t, kr_t = sb("ckv_t", [P, P]), sb("kr_t", [ROPE, P])
        q = sb("q", [P, HEADS, QK])
        q_t, kn_t, v = sb("q_t", [QK, HEADS, P]), sb("kn_t", [P, 4, P]), sb("v", [P, 512])
        q_sw, k_sw, v_sw = sb("q_sw", [P, 512]), sb("k_sw", [P, 512]), sb("v_sw", [P, 512])
        q_sw_t, k_sw_t = sb("q_sw_t", [P, 4, P]), sb("k_sw_t", [P, 4, P])
        bank = [ctx.enter_context(nc.psum_tensor(f"a_bank{n}", [P, 512], F32)) for n in range(8)]
        proj = bank[0:4]
        turn0, turn1, up0, up1 = bank[4:8]

        def quarters(b, rows=P):
            return b[0:rows, :].rearrange("p (a c) -> p a c", a=4)

        gain_in, weights_in, columns_in = sem("gain_in"), sem("weights_in"), [sem(f"columns_in{n}") for n in range(4)]
        COLUMNS = [(0, LATENTS)] + [(LATENTS + n * 512, 512) for n in range(3)]
        x_in, angles_in = sem("x_in"), sem("angles_in")
        x_squared, x_root, xn_done = sem("x_squared"), sem("x_root"), sem("xn_done")
        dve_link, x_link = sem("dve_link"), sem("x_link")
        x_turned, x_t_lo, x_t_hi = sem("x_turned"), sem("x_t_lo"), sem("x_t_hi")
        projected = sem("projected")
        lat_squared, lat_root, lat_normed, k_rotated = sem("lat_squared"), sem("lat_root"), sem("lat_normed"), sem("k_rotated")
        lat_turned, lat_t = sem("lat_turned"), sem("lat_t")
        q_up, kn_up, v_up = sem("q_up"), sem("kn_up"), sem("v_up")
        q_copied, q_rotated, kn_copied, v_copied = sem("q_copied"), sem("q_rotated"), sem("kn_copied"), sem("v_copied")
        q_sw_copied, k_sw_copied, v_sw_copied = sem("q_sw_copied"), sem("k_sw_copied"), sem("v_sw_copied")
        q_sw_turned, k_sw_turned, q_turned = sem("q_sw_turned"), sem("k_sw_turned"), sem("q_turned")
        q_sw_t_copied, k_sw_t_copied, q_t_lo, q_t_hi = sem("q_sw_t_copied"), sem("k_sw_t_copied"), sem("q_t_lo"), sem("q_t_hi")
        st = {n: sem(f"stored_{n}") for n in ("ckv", "kr", "k_sw", "v_sw", "q_t", "kn_t", "kr_t", "v", "q_sw_t", "k_sw_t")}
        N_W, LINKS = 4, 5
        block = ctx.enter_context(nc.Block())

        @block.sync
        def _(sp):
            def wait(sem, value):
                wait_apart(sp, t, sem, value)

            def load_x(row):
                sp.dma_start(x[:, :], t["x_all"][bass.ds(row, P), :]).then_inc(x_in, 16)

            def load_angles(row):
                sp.dma_start(angles[:, :], t["c_angles"][bass.ds(row, P), :]).then_inc(angles_in, 16)

            def store(done, row):
                at = bass.ds(row, P)
                wait(lat_normed, done)
                sp.dma_start(t["kv_all"][at, :], ckv[:, :]).then_inc(st["ckv"], 16)
                wait(k_rotated, done)
                sp.dma_start(t["kr_all"][at, :], kr[:, :]).then_inc(st["kr"], 16)
                wait(k_sw_copied, done)
                sp.dma_start(t["swk_all"][at, :], k_sw[:, :]).then_inc(st["k_sw"], 16)
                wait(v_sw_copied, done)
                sp.dma_start(t["swv_all"][at, :], v_sw[:, :]).then_inc(st["v_sw"], 16)
                wait(lat_t, done)
                sp.dma_start(t["kr_t"][:, at], kr_t[:, :]).then_inc(st["kr_t"], 16)
                wait(kn_copied, done)
                sp.dma_start(t["kn_t"].rearrange("(c p) n -> p c n", p=P)[:, :, at], kn_t[:, :, :]).then_inc(st["kn_t"], 16)
                wait(v_copied, done)
                sp.dma_start(t["v_mla"][at, :], v[:, :]).then_inc(st["v"], 16)
                wait(q_sw_t_copied, done)
                sp.dma_start(t["q_sw_t"].rearrange("(c p) n -> p c n", p=P)[:, :, at], q_sw_t[:, :, :]).then_inc(st["q_sw_t"], 16)
                wait(k_sw_t_copied, done)
                sp.dma_start(t["k_sw_t"].rearrange("(c p) n -> p c n", p=P)[:, :, at], k_sw_t[:, :, :]).then_inc(st["k_sw_t"], 16)
                wait(q_t_lo, done)
                wait(q_t_hi, done)
                sp.dma_start(t["q_t"].rearrange("h e n -> e h n")[:, :, at], q_t[:, :, :]).then_inc(st["q_t"], 16)

            load_x(0)
            load_angles(0)
            sp.dma_start(g_mix[:, :], row_broadcast(t["norm_mix"])).then_inc(gain_in, 16)
            for n, (c0, width) in enumerate(COLUMNS):
                sp.dma_start(w_in[:, :, c0:c0 + width], t["w_in"].rearrange("(k p) n -> p k n", p=P)[:, :, c0:c0 + width]).then_inc(columns_in[n], 16)
                if n == 0:
                    sp.dma_start(g_q[:, :], row_broadcast(t["norm_q_latent"])).then_inc(gain_in, 16)
                    sp.dma_start(g_kv[:, :], row_broadcast(t["norm_kv_latent"])).then_inc(gain_in, 16)
            sp.dma_start(w_uq0[:, :], t["w_uq"][0:P, :]).then_inc(weights_in, 16)
            sp.dma_start(w_uq1[:, :], t["w_uq"][P:Q_LORA, :]).then_inc(weights_in, 16)
            sp.dma_start(w_uk[:, :], t["w_uk"]).then_inc(weights_in, 16)
            sp.dma_start(w_uv[:, :], t["w_uv"]).then_inc(weights_in, 16)

            @stepped(sp, TILES - 1)
            def _(i):
                wait(xn_done, i + 1)
                load_x(i * P + P)
                store(i + 1, i * P)
                wait(q_rotated, i + 1)
                load_angles(i * P + P)
            store(TILES, (TILES - 1) * P)
            for s in st.values():
                sp.wait_ge(s, 16 * TILES)

        @block.scalar
        def _(act):
            def norm_x(i):
                act.wait_ge(x_in, 16 * i + 16)
                nc.scalar.activation(squares[:, :], x[:, :], ACT.Square, accum_out=stat[:, 0:1]).then_inc(x_squared, 1)
                act.wait_ge(x_link, 2 * i + 1)
                nc.scalar.activation(stat[:, 2:3], stat[:, 1:2], ACT.Sqrt).then_inc(x_root, 1)

            norm_x(0)

            @stepped_to_last(act, TILES)
            def _(i, is_last):
                act.wait_ge(x_turned, 2 * i + 2)
                nc.scalar.activation(x_t[:, 4:8, :], quarters(turn1), ACT.Copy).then_inc(x_t_hi, 1)
                act.wait_ge(projected, 4 * i + 1)
                nc.scalar.activation(squares[:, 0:Q_LORA], proj[0][:, 0:Q_LORA], ACT.Square, accum_out=stat2[:, 0:1]).then_inc(lat_squared, 1)
                nc.scalar.activation(squares[:, Q_LORA:Q_LORA + KV_LORA], proj[0][:, Q_LORA:Q_LORA + KV_LORA], ACT.Square,
                                     accum_out=stat2[:, 1:2]).then_inc(lat_squared, 1)
                act.wait_ge(dve_link, LINKS * i + 2)
                nc.scalar.activation(stat2[:, 4:6], stat2[:, 2:4], ACT.Sqrt).then_inc(lat_root, 1)
                if not is_last:
                    norm_x(i + 1)
                act.wait_ge(projected, 4 * i + 2)
                nc.scalar.activation(q_sw[:, :], proj[1][:, :], ACT.Copy, scale=SW_SCALE).then_inc(q_sw_copied, 1)
                act.wait_ge(projected, 4 * i + 4)
                after(act, st["v_sw"], 16 * i)
                nc.scalar.activation(v_sw[:, :], proj[3][:, :], ACT.Copy).then_inc(v_sw_copied, 1)
                act.wait_ge(q_up, i + 1)
                nc.scalar.activation(q[:, 0:4, :], up0[:, 0:4 * QK].rearrange("p (h e) -> p h e", h=4), ACT.Copy,
                                     scale=MLA_SCALE).then_inc(q_copied, 1)
                nc.scalar.activation(q[:, 4:8, :], up1[:, 0:4 * QK].rearrange("p (h e) -> p h e", h=4), ACT.Copy,
                                     scale=MLA_SCALE).then_inc(q_copied, 1)
                act.wait_ge(v_up, i + 1)
                after(act, st["v"], 16 * i)
                nc.scalar.activation(v[:, :], proj[0][:, :], ACT.Copy).then_inc(v_copied, 1)
                act.wait_ge(k_sw_turned, i + 1)
                after(act, st["k_sw_t"], 16 * i)
                nc.scalar.activation(k_sw_t[:, :, :], quarters(turn1), ACT.Copy).then_inc(k_sw_t_copied, 1)
                act.wait_ge(q_turned, 2 * i + 2)
                after(act, st["q_t"], 16 * i)
                nc.scalar.activation(q_t[:, 4:8, :], quarters(up1, QK), ACT.Copy).then_inc(q_t_hi, 1)

        @block.vector
        def _(dve):
            v_ = nc.vector

            def rotate(link, out_lo, out_hi, lo, hi, cos, sin, tmp, final):
                v_.tensor_tensor(tmp[0], lo, cos, ALU.mult)
                v_.tensor_tensor(tmp[1], hi, sin, ALU.mult)
                v_.tensor_tensor(tmp[2], lo, sin, ALU.mult)
                link(v_.tensor_tensor(tmp[3], hi, cos, ALU.mult))
                v_.tensor_tensor(out_lo, tmp[0], tmp[1], ALU.subtract)
                v_.tensor_tensor(out_hi, tmp[2], tmp[3], ALU.add).then_inc(final, 1)

            def norm_x(i):
                link = Chain(dve, x_link, 2 * i).link
                dve.wait_ge(x_squared, i + 1)
                link(v_.tensor_scalar(stat[:, 1:2], stat[:, 0:1], 1.0 / D_MODEL, EPS, ALU.mult, ALU.add))
                dve.wait_ge(x_root, i + 1)
                link(v_.reciprocal(stat[:, 0:1], stat[:, 2:3]))
                dve.wait_ge(gain_in, 16 * 3)
                after(dve, x_turned, 2 * i)
                v_.scalar_tensor_tensor(xn[:, :], x[:, :], stat[:, 0:1], g_mix[:, :], ALU.mult, ALU.mult).then_inc(xn_done, 1)

            norm_x(0)

            @stepped_to_last(dve, TILES)
            def _(i, is_last):
                chain = Chain(dve, dve_link, LINKS * i)
                link = chain.link
                dve.wait_ge(x_turned, 2 * i + 1)
                v_.tensor_copy(x_t[:, 0:4, :], quarters(turn0)).then_inc(x_t_lo, 1)
                dve.wait_ge(lat_squared, 2 * i + 2)
                link(v_.tensor_scalar(stat2[:, 2:3], stat2[:, 0:1], 1.0 / Q_LORA, EPS, ALU.mult, ALU.add))
                link(v_.tensor_scalar(stat2[:, 3:4], stat2[:, 1:2], 1.0 / KV_LORA, EPS, ALU.mult, ALU.add))
                dve.wait_ge(lat_root, i + 1)
                link(v_.reciprocal(stat2[:, 0:2], stat2[:, 4:6]))
                after(dve, st["ckv"], 16 * i)
                after(dve, lat_turned, i)
                v_.scalar_tensor_tensor(cq[:, :], proj[0][:, 0:Q_LORA], stat2[:, 0:1], g_q[:, :], ALU.mult, ALU.mult)
                v_.scalar_tensor_tensor(ckv[:, :], proj[0][:, Q_LORA:Q_LORA + KV_LORA], stat2[:, 1:2], g_kv[:, :],
                                        ALU.mult, ALU.mult).then_inc(lat_normed, 1)
                dve.wait_ge(angles_in, 16 * i + 16)
                after(dve, st["kr"], 16 * i)
                k0 = Q_LORA + KV_LORA
                rotate(link, kr[:, 0:HALF], kr[:, HALF:ROPE], proj[0][:, k0:k0 + HALF], proj[0][:, k0 + HALF:k0 + ROPE],
                       angles[:, 0:HALF], angles[:, HALF:ROPE], [rot_k[:, n, :] for n in range(4)], k_rotated)
                if not is_last:
                    norm_x(i + 1)
                dve.wait_ge(projected, 4 * i + 3)
                after(dve, st["k_sw"], 16 * i)
                after(dve, k_sw_turned, i)
                v_.tensor_copy(k_sw[:, :], proj[2][:, :]).then_inc(k_sw_copied, 1)
                dve.wait_ge(lat_turned, i + 1)
                after(dve, st["kr_t"], 16 * i)
                v_.tensor_copy(cq_t0[:, :], turn0[:, 0:P])
                v_.tensor_copy(cq_t1[:, :], turn0[0:Q_LORA - P, P:2 * P])
                v_.tensor_copy(ckv_t[:, :], turn0[:, 2 * P:3 * P])
                v_.tensor_copy(kr_t[:, :], turn0[0:ROPE, 3 * P:4 * P]).then_inc(lat_t, 1)
                dve.wait_ge(kn_up, i + 1)
                after(dve, st["kn_t"], 16 * i)
                v_.tensor_copy(kn_t[:, :, :], quarters(turn1)).then_inc(kn_copied, 1)
                dve.wait_ge(q_copied, 2 * i + 2)
                cos = angles[:, 0:HALF].unsqueeze(1).broadcast_to([P, HEADS, HALF])
                sin = angles[:, HALF:ROPE].unsqueeze(1).broadcast_to([P, HEADS, HALF])
                rotate(link, q[:, :, NOPE:NOPE + HALF], q[:, :, NOPE + HALF:QK], q[:, :, NOPE:NOPE + HALF],
                       q[:, :, NOPE + HALF:QK], cos, sin, [rot[:, n, :, :] for n in range(4)], q_rotated)
                dve.wait_ge(q_sw_turned, i + 1)
                after(dve, st["q_sw_t"], 16 * i)
                v_.tensor_copy(q_sw_t[:, :, :], quarters(turn0)).then_inc(q_sw_t_copied, 1)
                dve.wait_ge(q_turned, 2 * i + 1)
                after(dve, st["q_t"], 16 * i)
                v_.tensor_copy(q_t[:, 0:4, :], quarters(up0, QK)).then_inc(q_t_lo, 1)
                assert chain.n == LINKS

        @block.tensor
        def _(pe):
            mm, turn = nc.tensor.matmul, nc.tensor.transpose

            def turns(out_bank, src, step=P, rows=P):
                for a in range(4):
                    last = turn(quarters(out_bank, rows)[:, a, :], src(a), ident[:, :])
                return last

            @stepped(pe, TILES)
            def _(i):
                pe.wait_ge(xn_done, i + 1)
                after(pe, q_sw_t_copied, i)
                turns(turn0, lambda a: xn[:, a * P:(a + 1) * P]).then_inc(x_turned, 1)
                after(pe, k_sw_t_copied, i)
                turns(turn1, lambda a: xn[:, (4 + a) * P:(5 + a) * P]).then_inc(x_turned, 1)
                pe.wait_ge(x_t_lo, i + 1)
                pe.wait_ge(x_t_hi, i + 1)
                for n, free in enumerate((v_copied, q_sw_copied, k_sw_copied, v_sw_copied)):
                    after(pe, free, i)
                    pe.wait_ge(columns_in[n], 16)
                    c0, width = COLUMNS[n]
                    for k in range(KC):
                        last = mm(proj[n][:, 0:width], x_t[:, k, :], w_in[:, k, c0:c0 + width], start=(k == 0), stop=(k == KC - 1))
                    last.then_inc(projected, 1)
                pe.wait_ge(lat_normed, i + 1)
                pe.wait_ge(k_rotated, i + 1)
                turn(turn0[:, 0:P], cq[:, 0:P], ident[:, :])
                turn(turn0[0:Q_LORA - P, P:2 * P], cq[:, P:Q_LORA], ident[:, :])
                turn(turn0[:, 2 * P:3 * P], ckv[:, :], ident[:, :])
                turn(turn0[0:ROPE, 3 * P:4 * P], kr[:, :], ident[:, :]).then_inc(lat_turned, 1)
                pe.wait_ge(lat_t, i + 1)
                pe.wait_ge(weights_in, 16 * N_W)
                after(pe, q_t_lo, i)
                after(pe, q_t_hi, i)
                for n, out in enumerate((up0, up1)):
                    at = slice(n * 4 * QK, (n + 1) * 4 * QK)
                    mm(out[:, 0:4 * QK], cq_t0[:, :], w_uq0[:, at], start=True, stop=False)
                    last = mm(out[:, 0:4 * QK], cq_t1[:, :], w_uq1[:, at], start=False, stop=True)
                last.then_inc(q_up, 1)
                for a in range(4):
                    last = mm(turn1[:, a * P:(a + 1) * P], w_uk[:, a * P:(a + 1) * P], ckv_t[:, :], start=True, stop=True)
                last.then_inc(kn_up, 1)
                mm(proj[0][:, :], ckv_t[:, :], w_uv[:, :], start=True, stop=True).then_inc(v_up, 1)
                pe.wait_ge(q_sw_copied, i + 1)
                turns(turn0, lambda a: q_sw[:, a * P:(a + 1) * P]).then_inc(q_sw_turned, 1)
                pe.wait_ge(k_sw_copied, i + 1)
                pe.wait_ge(kn_copied, i + 1)
                turns(turn1, lambda a: k_sw[:, a * P:(a + 1) * P]).then_inc(k_sw_turned, 1)
                pe.wait_ge(q_rotated, i + 1)
                turns(up0, lambda a: q[:, a, :], rows=QK).then_inc(q_turned, 1)
                turns(up1, lambda a: q[:, 4 + a, :], rows=QK).then_inc(q_turned, 1)


class PromptHeads:

    def __init__(self, nc, t, sb, kind):
        self.t, self.kind, self.latent = t, kind, kind == "latent"
        self.dim = QK if self.latent else 64
        self.q_t, self.k_t = ([sb(f"{kind}_{n}{u}", [P, SEQ]) for u in range(2)] for n in ("q_t", "k_t"))
        self.v, self.bias = ([sb(f"{kind}_{n}{u}", shape) for u in range(2)] for n, shape in (("v", [P, PROMPT_TILES, 64]), ("bias", [P, SEQ])))
        self.head_in = [phase_semaphore(nc, t["phase_sems"], f"b_{kind}_head{u}_in") for u in range(2)]
        self.shared_in = phase_semaphore(nc, t["phase_sems"], f"b_{kind}_shared_in") if self.latent else None

    def pad(self, eng, padded):
        for u in range(2):
            eng.memset(self.q_t[u][self.dim:P, :], 0.0).then_inc(padded, 1)
            eng.memset(self.k_t[u][self.dim:P, :], 0.0).then_inc(padded, 1)

    def load_shared(self, sp):
        for u in range(2):
            sp.dma_start(self.k_t[u][NOPE:QK, :], self.t["kr_t"][:, 0:SEQ]).then_inc(self.shared_in, 16)
            sp.dma_start(self.bias[u][:, :], self.t["c_causal"][0]).then_inc(self.shared_in, 16)

    def load(self, sp, i, u):
        t, done, h = self.t, self.head_in[u], i * 2 + u
        q_t, k_t = self.q_t[u], self.k_t[u]
        if self.latent:
            sp.dma_start(q_t[0:QK, :], t["q_t"][bass.ds(h, 1), :, 0:SEQ].rearrange("a e n -> e (a n)")).then_inc(done, 16)
            sp.dma_start(k_t[0:NOPE, :], t["kn_t"][bass.ds(h * NOPE, NOPE), 0:SEQ]).then_inc(done, 16)
        else:
            sp.dma_start(q_t[0:64, :], t["q_sw_t"][bass.ds(h * 64, 64), 0:SEQ]).then_inc(done, 16)
            sp.dma_start(k_t[0:64, :], t["k_sw_t"][bass.ds(h * 64, 64), 0:SEQ]).then_inc(done, 16)
            sp.dma_start(self.bias[u][:, :], t["c_window"][bass.ds(h, 1), :, :].rearrange("a e n -> e (a n)")).then_inc(done, 16)
        values = (t["v_mla"] if self.latent else t["swv_all"]).rearrange("(a p) n -> p a n", p=P)
        sp.dma_start(self.v[u][:, :, :], values[:, 0:PROMPT_TILES, bass.ds(h * 64, 64)]).then_inc(done, 16)


def attend_prompt(nc, t, ident):
    with ExitStack() as ctx:
        def sb(name, shape, dt=F32):
            return ctx.enter_context(nc.sbuf_tensor(f"b_{name}", shape, dt))

        def pair(name, shape):
            return [sb(f"{name}{n}", shape) for n in range(2)]

        kinds = [PromptHeads(nc, t, sb, kind) for kind in ("latent", "window")]
        scores, probs_t = [sb(f"scores{n}", [P, SEQ]) for n in range(4)], pair("probs_t", [P, PROMPT_TILES, P])
        out = pair("out", [P, PROMPT_TILES, 64])
        top, low = sb("top", [P, 16]), sb("low", [P, 16])
        total, inverse = sb("total", [P, 16]), sb("inverse", [P, 16])
        carrier = sb("carrier", [1, 1])
        score_bank = [ctx.enter_context(nc.psum_tensor(f"b_scorebank{n}", [P, SEQ], F32)) for n in range(2)]
        turn = [ctx.enter_context(nc.psum_tensor(f"b_turn{n}", [P, 4, P], F32)) for n in range(2)]
        out_bank = [ctx.enter_context(nc.psum_tensor(f"b_sum{n}", [P, 512], F32)) for n in range(2)]

        STEPS = [(u, tile) for u in range(2) for tile in range(PROMPT_TILES)]
        N = len(STEPS)
        WIDE = [s for s, (_, tile) in enumerate(STEPS) if tile >= 4]

        padded = phase_semaphore(nc, t["phase_sems"], "b_padded")

        for heads in kinds:
            latent = heads.latent
            q_t, k_t, v, bias, shared_in, head_in = heads.q_t, heads.k_t, heads.v, heads.bias, heads.shared_in, heads.head_in

            def sem(name):
                return phase_semaphore(nc, t["phase_sems"], f"b_{heads.kind}_{name}")

            scored, maxed, lowered, exped, inverted = sem("scored"), sem("maxed"), sem("lowered"), sem("exped"), sem("inverted")
            turned0, turned1, copied0, copied1 = sem("turned0"), sem("turned1"), sem("copied0"), sem("copied1")
            summed, normed = sem("summed"), sem("normed")
            stored = [sem("stored0"), sem("stored1")]
            LOADS = 3 if latent else 4

            def wide_before(s):
                return sum(1 for w in WIDE if w < s)

            with nc.Block() as block:
                @block.sync
                def _(sp):
                    if latent:
                        heads.load_shared(sp)
                        for u in range(2):
                            heads.load(sp, 0, u)

                    with sp.Fori(1, 4) as i:
                        for u in range(2):
                            wait_apart(sp, t, summed, N * i - (N // 2) * (1 - u))
                            heads.load(sp, i, u)
                    if latent:
                        for u in range(2):
                            kinds[1].load(sp, 0, u)

                @block.scalar
                def _(act):
                    o_cat = t["o_cat"].rearrange("(a p) n -> p a n", p=P)

                    def copy_wide(act, i, s):
                        w = len(WIDE) * i + wide_before(s)
                        n = STEPS[s][1] - 3
                        act.wait_ge(turned1, w + 1)
                        after(act, summed, N * i + max(s - 1, 0))
                        nc.scalar.activation(probs_t[s % 2][:, 4:4 + n, :], turn[1][:, 0:n, :], ACT.Copy).then_inc(copied1, 1)

                    def store(act, i, u):
                        act.wait_ge(normed, N * i + PROMPT_TILES * (u + 1))
                        at = i * 128 + (u * 64 + (0 if latent else 512))
                        act.dma_start(o_cat[:, 0:PROMPT_TILES, bass.ds(at, 64)], out[u][:, :, :]).then_inc(stored[u], 16)

                    @stepped(act, 4)
                    def _(i):
                        for s, (u, tile) in enumerate(STEPS):
                            width = P * (tile + 1)
                            act.wait_ge(lowered, N * i + s + 1)
                            nc.scalar.activation(scores[s % 4][:, 0:width], scores[s % 4][:, 0:width], ACT.Exp, bias=low[:, s:s + 1],
                                                 accum_out=total[:, s:s + 1]).then_inc(exped, 1)
                            if s >= 2 and STEPS[s - 2][1] >= 4:
                                copy_wide(act, i, s - 2)
                            if s == 11:
                                store(act, i, 0)
                            if s == 4:
                                shift_window(act, t, "k", i + (0 if latent else DEC_BATCH // 2))
                        copy_wide(act, i, N - 2)
                        copy_wide(act, i, N - 1)
                        store(act, i, 1)

                    for u in range(2):
                        act.wait_ge(stored[u], 16 * 4)

                @block.vector
                def _(dve):
                    v_ = nc.vector
                    if latent:
                        for kind in kinds:
                            kind.pad(v_, padded)

                    def copy_first(i, s):
                        n = min(STEPS[s][1] + 1, 4)
                        dve.wait_ge(turned0, N * i + s + 1)
                        after(dve, summed, N * i + max(s - 1, 0))
                        v_.tensor_copy(probs_t[s % 2][:, 0:n, :], turn[0][:, 0:n, :]).then_inc(copied0, 1)

                    def norm(i, s):
                        u, tile = STEPS[s]
                        dve.wait_ge(exped, N * i + s + 1)
                        v_.reciprocal(inverse[:, s:s + 1], total[:, s:s + 1]).then_inc(inverted, 1)
                        dve.wait_ge(inverted, N * i + s + 1)
                        dve.wait_ge(summed, N * i + s + 1)
                        if tile == 0:
                            after(dve, stored[u], 16 * i)
                        v_.tensor_scalar(out[u][:, tile, :], out_bank[s % 2][:, 0:64], inverse[:, s:s + 1], None, ALU.mult).then_inc(normed, 1)

                    @stepped(dve, 4)
                    def _(i):
                        dve.wait_ge(head_in[0], 16 * LOADS * i + 16 * LOADS)
                        if latent:
                            dve.wait_ge(shared_in, 16 * 4)
                        for s, (u, tile) in enumerate(STEPS):
                            b, width = s % 2, P * (tile + 1)
                            if s == PROMPT_TILES:
                                dve.wait_ge(head_in[1], 16 * LOADS * i + 16 * LOADS)
                            if s >= 4:
                                dve.wait_ge(turned0, N * i + s - 3)
                                if STEPS[s - 4][1] >= 4:
                                    dve.wait_ge(turned1, len(WIDE) * i + wide_before(s - 3))
                            dve.wait_ge(scored, N * i + s + 1)
                            v_.memset(carrier[:, :], 0.0)
                            v_.tensor_tensor_reduce(scores[s % 4][:, 0:width], score_bank[b][:, 0:width], bias[u][:, SEQ - width:SEQ], 1.0, -3e38,
                                                    ALU.add, ALU.max, top[:, s:s + 1]).then_inc(maxed, 1)
                            dve.wait_ge(maxed, N * i + s + 1)
                            v_.tensor_scalar(low[:, s:s + 1], top[:, s:s + 1], -1.0, None, ALU.mult).then_inc(lowered, 1)
                            if s >= 2:
                                copy_first(i, s - 2)
                            if s >= 3:
                                norm(i, s - 3)
                        copy_first(i, N - 2)
                        norm(i, N - 3)
                        copy_first(i, N - 1)
                        norm(i, N - 2)
                        norm(i, N - 1)

                @block.tensor
                def _(pe):
                    mm, transpose = nc.tensor.matmul, nc.tensor.transpose

                    def score(i, s):
                        u, tile = STEPS[s]
                        if tile == 0:
                            pe.wait_ge(head_in[u], 16 * LOADS * i + 16 * LOADS)
                            if latent:
                                pe.wait_ge(shared_in, 16 * 4)
                                pe.wait_ge(padded, 4)
                        after(pe, maxed, N * i + max(s - 1, 0))
                        width = P * (tile + 1)
                        for c in range(0, width, 512):
                            w = min(512, width - c)
                            last = mm(score_bank[s % 2][:, c:c + w], q_t[u][:, tile * P:(tile + 1) * P], k_t[u][:, c:c + w],
                                      start=True, stop=True)
                        last.then_inc(scored, 1)

                    def turns(i, s):
                        tile = STEPS[s][1]
                        pe.wait_ge(exped, N * i + s + 1)
                        after(pe, copied0, N * i + s)
                        for k in range(min(tile + 1, 4)):
                            last = transpose(turn[0][:, k, :], scores[s % 4][:, k * P:(k + 1) * P], ident[:, :])
                        last.then_inc(turned0, 1)
                        if tile >= 4:
                            after(pe, copied1, len(WIDE) * i + wide_before(s))
                            for k in range(4, tile + 1):
                                last = transpose(turn[1][:, k - 4, :], scores[s % 4][:, k * P:(k + 1) * P], ident[:, :])
                            last.then_inc(turned1, 1)

                    def sums(i, s):
                        u, tile = STEPS[s]
                        pe.wait_ge(copied0, N * i + s + 1)
                        after(pe, normed, N * i + max(s - 1, 0))
                        for k in range(tile + 1):
                            if k == 4:
                                pe.wait_ge(copied1, len(WIDE) * i + wide_before(s) + 1)
                            last = mm(out_bank[s % 2][:, 0:64], probs_t[s % 2][:, k, :], v[u][:, k, :], start=(k == 0), stop=(k == tile))
                        last.then_inc(summed, 1)

                    @stepped(pe, 4)
                    def _(i):
                        score(i, 0)
                        score(i, 1)
                        for s in range(N):
                            if s + 2 < N:
                                score(i, s + 2)
                            turns(i, s)
                            if s >= 1:
                                sums(i, s - 1)
                        sums(i, N - 1)


CHUNKS = 4
TILES_CHUNK = 16
HT = HEADS * DEC_SEQ


def attend_latent(nc, t, ident):
    with ExitStack() as ctx:
        def sb(name, shape, dt=F32):
            return ctx.enter_context(nc.sbuf_tensor(f"lat_{name}", shape, dt))

        def sem(name):
            return phase_semaphore(nc, t["phase_sems"], f"lat_{name}")

        page_rows, page_part = sb("page_rows", [P, 4 * DEC_BATCH], I32), sb("page_part", [P, 1])
        gather_rows = sb("gather_rows", [P, 4 * DEC_BATCH], I32)
        rows_of = [sb(f"rows{u}", [P, CHUNKS], I32) for u in range(2)]
        kv_of = [[sb(f"kv{u}{c}", [P, TILES_CHUNK * KV_LORA]) for c in range(CHUNKS)] for u in range(2)]
        kr_of = [[sb(f"kr{u}{c}", [P, TILES_CHUNK * ROPE]) for c in range(CHUNKS)] for u in range(2)]
        kv_t = [sb(f"kv_t{n}", [P, TILES_CHUNK, P]) for n in range(2)]
        kr_t = [sb(f"kr_t{n}", [P, 4, P]) for n in range(2)]
        q_nope, q_rope = sb("q_nope", [NOPE, HEADS, N_SAMPLE]), sb("q_rope", [P, HEADS, N_SAMPLE])
        w_uk_t, w_uv = sb("w_uk_t", [NOPE, HEADS, KV_LORA]), sb("w_uv", [P, 512])
        q_lat = sb("q_lat", [P, DEC_BATCH, HT])
        q_pad = sb("q_pad", [P, DEC_BATCH, 4, HT])
        new_rows, new_t, new_kr_t = sb("new_rows", [N_SAMPLE, KV_LORA]), sb("new_t", [P, N_SAMPLE]), sb("new_kr_t", [ROPE, N_SAMPLE])
        new_kv, new_kv_of = sb("new_kv", [DEC_SEQ, DEC_BATCH, KV_LORA]), [sb(f"new_kv{u}", [DEC_SEQ, KV_LORA]) for u in range(2)]
        new_mask, new_scores = sb("new_mask", [DEC_SEQ, HT]), sb("new_scores", [DEC_SEQ, DEC_BATCH, HT])
        scores_of = [sb(f"scores{u}", [P, CHUNKS * TILES_CHUNK + 1, HT]) for u in range(2)]
        part_max, part_sum = sb("part_max", [P, CHUNKS + 1, HT]), sb("part_sum", [P, CHUNKS + 1, HT])
        all_max, all_sum = sb("all_max", [P, P]), sb("all_sum", [P, HT])
        carrier = sb("carrier", [P, 1])
        top, top_wide = sb("top", [HT, 1]), sb("top_wide", [HT, P])
        ones, inverse = sb("ones", [P, P]), sb("inverse", [P, HT])
        o_lat = sb("o_lat", [P, HEADS, DEC_BATCH, DEC_SEQ])
        out = sb("out", [N_SAMPLE, 512])

        def bank(name):
            return ctx.enter_context(nc.psum_tensor(f"lat_{name}", [P, 512], F32))

        turn, turn_kr = [bank("turn0"), bank("turn1")], bank("turn_kr")
        score_bank = [bank("score0"), bank("score1")]
        misc, out_bank = bank("misc"), bank("out_bank")
        max_t_bank, max_t, spread, total = misc[:, 0:P], misc[0:HT, 0:P], misc[:, P:P + HT], misc[:, P + HT:P + 2 * HT]

        inputs_in, rows_ready, rows_copied = sem("inputs_in"), sem("rows_ready"), sem("rows_copied")
        gathered_kv, gathered_kr = [[[sem(f"gathered_{k}{u}{c}") for c in range(CHUNKS)] for u in range(2)] for k in ("kv", "kr")]
        kr_turned, kr_copied = sem("kr_turned"), sem("kr_copied")
        even_turned, odd_turned, even_copied, odd_copied = sem("even_turned"), sem("odd_turned"), sem("even_copied"), sem("odd_copied")
        scored, score_copied = sem("scored"), sem("score_copied")
        maxed, max_turned, topped, top_spread = sem("maxed"), sem("max_turned"), sem("topped"), sem("top_spread")
        lowered, exped, summed_parts, totalled = sem("lowered"), sem("exped"), sem("summed_parts"), sem("totalled")
        used, weighted, normed = [sem(f"used{c}") for c in range(CHUNKS)], sem("weighted"), sem("normed")
        dve_link, new_placed, inverted = sem("dve_link"), sem("new_placed"), sem("inverted")
        top_found, parts_added = sem("top_found"), sem("parts_added")
        q_lat_done, q_lat_copied, new_turned, new_t_copied, new_scored, q_padded = (
            sem("q_lat_done"), sem("q_lat_copied"), sem("new_turned"), sem("new_t_copied"), sem("new_scored"), sem("q_padded"))
        ones_set, out_done, out_copied, stored = sem("ones_set"), sem("out_done"), sem("out_copied"), sem("stored")
        sample = slice(SEQ, SEQ + N_SAMPLE)
        LINKS = 3
        N_IN = 13
        C2, C5 = 2 * CHUNKS, CHUNKS + 1

        def by_requests(eng, step):
            @stepped(eng, DEC_BATCH // 2)
            def _(i):
                for u in range(2):
                    step(2 * i + u, u, i)

        def has_previous(n):
            return not (isinstance(n, int) and n == 0)

        with nc.Block() as block:
            @block.sync
            def _(sp):
                def load(dst, src):
                    sp.dma_start(dst, src).then_inc(inputs_in, 16)

                load(page_rows[:, :], t["page_rows"])
                load(page_part[:, :], t["c_page_part"])
                load(q_nope[:, :, :], t["q_t"][:, 0:NOPE, sample].rearrange("h e n -> e h n"))
                load(w_uk_t[:, :, :], t["w_uk_t"])
                for u in range(4):
                    load(q_rope[u * ROPE:(u + 1) * ROPE, :, :], t["q_t"][:, NOPE:QK, sample].rearrange("h e n -> e h n"))
                load(new_rows[:, :], t["kv_all"][sample, :])
                load(new_kr_t[:, :], t["kr_t"][:, sample])
                load(new_kv[:, :, :], t["kv_all"][sample, :].rearrange("(b t) c -> t b c", t=DEC_SEQ))
                load(new_mask[:, :], t["c_new_mask"])
                load(w_uv[:, :], t["w_uv"])

                @stepped(sp, DEC_BATCH)
                def _(n):
                    for part in range(SHIFT_PARTS):
                        wait_apart(sp, t, scored, C2 * n + 2 * (part + 1))
                        shift_window(sp, t, "v", n, part, SHIFT_PARTS)

                sp.wait_ge(out_copied, 1)
                sp.dma_start(t["o_cat"][sample, 0:512], out[:, :]).then_inc(stored, 16)
                sp.wait_ge(stored, 16)

            @block.gpsimd
            def _(gp):
                gp.wait_ge(rows_ready, 1)

                def step(n, u, r):
                    for c in range(CHUNKS):
                        after(gp, used[c], n - 1)
                        nc.gpsimd.tensor_copy(rows_of[u][:, c:c + 1], gather_rows[:, bass.ds(n * CHUNKS + c, 1)]).then_inc(rows_copied, 1)
                        gp.wait_ge(rows_copied, n * CHUNKS + (c + 1))
                        nc.gpsimd.tensor_tensor(carrier[:, 0:1], page_part[:, 0:1], page_part[:, 0:1], ALU.add)
                        offset = bass.IndirectOffsetOnAxis(ap=rows_of[u][:, c:c + 1], axis=0)
                        gp.indirect_dma_start(out=kv_of[u][c][:, :], out_offset=None, in_=t["cache_kv"], in_offset=offset).then_inc(gathered_kv[u][c], 16)
                        gp.indirect_dma_start(out=kr_of[u][c][:, :], out_offset=None, in_=t["cache_kr"], in_offset=offset).then_inc(gathered_kr[u][c], 16)

                by_requests(gp, step)

            @block.tensor
            def _(pe):
                mm, transpose = nc.tensor.matmul, nc.tensor.transpose
                pe.wait_ge(inputs_in, 16 * N_IN)
                for h in range(HEADS):
                    last = mm(score_bank[0][:, h * 64:(h + 1) * 64], w_uk_t[:, h, :], q_nope[:, h, :], start=True, stop=True)
                last.then_inc(q_lat_done, 1)
                transpose(score_bank[1][:, 0:N_SAMPLE], new_rows[:, :], ident[0:N_SAMPLE, 0:N_SAMPLE]).then_inc(new_turned, 1)
                pe.wait_ge(q_lat_copied, 1)
                pe.wait_ge(new_t_copied, 1)
                for b in range(DEC_BATCH):
                    at = slice(b * DEC_SEQ, (b + 1) * DEC_SEQ)
                    place = score_bank[1][0:DEC_SEQ, b * HT:(b + 1) * HT]
                    mm(place, new_t[:, at], q_lat[:, b, :], start=True, stop=False)
                    last = mm(place.rearrange("p (h t) -> p h t", h=HEADS), new_kr_t[:, at], q_rope[0:ROPE, :, at], start=False, stop=True)
                last.then_inc(new_scored, 1)
                pe.wait_ge(new_placed, 1)
                pe.wait_ge(q_padded, 1)
                pe.wait_ge(ones_set, 1)

                def turn_rotary(n, u, r, c):
                    kr = kr_of[u]
                    pe.wait_ge(gathered_kr[u][c], 16 * r + 16)
                    after(pe, kr_copied, CHUNKS * n + c)
                    for g in range(4):
                        last = transpose(turn_kr[:, g * P:(g + 1) * P], kr[c][:, g * P:(g + 1) * P], ident[:, :])
                    last.then_inc(kr_turned, 1)
                    pe.wait_ge(gathered_kv[u][c], 16 * r + 16)

                def turns(n, u, c, half):
                    kv = kv_of[u]
                    for g in (2 * half, 2 * half + 1):
                        copied, turned = ((even_copied, even_turned), (odd_copied, odd_turned))[g % 2]
                        after(pe, copied, C2 * n + (2 * c + g // 2))
                        for a in range(4):
                            at = (4 * g + a) * P
                            last = transpose(turn[g % 2][:, a * P:(a + 1) * P], kv[c][:, at:at + P], ident[:, :])
                        last.then_inc(turned, 1)

                def score(n, c, half):
                    pe.wait_ge(kr_copied, CHUNKS * n + (c + 1))
                    pe.wait_ge(even_copied, C2 * n + (2 * c + half + 1))
                    pe.wait_ge(odd_copied, C2 * n + (2 * c + half + 1))
                    after(pe, score_copied, C2 * n + (2 * c + half - 1))
                    for g in (2 * half, 2 * half + 1):
                        place = score_bank[half][:, (g % 2) * 4 * HT:(g % 2 + 1) * 4 * HT]
                        mm(place, kr_t[c % 2][:, g, :], q_pad[:, bass.ds(n, 1), :, :].rearrange("p a u q -> p (a u q)"), start=True, stop=False,
                           skip_group_check=True)
                        for a in range(4):
                            last = mm(place[:, a * HT:(a + 1) * HT], kv_t[c % 2][:, 4 * g + a, :],
                                      q_lat[:, bass.ds(n, 1), :].rearrange("p a q -> p (a q)"), start=False, stop=(a == 3), skip_group_check=True)
                    last.then_inc(scored, 1)

                def spread_top(n):
                    pe.wait_ge(topped, n)
                    mm(spread, top_wide[:, :], ident[0:HT, 0:HT], start=True, stop=True).then_inc(top_spread, 1)

                def weigh(n, u):
                    kv, scores = kv_of[u], scores_of[u]
                    after(pe, normed, n - 1)
                    for c in range(CHUNKS):
                        pe.wait_ge(exped, C5 * n - (CHUNKS - c))
                        for k in range(TILES_CHUNK):
                            last = mm(out_bank[:, 0:HT], kv[c][:, k * P:(k + 1) * P], scores[:, c * TILES_CHUNK + k, :],
                                      start=(c == 0 and k == 0), stop=False)
                        last.then_inc(used[c], 1)
                    pe.wait_ge(exped, C5 * n)
                    mm(out_bank[:, 0:HT], new_kv_of[u][:, :], scores[0:DEC_SEQ, CHUNKS * TILES_CHUNK, :], start=False, stop=True).then_inc(weighted, 1)

                def total_up(n):
                    pe.wait_ge(summed_parts, n)
                    mm(total, ones[:, :], all_sum[:, :], start=True, stop=True).then_inc(totalled, 1)

                def step(n, u, r):
                    turn_rotary(n, u, r, 0)
                    turns(n, u, 0, 0)
                    turns(n, u, 0, 1)
                    if has_previous(n):
                        spread_top(n)
                    for c in range(CHUNKS):
                        if c + 1 < CHUNKS:
                            turn_rotary(n, u, r, c + 1)
                        for half in range(2):
                            if c + 1 < CHUNKS:
                                turns(n, u, c + 1, half)
                            score(n, c, half)
                    if has_previous(n):
                        weigh(n, 1 - u)
                    pe.wait_ge(maxed, n + 1)
                    transpose(max_t_bank, all_max[:, :], ident[:, :]).then_inc(max_turned, 1)
                    if has_previous(n):
                        total_up(n)

                by_requests(pe, step)
                spread_top(DEC_BATCH)
                weigh(DEC_BATCH, 1)
                total_up(DEC_BATCH)

                pe.wait_ge(normed, DEC_BATCH)
                for h in range(HEADS):
                    last = mm(score_bank[0][0:N_SAMPLE, h * 64:(h + 1) * 64], o_lat[:, h, :, :].rearrange("p b t -> p (b t)"),
                              w_uv[:, h * 64:(h + 1) * 64], start=True, stop=True)
                last.then_inc(out_done, 1)

            @block.scalar
            def _(act):
                copy = ACT.Copy

                def evacuate_rotary(n, c):
                    act.wait_ge(kr_turned, CHUNKS * n + (c + 1))
                    after(act, scored, C2 * n + (2 * c - 2))
                    nc.scalar.activation(kr_t[c % 2][:, :, :], turn_kr[:, :].rearrange("p (g k) -> p g k", g=4), copy).then_inc(kr_copied, 1)

                def evacuate(n, c, half):
                    g = 2 * half + 1
                    act.wait_ge(odd_turned, C2 * n + (2 * c + half + 1))
                    nc.scalar.activation(kv_t[c % 2][:, 4 * g:4 * g + 4, :], turn[1][:, :].rearrange("p (g k) -> p g k", g=4), copy).then_inc(odd_copied, 1)

                def exps(n, u, c):
                    scores = scores_of[u]
                    act.wait_ge(lowered, C5 * n - (CHUNKS - c))
                    at = slice(c * TILES_CHUNK, min((c + 1) * TILES_CHUNK, CHUNKS * TILES_CHUNK + 1))
                    nc.scalar.activation(scores[:, at, :], scores[:, at, :], ACT.Exp).then_inc(exped, 1)

                def step(n, u, r):
                    scores = scores_of[u]
                    evacuate_rotary(n, 0)
                    evacuate(n, 0, 0)
                    evacuate(n, 0, 1)
                    after(act, weighted, n - 1)
                    after(act, summed_parts, n - 1)
                    for c in range(CHUNKS):
                        if c + 1 < CHUNKS:
                            evacuate_rotary(n, c + 1)
                        for half in range(2):
                            if c + 1 < CHUNKS:
                                evacuate(n, c + 1, half)
                            act.wait_ge(scored, C2 * n + (2 * c + half + 1))
                            at = c * TILES_CHUNK + 8 * half
                            nc.scalar.activation(scores[:, at:at + 8, :], score_bank[half][:, :].rearrange("p (u q) -> p u q", u=8), copy).then_inc(score_copied, 1)
                        if has_previous(n):
                            exps(n, 1 - u, c)
                    if has_previous(n):
                        exps(n, 1 - u, CHUNKS)

                by_requests(act, step)
                for c in range(CHUNKS + 1):
                    exps(DEC_BATCH, 1, c)

            @block.vector
            def _(dve):
                v_ = nc.vector
                dve.wait_ge(inputs_in, 16 * N_IN)
                v_.tensor_scalar(gather_rows[:, :], page_rows[:, :], float(PAGE // TILES_CHUNK), page_part[:, 0:1], ALU.mult, ALU.add).then_inc(rows_ready, 1)
                v_.memset(ones[:, :], 1.0).then_inc(ones_set, 1)
                setup = Chain(dve, sem("setup_link"))
                setup.link(v_.memset(all_max[:, :], 0.0))
                setup.link(v_.memset(q_pad[:, :, :, :], 0.0))
                for u in range(4):
                    rows = slice(u * ROPE, (u + 1) * ROPE)
                    last = v_.tensor_copy(q_pad[rows, :, u, :].rearrange("p b (h t) -> p b h t", h=HEADS),
                                          q_rope[rows, :, :].rearrange("p h (b t) -> p b h t", b=DEC_BATCH))
                last.then_inc(q_padded, 1)
                dve.wait_ge(q_lat_done, 1)
                v_.tensor_copy(q_lat[:, :, :].rearrange("p b (h t) -> p b h t", h=HEADS),
                               score_bank[0][:, :].rearrange("p (h b t) -> p b h t", h=HEADS, b=DEC_BATCH)).then_inc(q_lat_copied, 1)
                dve.wait_ge(new_turned, 1)
                v_.tensor_copy(new_t[:, :], score_bank[1][:, 0:N_SAMPLE]).then_inc(new_t_copied, 1)
                dve.wait_ge(new_scored, 1)
                v_.tensor_tensor(new_scores[:, :, :], score_bank[1][0:DEC_SEQ, :].rearrange("p (b q) -> p b q", b=DEC_BATCH),
                                 new_mask[:, :].unsqueeze(1).broadcast_to([DEC_SEQ, DEC_BATCH, HT]), ALU.add).then_inc(new_placed, 1)
                dve.wait_ge(new_placed, 1)
                NEW = CHUNKS * TILES_CHUNK

                def evacuate(n, c, half):
                    g = 2 * half
                    after(dve, scored, C2 * n + (2 * c + half - 3))
                    dve.wait_ge(even_turned, C2 * n + (2 * c + half + 1))
                    v_.tensor_copy(kv_t[c % 2][:, 4 * g:4 * g + 4, :], turn[0][:, :].rearrange("p (g k) -> p g k", g=4)).then_inc(even_copied, 1)

                def chunk(u, c):
                    return scores_of[u][:, c * TILES_CHUNK:(c + 1) * TILES_CHUNK, :]

                def by_column(ap):
                    return ap.rearrange("p u q -> p q u")

                def find_top(n):
                    dve.wait_ge(max_turned, n)
                    v_.tensor_reduce(top[:, :], max_t, AX.X, ALU.max).then_inc(top_found, 1)
                    dve.wait_ge(top_found, n)
                    v_.tensor_copy(top_wide[:, :], top[:, 0:1].broadcast_to([HT, P])).then_inc(topped, 1)

                def lower(n, u, c):
                    if c < CHUNKS:
                        v_.tensor_tensor(chunk(u, c), chunk(u, c), spread.unsqueeze(1).broadcast_to([P, TILES_CHUNK, HT]), ALU.subtract).then_inc(lowered, 1)
                    else:
                        v_.tensor_tensor(scores_of[u][:, NEW, :], scores_of[u][:, NEW, :], spread, ALU.subtract).then_inc(lowered, 1)

                def add_up(n, u, c):
                    dve.wait_ge(exped, C5 * n - (CHUNKS - c))
                    if c < CHUNKS:
                        v_.tensor_reduce(part_sum[:, c, :], by_column(chunk(u, c)), AX.X, ALU.add)
                    else:
                        v_.tensor_copy(part_sum[:, CHUNKS, :], scores_of[u][:, NEW, :]).then_inc(parts_added, 1)
                        dve.wait_ge(parts_added, n)
                        v_.tensor_reduce(all_sum[:, :], by_column(part_sum[:, :, :]), AX.X, ALU.add).then_inc(summed_parts, 1)

                def normalise(n):
                    dve.wait_ge(totalled, n)
                    v_.reciprocal(inverse[:, :], total).then_inc(inverted, 1)
                    dve.wait_ge(inverted, n)
                    dve.wait_ge(weighted, n)
                    v_.tensor_tensor(o_lat[:, :, bass.ds(n - 1, 1), :].rearrange("p h a t -> p h (a t)"), out_bank[:, 0:HT].rearrange("p (h t) -> p h t", h=HEADS),
                                     inverse[:, :].rearrange("p (h t) -> p h t", h=HEADS), ALU.mult).then_inc(normed, 1)

                def step(n, u, r):
                    scores, link = scores_of[u], Chain(dve, dve_link, LINKS * n).link
                    if has_previous(n):
                        find_top(n)
                    v_.tensor_copy(new_kv_of[u][:, :], new_kv[:, bass.ds(n, 1), :].rearrange("p a c -> p (a c)"))
                    link(v_.memset(scores[:, NEW, :], MASK))
                    link(v_.tensor_copy(scores[0:DEC_SEQ, NEW, :], new_scores[:, bass.ds(n, 1), :].rearrange("p a q -> p (a q)")))
                    v_.tensor_copy(part_max[:, CHUNKS, :], scores[:, NEW, :])
                    evacuate(n, 0, 0)
                    evacuate(n, 0, 1)
                    if has_previous(n):
                        dve.wait_ge(top_spread, n)
                    for c in range(CHUNKS):
                        if c + 1 < CHUNKS:
                            evacuate(n, c + 1, 0)
                        if has_previous(n):
                            lower(n, 1 - u, c)
                        if c + 1 < CHUNKS:
                            evacuate(n, c + 1, 1)
                        if has_previous(n):
                            if c > 0:
                                add_up(n, 1 - u, c - 1)
                        dve.wait_ge(score_copied, C2 * n + (2 * c + 2))
                        last = v_.tensor_reduce(part_max[:, c, :], by_column(chunk(u, c)), AX.X, ALU.max)
                    link(last)
                    v_.tensor_reduce(all_max[:, 0:HT], by_column(part_max[:, :, :]), AX.X, ALU.max).then_inc(maxed, 1)
                    if has_previous(n):
                        lower(n, 1 - u, CHUNKS)
                        add_up(n, 1 - u, CHUNKS - 1)
                        add_up(n, 1 - u, CHUNKS)
                        normalise(n)

                by_requests(dve, step)
                find_top(DEC_BATCH)
                dve.wait_ge(top_spread, DEC_BATCH)
                for c in range(CHUNKS + 1):
                    lower(DEC_BATCH, 1, c)
                for c in range(CHUNKS + 1):
                    add_up(DEC_BATCH, 1, c)
                normalise(DEC_BATCH)

                dve.wait_ge(out_done, 1)
                v_.tensor_copy(out[:, :], score_bank[0][0:N_SAMPLE, :]).then_inc(out_copied, 1)


class MixWeights:

    LOADS = 10

    def __init__(self, nc, ctx):
        def sb(name, shape, dt=F32):
            return ctx.enter_context(nc.sbuf_tensor(f"mix_{name}", shape, dt))

        self.w_out, self.w_router = sb("w_out", [P, KC, D_MODEL]), sb("w_router", [P, KC, GROUPS + EXPERTS])
        self.g_out, self.g_ffn, self.b_router = sb("g_out", [P, D_MODEL]), sb("g_ffn", [P, D_MODEL]), sb("b_router", [P, GROUPS + EXPERTS])
        self.before, self.iota = sb("before", [P, P]), sb("iota", [P, P])
        self.choice = sb("choice", [P, TILES * TOP_K, 2])
        self.real, self.spare = sb("real", [P, TILES]), sb("spare", [P, 1])
        self.loaded = nc.alloc_semaphore("mix_weights_in")


def load_mix_weights(sp, t):
    m = t["mix"]
    for dst, src in ((m.g_out[:, :], row_broadcast(t["norm_out"])), (m.w_out[:, :, :], t["w_out"].rearrange("(k p) n -> p k n", p=P)),
                     (m.g_ffn[:, :], row_broadcast(t["norm_ffn"])), (m.w_router[:, :, :], t["w_router"].rearrange("(k p) n -> p k n", p=P)),
                     (m.b_router[:, :], row_broadcast(t["b_router"])), (m.before[:, :], t["c_before"]), (m.iota[:, :], t["c_iota"]),
                     (m.choice[:, :, :], t["c_choice"]), (m.real[:, :], t["c_real"]), (m.spare[:, :], t["c_spare"])):
        sp.dma_start(dst, src).then_inc(m.loaded, 16)


def attend_window(nc, t, ident):
    with ExitStack() as ctx:
        def sb(name, shape, dt=F32):
            return ctx.enter_context(nc.sbuf_tensor(f"win_{name}", shape, dt))

        def sem(name):
            return phase_semaphore(nc, t["phase_sems"], f"win_{name}")

        def psum(name, cols):
            return ctx.enter_context(nc.psum_tensor(f"win_{name}", [P, cols], F32))

        def pair(name, shape):
            return [sb(f"{name}{u}", shape) for u in range(2)]

        bias, own_head = sb("bias", [HT, WIN_ALL]), sb("own_head", [HT, 512])
        q_heads, q_all = sb("q_heads", [P, 4, N_SAMPLE]), sb("q_all", [P, DEC_BATCH, 4, HT])
        q_now = pair("q_now", [P, 4, HT])
        k_t, v = pair("k_t", [P, 4, WIN_ALL]), pair("v", [P, WIN_TILES + 1, 512])
        scores = pair("scores", [P, WIN_ALL])
        weights = pair("weights", [P, WIN_TILES + 1, HT])
        top, low, total, inverse = pair("top", [HT, 1]), pair("low", [HT, 1]), pair("total", [HT, 1]), pair("inverse", [HT, 1])
        own, out_raw, out = sb("own", [HT, HEADS, 64]), sb("out_raw", [HT, 64]), pair("out", [HT, 64])
        carrier = sb("carrier", [1, 1])
        score_bank, turn, sum_bank = psum("score_bank", 1536), psum("turn", 1024), psum("sum_bank", 512)

        def sems(name):
            return [sem(f"{name}{u}") for u in range(2)]

        inputs_in, k_in, v_in, stored = sem("inputs_in"), sems("k_in"), sems("v_in"), sems("stored")
        q_placed, q_copied, scored, maxed, lowered, exped = sem("q_placed"), sem("q_copied"), sem("scored"), sem("maxed"), sem("lowered"), sem("exped")
        turned, copied_lo, copied_hi, summed = sem("turned"), sem("copied_lo"), sem("copied_hi"), sem("summed")
        inverted, masked, reduced, normed = sem("inverted"), sem("masked"), sem("reduced"), sem("normed")
        sample = slice(SEQ, SEQ + N_SAMPLE)
        PIECES = [(0, 512), (512, 512), (1024, WIN_ALL - 1024)]
        TILES_LO = 512 // HT

        def by_requests(eng, step):
            @stepped(eng, DEC_BATCH // 2)
            def _(i):
                for u in range(2):
                    step(2 * i + u, u, i)

        def has_previous(n):
            return not (isinstance(n, int) and n == 0)

        with nc.Block() as block:
            @block.sync
            def _(sp):
                sp.dma_start(q_heads[:, :, :], t["q_sw_t"][:, sample].rearrange("(c p) n -> p c n", p=P)).then_inc(inputs_in, 16)
                sp.dma_start(bias[:, :], t["c_window_sample"]).then_inc(inputs_in, 16)
                sp.dma_start(own_head[:, :], t["c_own_head"]).then_inc(inputs_in, 16)
                new_k = t["k_sw_t"].rearrange("(c p) n -> p c n", p=P)

                def load(n, u, r):
                    wait_apart(sp, t, scored, n - 1)
                    new = n * DEC_SEQ + SEQ
                    sp.dma_start(k_t[u][:, :, 0:WIN_KEYS], t["window_k_t"][bass.ds(n, 1), :, :, :].rearrange("b p c n -> p (b c) n")).then_inc(k_in[u], 16)
                    sp.dma_start(k_t[u][:, :, WIN_KEYS:WIN_ALL], new_k[:, :, bass.ds(new, DEC_SEQ)]).then_inc(k_in[u], 16)
                    wait_apart(sp, t, summed, n - 1)
                    sp.dma_start(v[u][:, 0:WIN_TILES, :], t["window_v"][bass.ds(n, 1), :, :, :].rearrange("b p k f -> p (b k) f")).then_inc(v_in[u], 16)
                    sp.dma_start(v[u][0:DEC_SEQ, WIN_TILES, :], t["swv_all"][bass.ds(new, DEC_SEQ), :]).then_inc(v_in[u], 16)

                by_requests(sp, load)
                load_mix_weights(sp, t)

            @block.tensor
            def _(pe):
                mm, transpose = nc.tensor.matmul, nc.tensor.transpose

                def turns(n, u):
                    pe.wait_ge(exped, n)
                    after(pe, copied_lo, n - 1)
                    after(pe, copied_hi, n - 1)
                    transpose(turn[:, 0:P], scores[u][:, 0:P], ident[:, :])
                    for k in range(1, WIN_TILES):
                        transpose(turn[:, k * HT:(k + 1) * HT], scores[u][0:HT, k * P:(k + 1) * P], ident[0:HT, 0:HT])
                    transpose(turn[0:DEC_SEQ, WIN_TILES * HT:(WIN_TILES + 1) * HT], scores[u][0:HT, WIN_KEYS:WIN_ALL], ident[0:HT, 0:HT]).then_inc(turned, 1)

                def score(n, u, r):
                    pe.wait_ge(k_in[u], 32 * r + 32)
                    pe.wait_ge(q_copied, n + 1)
                    after(pe, maxed, n)
                    for c0, width in PIECES:
                        for c in range(4):
                            last = mm(score_bank[0:HT, c0:c0 + width], q_now[u][:, c, :], k_t[u][:, c, c0:c0 + width], start=(c == 0), stop=(c == 3))
                    last.then_inc(scored, 1)

                def weigh(n, u, r):
                    pe.wait_ge(v_in[u], 32 * r + 32)
                    pe.wait_ge(copied_lo, n)
                    pe.wait_ge(copied_hi, n)
                    after(pe, masked, n - 1)
                    for k in range(WIN_TILES):
                        mm(sum_bank[0:HT, :], weights[u][:, k, :], v[u][:, k, :], start=(k == 0), stop=False)
                    mm(sum_bank[0:HT, :], weights[u][0:DEC_SEQ, WIN_TILES, :], v[u][0:DEC_SEQ, WIN_TILES, :], start=False, stop=True).then_inc(summed, 1)

                def step(n, u, r):
                    if has_previous(n):
                        turns(n, 1 - u)
                    score(n, u, r)
                    if has_previous(n):
                        weigh(n, 1 - u, r - 1 + u)

                by_requests(pe, step)
                turns(DEC_BATCH, 1)
                weigh(DEC_BATCH, 1, DEC_BATCH // 2 - 1)

            @block.scalar
            def _(act):
                def copy_hi(n, u):
                    act.wait_ge(turned, n)
                    after(act, summed, n - 2)
                    nc.scalar.activation(weights[u][:, TILES_LO:WIN_TILES, :], turn[:, TILES_LO * HT:WIN_TILES * HT].rearrange("p (k q) -> p k q", q=HT), ACT.Copy)
                    nc.scalar.activation(weights[u][0:DEC_SEQ, WIN_TILES, :], turn[0:DEC_SEQ, WIN_TILES * HT:(WIN_TILES + 1) * HT], ACT.Copy).then_inc(copied_hi, 1)

                def store(n, u):
                    act.wait_ge(normed, n)
                    act.dma_start(t["o_window"][bass.ds(n - 1, 1), :, :].rearrange("b q d -> (b q) d"), out[u][:, :]).then_inc(stored[u], 16)

                def step(n, u, r):
                    if has_previous(n):
                        copy_hi(n, 1 - u)
                    act.wait_ge(lowered, n + 1)
                    nc.scalar.activation(scores[u][0:HT, :], scores[u][0:HT, :], ACT.Exp, bias=low[u][:, 0:1], accum_out=total[u][:, 0:1]).then_inc(exped, 1)
                    if has_previous(n):
                        store(n, 1 - u)

                by_requests(act, step)
                copy_hi(DEC_BATCH, 1)
                store(DEC_BATCH, 1)
                for u in range(2):
                    act.wait_ge(stored[u], 16 * (DEC_BATCH // 2))

            @block.vector
            def _(dve):
                v_ = nc.vector
                setup = Chain(dve, sem("setup_link"))
                for u in range(2):
                    v_.memset(scores[u][:, :], 0.0)
                setup.link(v_.memset(q_all[:, :, :, :], 0.0))
                dve.wait_ge(inputs_in, 16 * 3)
                for h in range(HEADS):
                    rows = slice((h % 2) * 64, (h % 2) * 64 + 64)
                    last = v_.tensor_copy(q_all[rows, :, h // 2, h * DEC_SEQ:(h + 1) * DEC_SEQ],
                                          q_heads[rows, h // 2, :].rearrange("p (b t) -> p b t", b=DEC_BATCH))
                last.then_inc(q_placed, 1)
                dve.wait_ge(q_placed, 1)

                def copy_q(n, u):
                    v_.tensor_copy(q_now[u][:, :, :], q_all[:, bass.ds(n, 1), :, :].rearrange("p b c q -> p (b c) q")).then_inc(q_copied, 1)

                def copy_lo(n, u):
                    dve.wait_ge(turned, n)
                    v_.tensor_copy(weights[u][:, 0:TILES_LO, :], turn[:, 0:TILES_LO * HT].rearrange("p (k q) -> p k q", q=HT)).then_inc(copied_lo, 1)

                def normalise(n, u):
                    v_.reciprocal(inverse[u][:, :], total[u][:, :]).then_inc(inverted, 1)
                    dve.wait_ge(summed, n)
                    v_.tensor_tensor(own[:, :, :], sum_bank[0:HT, :].rearrange("p (h d) -> p h d", h=HEADS),
                                     own_head[:, :].rearrange("p (h d) -> p h d", h=HEADS), ALU.mult).then_inc(masked, 1)
                    dve.wait_ge(masked, n)
                    dve.wait_ge(inverted, n)
                    v_.tensor_reduce(out_raw[:, :], own[:, :, :].rearrange("p h d -> p d h"), AX.X, ALU.add).then_inc(reduced, 1)
                    dve.wait_ge(reduced, n)

                def step(n, u, r):
                    copy_q(n, u)
                    if has_previous(n):
                        copy_lo(n, 1 - u)
                    dve.wait_ge(scored, n + 1)
                    v_.memset(carrier[:, :], 0.0)
                    v_.tensor_tensor_reduce(scores[u][0:HT, :], score_bank[0:HT, 0:WIN_ALL], bias[:, :], 1.0, -3e38, ALU.add, ALU.max,
                                            top[u][:, :]).then_inc(maxed, 1)
                    dve.wait_ge(maxed, n + 1)
                    v_.tensor_scalar(low[u][:, :], top[u][:, :], -1.0, None, ALU.mult).then_inc(lowered, 1)
                    if has_previous(n):
                        normalise(n, 1 - u)
                        after(dve, stored[1 - u], 16 * (r - 1 + u))
                        v_.tensor_scalar(out[1 - u][:, :], out_raw[:, :], inverse[1 - u][:, 0:1], None, ALU.mult).then_inc(normed, 1)

                by_requests(dve, step)
                copy_lo(DEC_BATCH, 1)
                normalise(DEC_BATCH, 1)
                dve.wait_ge(stored[1], 16 * (DEC_BATCH // 2 - 1))
                v_.tensor_scalar(out[1][:, :], out_raw[:, :], inverse[1][:, 0:1], None, ALU.mult).then_inc(normed, 1)


class ExpertWeights:

    def __init__(self, nc, ctx):
        def sb(name, shape):
            return ctx.enter_context(nc.sbuf_tensor(f"ex_{name}", shape, F32))

        self.w_gate, self.w_up, self.w_down = sb("w_gate", [P, KC, D_EXPERT]), sb("w_up", [P, KC, D_EXPERT]), sb("w_down", [P, FC, D_MODEL])
        self.tickets = ctx.enter_context(nc.sbuf_tensor("ex_tickets", [P, SLOT_BLOCKS, 2], I32))
        self.x_kept = ctx.enter_context(nc.sbuf_tensor("x_kept", [P, TILES, D_MODEL], F32))
        self.gate_in, self.up_in, self.down_in = (nc.alloc_semaphore(f"ex_{n}_in") for n in ("gate", "up", "down"))


def load_expert(sp, w, t, b, before_each=(None, None, None)):
    e = sp.value_load(t["block_expert"][0:1, bass.ds(b, 1)], min_val=0, max_val=EXPERTS - 1)
    for tile, name, ready, used in ((w.w_gate, "w_gate", w.gate_in, before_each[0]), (w.w_up, "w_up", w.up_in, before_each[1]),
                                    (w.w_down, "w_down", w.down_in, before_each[2])):
        if used is not None:
            wait_apart(sp, t, used, b)
        sp.dma_start(tile[:, :, :], t[name][bass.ds(e, 1), :, :].rearrange("e (p k) n -> p (e k) n", k=tile.shape[1])).then_inc(ready, 16)


def mix_and_route(nc, t, ident):
    with ExitStack() as ctx:
        def sb(name, shape, dt=F32):
            return ctx.enter_context(nc.sbuf_tensor(f"mix_{name}", shape, dt))

        def sem(name):
            return phase_semaphore(nc, t["phase_sems"], f"mix_{name}")

        m = t["mix"]
        w_out, w_router, g_out, g_ffn, b_router = m.w_out, m.w_router, m.g_out, m.g_ffn, m.b_router
        before, iota, choice, spare, weights_in = m.before, m.iota, m.choice, m.spare, m.loaded
        real = m.real
        ones = sb("ones", [P, P])
        o, o_n, o_t = sb("o", [P, D_MODEL]), sb("o_n", [P, D_MODEL]), sb("o_t", [P, KC, P])
        x, x_mid = sb("x", [P, D_MODEL]), sb("x_mid", [P, D_MODEL])
        h, h_t = sb("h", [P, D_MODEL]), sb("h_t", [P, KC, P])
        squares, o_stat, h_stat = sb("squares", [P, D_MODEL]), sb("o_stat", [P, 6]), sb("h_stat", [P, 3])
        logits = sb("logits", [P, 8 + EXPERTS])
        group_top, group_at = sb("group_top", [P, 8]), sb("group_at", [P, 8], U32)
        group, neg_top, group_hot = sb("group", [P, 2]), sb("neg_top", [P, 2]), sb("group_hot", [P, GROUPS])
        of_group, chosen = sb("of_group", [P, GROUPS, PER_GROUP]), sb("chosen", [P, PER_GROUP])
        best, best_at, best_f = sb("best", [P, 8]), sb("best_at", [P, 8], U32), sb("best_f", [P, 2])
        group_exp, pair_exp, sums, scale = sb("group_exp", [P, GROUPS]), sb("pair_exp", [P, 2]), sb("sums", [P, 2]), sb("scale", [P, 2])
        pair, hot, hot_sum, hot_total = sb("pair", [P, 2]), sb("hot", [P, 2, EXPERTS]), sb("hot_sum", [P, EXPERTS]), sb("hot_total", [P, EXPERTS])
        ranked, real_now = sb("ranked", [P, 2, EXPERTS]), sb("real_now", [P, 1])
        CHOICES = TILES * TOP_K
        start, per_tile, blocks_of, block_end = sb("start", [P, EXPERTS]), sb("per_tile", [P, TILES]), sb("blocks_of", [P, EXPERTS]), sb("block_end", [P, EXPERTS])
        fills, upto = sb("fills", [P, EXPERTS, TILES]), sb("upto", [P, EXPERTS, EXPERTS])
        starts, past = sb("starts", [P, CHOICES, EXPERTS]), sb("past", [P, CHOICES, TILES])
        row, in_block, to_spare = sb("row", [P, CHOICES]), sb("in_block", [P, CHOICES]), sb("to_spare", [P, CHOICES])
        row_hot, block_hot, tickets_of = sb("row_hot", [P, CHOICES, P]), sb("block_hot", [P, CHOICES, SLOT_BLOCKS]), sb("tickets_of", [P, CHOICES, 2, SLOT_BLOCKS])
        passed, block_f = sb("passed", [1, MAX_BLOCKS, EXPERTS]), sb("block_f", [1, MAX_BLOCKS])
        carrier, pool_carrier = sb("carrier", [1, 1]), sb("pool_carrier", [P, 1])
        all_hot, all_rank = sb("all_hot", [P, TILES * 2, EXPERTS]), sb("all_rank", [P, TILES * 2])
        turn = ctx.enter_context(nc.psum_tensor("mix_turn", [P, D_MODEL], F32))
        turn_h = ctx.enter_context(nc.psum_tensor("mix_turn_h", [P, D_MODEL], F32))
        mixed_bank = ctx.enter_context(nc.psum_tensor("mix_bank", [P, D_MODEL], F32))
        router_bank = ctx.enter_context(nc.psum_tensor("mix_router_bank", [P, 512], F32))
        rank_bank = ctx.enter_context(nc.psum_tensor("mix_rank_bank", [P, 512], F32))

        o_in, x_in = sem("o_in"), sem("x_in")
        o_squared, o_root, o_normed, o_cleared = sem("o_squared"), sem("o_root"), sem("o_normed"), sem("o_cleared")
        o_turned, o_t_lo, o_t_hi, mixed = sem("o_turned"), sem("o_t_lo"), sem("o_t_hi"), sem("mixed")
        x_added, x_squared, x_root, h_normed = sem("x_added"), sem("x_squared"), sem("x_root"), sem("h_normed")
        h_turned, h_t_lo, h_t_hi, routed = sem("h_turned"), sem("h_t_lo"), sem("h_t_hi"), sem("routed")
        logits_done, group_topped, group_exped = sem("logits_done"), sem("group_topped"), sem("group_exped")
        pair_topped, pair_exped = sem("pair_topped"), sem("pair_exped")
        hot_done, rank_done, total_added = sem("hot_done"), sem("rank_done"), sem("total_added")
        gates_scaled, rank_picked = sem("gates_scaled"), sem("rank_picked")
        x_kept, h_stored = sem("x_kept"), sem("h_stored")
        counted, planned, sorted_out = sem("counted"), sem("planned"), sem("sorted_out")
        experts_known = sem("experts_known")
        head_link, body_link, tail_link = sem("head_link"), sem("body_link"), sem("tail_link")
        HEAD_LINKS, BODY_LINKS, TAIL_LINKS = 2, 2, 13
        N_W = MixWeights.LOADS
        LAST = TILES - 1
        HALF_D = D_MODEL // 2

        def tiled(eng, step):
            step(0)
            step(1)
            with eng.Fori(2, LAST - 1) as i:
                step(i)
            step(LAST - 1)
            step(LAST)

        def has_earlier(i, back):
            return not isinstance(i, int) or i >= back

        def is_step(i, n):
            return isinstance(i, int) and i == n

        def quarters(ap):
            return ap.rearrange("p (a c) -> p a c", a=4)

        with nc.Block() as block:
            @block.sync
            def _(sp):
                def wait(sem, value):
                    wait_apart(sp, t, sem, value)

                sp.dma_start(o[:, :], t["o_cat"][0:P, :]).then_inc(o_in, 16)
                sp.dma_start(x[:, :], t["x_all"][0:P, :]).then_inc(x_in, 16)
                def finish(i):
                    at = bass.ds(i * P, P)
                    wait(x_added, i + 1)
                    if not is_step(i, LAST):
                        sp.dma_start(x[:, :], t["x_all"][bass.ds(i * P + P, P), :]).then_inc(x_in, 16)
                    wait(h_normed, i + 1)
                    sp.dma_start(t["h_ffn"][at, :], h[:, :]).then_inc(h_stored, 16)

                @stepped(sp, LAST - 1)
                def _(i):
                    wait(o_normed, i + 1)
                    sp.dma_start(o[:, :], t["o_cat"][bass.ds(i * P + P, P), :]).then_inc(o_in, 16)
                    finish(i)

                sp.wait_ge(o_normed, LAST)
                sp.dma_start(o[0:N_SAMPLE, 0:HALF_D], t["o_cat"][SEQ:SEQ + N_SAMPLE, 0:HALF_D]).then_inc(o_in, 16)
                for b in range(DEC_BATCH):
                    sp.dma_start(o[b * DEC_SEQ:(b + 1) * DEC_SEQ, HALF_D:D_MODEL].rearrange("t (h d) -> t h d", h=HEADS),
                                 t["o_window"][b].rearrange("(h t) d -> t h d", h=HEADS)).then_inc(o_in, 16)
                finish(LAST - 1)
                finish(LAST)
                sp.wait_ge(experts_known, 1)
                load_expert(sp, t["expert"], t, 0)
                sp.wait_ge(h_stored, 16 * TILES)

            @block.tensor
            def _(pe):
                mm, transpose = nc.tensor.matmul, nc.tensor.transpose

                def turn_tile(to, of, done):
                    for k in range(KC):
                        last = transpose(to[:, k * P:(k + 1) * P], of[:, k * P:(k + 1) * P], ident[:, :])
                        if k % 4 == 3:
                            last.then_inc(done, 1)

                def turn_h_tile(j):
                    pe.wait_ge(h_normed, j + 1)
                    after(pe, h_t_lo, j)
                    after(pe, h_t_hi, j)
                    turn_tile(turn_h, h, h_turned)

                def route(j):
                    pe.wait_ge(h_t_lo, j + 1)
                    pe.wait_ge(h_t_hi, j + 1)
                    for k in range(KC):
                        last = mm(router_bank[:, 0:GROUPS + EXPERTS], h_t[:, k, :], w_router[:, k, :], start=(k == 0), stop=(k == KC - 1))
                    last.then_inc(routed, 1)

                def rank(j):
                    pe.wait_ge(hot_done, j + 1)
                    mm(rank_bank[:, 0:EXPERTS], before[:, :], hot_sum[:, :], start=True, stop=False)
                    mm(rank_bank[:, 0:EXPERTS], ones[:, :], hot_total[:, :], start=False, stop=True).then_inc(rank_done, 1)

                def step(i):
                    pe.wait_ge(o_normed, i + 1)
                    turn_tile(turn, o_n, o_turned)
                    if has_earlier(i, 2):
                        route(i - 2)
                    pe.wait_ge(o_t_lo, i + 1)
                    pe.wait_ge(o_t_hi, i + 1)
                    after(pe, x_added, i)
                    for k in range(KC):
                        for half in range(2):
                            cols = slice(half * HALF_D, (half + 1) * HALF_D)
                            last = mm(mixed_bank[:, cols], o_t[:, k, :], w_out[:, k, cols], start=(k == 0), stop=(k == KC - 1))
                    last.then_inc(mixed, 1)
                    if has_earlier(i, 1):
                        turn_h_tile(i - 1)
                    if has_earlier(i, 2):
                        rank(i - 2)

                pe.wait_ge(weights_in, 16 * N_W)
                tiled(pe, step)
                route(LAST - 1)
                rank(LAST - 1)
                turn_h_tile(LAST)
                route(LAST)
                rank(LAST)
                pe.wait_ge(total_added, TILES)
                pe.wait_ge(rank_picked, TILES)
                mm(rank_bank[:, 0:EXPERTS], ones[:, :], hot_total[:, :], start=True, stop=True).then_inc(counted, 1)
                pe.wait_ge(planned, 1)
                for c in range(CHOICES):
                    last = mm(router_bank[:, 0:2 * SLOT_BLOCKS], row_hot[:, c, :], tickets_of[:, c, :, :].rearrange("p v b -> p (v b)"),
                              start=(c == 0), stop=(c == CHOICES - 1))
                last.then_inc(sorted_out, 1)

            @block.scalar
            def _(act):
                def norm_o(i):
                    if is_step(i, LAST):
                        act.wait_ge(o_cleared, 1)
                        act.wait_ge(o_in, 16 * LAST + 16 * (1 + DEC_BATCH))
                    else:
                        act.wait_ge(o_in, 16 * i + 16)
                    for half in range(2):
                        cols = slice(half * HALF_D, (half + 1) * HALF_D)
                        nc.scalar.activation(squares[:, cols], o[:, cols], ACT.Square, accum_out=o_stat[:, half:half + 1]).then_inc(o_squared, 1)
                    act.wait_ge(head_link, HEAD_LINKS * i + 1)
                    nc.scalar.activation(o_stat[:, 4:6], o_stat[:, 2:4], ACT.Sqrt).then_inc(o_root, 1)

                def copy_h(j):
                    act.wait_ge(h_turned, 2 * j + 2)
                    after(act, routed, j)
                    nc.scalar.activation(h_t[:, 4:8, :], quarters(turn_h[:, HALF_D:D_MODEL]), ACT.Copy).then_inc(h_t_hi, 1)

                def route(j):
                    act.wait_ge(group_topped, j + 1)
                    nc.scalar.activation(group_exp[:, :], logits[:, 0:GROUPS], ACT.Exp, bias=neg_top[:, 0:1], accum_out=sums[:, 0:1]).then_inc(group_exped, 1)
                    act.wait_ge(pair_topped, j + 1)
                    nc.scalar.activation(pair_exp[:, :], best[:, 0:2], ACT.Exp, bias=neg_top[:, 1:2], accum_out=sums[:, 1:2]).then_inc(pair_exped, 1)

                def copy_o(i):
                    act.wait_ge(o_turned, 2 * i + 2)
                    after(act, mixed, i)
                    nc.scalar.activation(o_t[:, 4:8, :], quarters(turn[:, HALF_D:D_MODEL]), ACT.Copy).then_inc(o_t_hi, 1)

                def step(i):
                    if has_earlier(i, 2):
                        route(i - 2)
                    if not is_step(i, LAST):
                        norm_o(i + 1)
                    if has_earlier(i, 1):
                        copy_h(i - 1)
                    if not is_step(i, LAST):
                        copy_o(i + 1)
                    act.wait_ge(x_added, i + 1)
                    nc.scalar.activation(squares[:, :], x_mid[:, :], ACT.Square, accum_out=h_stat[:, 0:1]).then_inc(x_squared, 1)
                    act.wait_ge(body_link, BODY_LINKS * i + 1)
                    nc.scalar.activation(h_stat[:, 2:3], h_stat[:, 1:2], ACT.Sqrt).then_inc(x_root, 1)

                norm_o(0)
                copy_o(0)
                tiled(act, step)
                route(LAST - 1)
                copy_h(LAST)
                route(LAST)

            @block.vector
            def _(dve):
                v_ = nc.vector

                def norm_o(i):
                    if is_step(i, LAST):
                        dve.wait_ge(o_normed, LAST)
                        v_.memset(o[N_SAMPLE:P, :], 0.0).then_inc(o_cleared, 1)
                    link = Chain(dve, head_link, HEAD_LINKS * i).link
                    dve.wait_ge(o_squared, 2 * i + 2)
                    link(v_.tensor_scalar(o_stat[:, 2:4], o_stat[:, 0:2], 1.0 / HALF_D, EPS, ALU.mult, ALU.add))
                    dve.wait_ge(o_root, i + 1)
                    link(v_.reciprocal(o_stat[:, 0:2], o_stat[:, 4:6]))
                    after(dve, o_turned, 2 * i)
                    for half in range(2):
                        cols = slice(half * HALF_D, (half + 1) * HALF_D)
                        last = v_.scalar_tensor_tensor(o_n[:, cols], o[:, cols], o_stat[:, half:half + 1], g_out[:, cols], ALU.mult, ALU.mult)
                    last.then_inc(o_normed, 1)

                def copy_h(j):
                    dve.wait_ge(h_turned, 2 * j + 1)
                    after(dve, routed, j)
                    v_.tensor_copy(h_t[:, 0:4, :], quarters(turn_h[:, 0:HALF_D])).then_inc(h_t_lo, 1)

                def route(j):
                    link = Chain(dve, tail_link, TAIL_LINKS * j).link
                    dve.wait_ge(routed, j + 1)
                    v_.tensor_copy(real_now[:, :], real[:, bass.ds(j, 1)])
                    v_.tensor_tensor(logits[:, 0:GROUPS], router_bank[:, 0:GROUPS], b_router[:, 0:GROUPS], ALU.add)
                    link(v_.tensor_tensor(logits[:, 8:8 + EXPERTS], router_bank[:, GROUPS:GROUPS + EXPERTS], b_router[:, GROUPS:GROUPS + EXPERTS], ALU.add))
                    v_.memset(carrier[:, :], 0.0)
                    link(v_.max(group_top[:, :], logits[:, 0:8]))
                    v_.tensor_scalar(neg_top[:, 0:1], group_top[:, 0:1], -1.0, None, ALU.mult).then_inc(group_topped, 1)
                    v_.memset(carrier[:, :], 0.0)
                    link(v_.max_index(group_at[:, :], group_top[:, :], logits[:, 0:8]))
                    link(v_.tensor_copy(group[:, 0:1], group_at[:, 0:1]))
                    v_.tensor_scalar(group[:, 1:2], group[:, 0:1], float(PER_GROUP), None, ALU.mult)
                    link(v_.tensor_scalar(group_hot[:, :], iota[:, 0:GROUPS], group[:, 0:1], None, ALU.is_equal))
                    link(v_.tensor_tensor(of_group[:, :, :], logits[:, 8:8 + EXPERTS].rearrange("p (g j) -> p g j", g=GROUPS),
                                          group_hot[:, :].unsqueeze(2).broadcast_to([P, GROUPS, PER_GROUP]), ALU.mult))
                    link(v_.tensor_reduce(chosen[:, :], of_group[:, :, :].rearrange("p g j -> p j g"), AX.X, ALU.add))
                    v_.memset(carrier[:, :], 0.0)
                    link(v_.max(best[:, :], chosen[:, :]))
                    v_.tensor_scalar(neg_top[:, 1:2], best[:, 0:1], -1.0, None, ALU.mult).then_inc(pair_topped, 1)
                    v_.memset(carrier[:, :], 0.0)
                    link(v_.max_index(best_at[:, :], best[:, :], chosen[:, :]))
                    link(v_.tensor_copy(best_f[:, :], best_at[:, 0:2]))
                    link(v_.tensor_scalar(pair[:, :], best_f[:, :], group[:, 1:2], None, ALU.add))
                    link(v_.tensor_tensor(ranked[:, :, :], iota[:, 0:EXPERTS].unsqueeze(1).broadcast_to([P, 2, EXPERTS]),
                                          pair[:, :].unsqueeze(2).broadcast_to([P, 2, EXPERTS]), ALU.is_equal))
                    rows = bass.ds(2 * j, 2)
                    v_.tensor_scalar(hot[:, :, :], ranked[:, :, :], real_now[:, 0:1], None, ALU.mult)
                    link(v_.tensor_copy(all_hot[:, rows, :], ranked[:, :, :]))
                    v_.tensor_tensor(hot_sum[:, :], hot[:, 0, :], hot[:, 1, :], ALU.add).then_inc(hot_done, 1)
                    dve.wait_ge(group_exped, j + 1)
                    dve.wait_ge(pair_exped, j + 1)
                    v_.tensor_tensor(scale[:, 0:1], sums[:, 0:1], sums[:, 1:2], ALU.mult).then_inc(gates_scaled, 1)
                    dve.wait_ge(gates_scaled, 2 * j + 1)
                    v_.reciprocal(scale[:, 1:2], scale[:, 0:1]).then_inc(gates_scaled, 1)
                    dve.wait_ge(gates_scaled, 2 * j + 2)
                    v_.tensor_scalar(t["gates"][:, rows], pair_exp[:, :], scale[:, 1:2], None, ALU.mult)

                def keep_rank(j):
                    rows = bass.ds(2 * j, 2)
                    dve.wait_ge(rank_done, j + 1)
                    v_.tensor_tensor(hot_total[:, :], hot_total[:, :], hot_sum[:, :], ALU.add).then_inc(total_added, 1)
                    v_.tensor_tensor(ranked[:, :, :], hot[:, :, :], rank_bank[:, 0:EXPERTS].unsqueeze(1).broadcast_to([P, 2, EXPERTS]), ALU.mult).then_inc(rank_picked, 1)
                    dve.wait_ge(rank_picked, j + 1)
                    v_.tensor_reduce(all_rank[:, rows], ranked[:, :, :], AX.X, ALU.add)

                def copy_o(i):
                    dve.wait_ge(o_turned, 2 * i + 1)
                    after(dve, mixed, i)
                    v_.tensor_copy(o_t[:, 0:4, :], quarters(turn[:, 0:HALF_D])).then_inc(o_t_lo, 1)

                def step(i):
                    if has_earlier(i, 2):
                        route(i - 2)
                    if not is_step(i, LAST):
                        norm_o(i + 1)
                    link = Chain(dve, body_link, BODY_LINKS * i).link
                    dve.wait_ge(mixed, i + 1)
                    dve.wait_ge(x_in, 16 * i + 16)
                    after(dve, x_kept, i)
                    v_.tensor_tensor(x_mid[:, :], mixed_bank[:, :], x[:, :], ALU.add).then_inc(x_added, 1)
                    if has_earlier(i, 1):
                        copy_h(i - 1)
                    if not is_step(i, LAST):
                        copy_o(i + 1)
                    dve.wait_ge(x_squared, i + 1)
                    link(v_.tensor_scalar(h_stat[:, 1:2], h_stat[:, 0:1], 1.0 / D_MODEL, EPS, ALU.mult, ALU.add))
                    dve.wait_ge(x_root, i + 1)
                    link(v_.reciprocal(h_stat[:, 0:1], h_stat[:, 2:3]))
                    after(dve, h_turned, 2 * i)
                    after(dve, h_stored, 16 * i)
                    v_.scalar_tensor_tensor(h[:, :], x_mid[:, :], h_stat[:, 0:1], g_ffn[:, :], ALU.mult, ALU.mult).then_inc(h_normed, 1)
                    if has_earlier(i, 2):
                        keep_rank(i - 2)


                dve.wait_ge(weights_in, 16 * N_W)
                setup = Chain(dve, sem("setup_link"))
                v_.memset(logits[:, :], -3e38)
                setup.link(v_.memset(hot_total[:, :], 0.0))
                setup.link(v_.memset(ones[:, :], 1.0))
                norm_o(0)
                copy_o(0)
                tiled(dve, step)
                route(LAST - 1)
                keep_rank(LAST - 1)
                copy_h(LAST)
                route(LAST)
                keep_rank(LAST)

                dve.wait_ge(counted, 1)
                plan = Chain(dve, sem("plan_link")).link
                plan(v_.tensor_scalar(per_tile[:, :], iota[:, 0:TILES], float(P), None, ALU.mult))
                plan(v_.tensor_tensor(fills[:, :, :], rank_bank[:, 0:EXPERTS].unsqueeze(2).broadcast_to([P, EXPERTS, TILES]),
                                      per_tile[:, :].unsqueeze(1).broadcast_to([P, EXPERTS, TILES]), ALU.is_gt))
                plan(v_.tensor_reduce(blocks_of[:, :], fills[:, :, :], AX.X, ALU.add))
                plan(v_.tensor_tensor(upto[:, :, :], iota[:, 0:EXPERTS].unsqueeze(1).broadcast_to([P, EXPERTS, EXPERTS]),
                                      iota[:, 0:EXPERTS].unsqueeze(2).broadcast_to([P, EXPERTS, EXPERTS]), ALU.is_le))
                plan(v_.tensor_tensor(upto[:, :, :], upto[:, :, :], blocks_of[:, :].unsqueeze(1).broadcast_to([P, EXPERTS, EXPERTS]), ALU.mult))
                plan(v_.tensor_reduce(block_end[:, :], upto[:, :, :], AX.X, ALU.add))
                plan(v_.tensor_tensor(passed[:, :, :], block_end[0:1, :].unsqueeze(1).broadcast_to([1, MAX_BLOCKS, EXPERTS]),
                                      iota[0:1, 0:MAX_BLOCKS].unsqueeze(2).broadcast_to([1, MAX_BLOCKS, EXPERTS]), ALU.is_le))
                plan(v_.tensor_reduce(block_f[:, :], passed[:, :, :], AX.X, ALU.add))
                v_.tensor_scalar(t["block_expert"][:, 0:MAX_BLOCKS], block_f[:, :], float(EXPERTS - 1), None, ALU.min)
                v_.tensor_copy(t["block_expert"][:, MAX_BLOCKS:MAX_BLOCKS + 1], block_end[0:1, EXPERTS - 1:EXPERTS]).then_inc(experts_known, 1)
                plan(v_.tensor_tensor(start[:, :], block_end[:, :], blocks_of[:, :], ALU.subtract))
                v_.tensor_tensor(starts[:, :, :], all_hot[:, :, :], start[:, :].unsqueeze(1).broadcast_to([P, CHOICES, EXPERTS]), ALU.mult)
                plan(v_.tensor_tensor(past[:, :, :], all_rank[:, :].unsqueeze(2).broadcast_to([P, CHOICES, TILES]),
                                      per_tile[:, :].unsqueeze(1).broadcast_to([P, CHOICES, TILES]), ALU.is_ge))
                v_.tensor_reduce(in_block[:, :], starts[:, :, :], AX.X, ALU.add)
                plan(v_.tensor_reduce(row[:, :], past[:, :, :], AX.X, ALU.add))
                plan(v_.tensor_scalar(row[:, :], row[:, :], -1.0, None, ALU.add))
                v_.tensor_tensor(in_block[:, :], in_block[:, :], row[:, :], ALU.add)
                plan(v_.tensor_scalar(to_spare[:, :], row[:, :], float(P), None, ALU.mult))
                plan(v_.tensor_tensor(row[:, :], all_rank[:, :], to_spare[:, :], ALU.subtract))
                v_.tensor_tensor(to_spare[:, :], choice[:, :, 1], row[:, :], ALU.subtract)
                v_.tensor_tensor(block_hot[:, :, :], iota[:, 0:SLOT_BLOCKS].unsqueeze(1).broadcast_to([P, CHOICES, SLOT_BLOCKS]),
                                 in_block[:, :].unsqueeze(2).broadcast_to([P, CHOICES, SLOT_BLOCKS]), ALU.is_equal)
                plan(v_.tensor_tensor(row_hot[:, :, :], iota[:, :].unsqueeze(1).broadcast_to([P, CHOICES, P]),
                                      row[:, :].unsqueeze(2).broadcast_to([P, CHOICES, P]), ALU.is_equal))
                for tile in range(N_TOKENS // P, TILES):
                    pad = slice(tile * TOP_K, (tile + 1) * TOP_K)
                    v_.tensor_scalar(row_hot[:, pad, :], row_hot[:, pad, :], real[:, tile:tile + 1], None, ALU.mult)
                for value, of in enumerate((choice[:, :, 0], to_spare[:, :])):
                    last = v_.tensor_tensor(tickets_of[:, :, value, :], block_hot[:, :, :], of.unsqueeze(2).broadcast_to([P, CHOICES, SLOT_BLOCKS]), ALU.mult)
                last.then_inc(planned, 1)
                dve.wait_ge(sorted_out, 1)
                v_.tensor_copy(t["expert"].tickets[:, :, 0], router_bank[:, 0:SLOT_BLOCKS])
                plan(v_.tensor_scalar(t["expert"].tickets[:, :, 1], router_bank[:, SLOT_BLOCKS:2 * SLOT_BLOCKS], spare[:, 0:1], None, ALU.add))

            @block.gpsimd
            def _(gp):
                @stepped(gp, TILES)
                def _(i):
                    gp.wait_ge(x_added, i + 1)
                    nc.gpsimd.tensor_tensor(pool_carrier[:, :], ident[:, 0:1], ident[:, 0:1], ALU.add)
                    nc.gpsimd.tensor_copy(t["expert"].x_kept[:, bass.ds(i, 1), :].rearrange("p a n -> p (a n)"), x_mid[:, :]).then_inc(x_kept, 1)

                gp.wait_ge(x_kept, TILES)


def experts(nc, t, ident):
    with ExitStack() as ctx:
        def sb(name, shape, dt=F32):
            return ctx.enter_context(nc.sbuf_tensor(f"ex_{name}", shape, dt))

        def sem(name):
            return phase_semaphore(nc, t["phase_sems"], f"ex_{name}")

        w = t["expert"]
        w_gate, w_up, w_down, gate_in, up_in, down_in = w.w_gate, w.w_up, w.w_down, w.gate_in, w.up_in, w.down_in
        tickets = w.tickets
        token, goal = sb("token", [P, 1], I32), sb("goal", [P, 1], I32)
        x, x_t = sb("x", [P, D_MODEL]), sb("x_t", [P, KC, P])
        gated, hidden, hidden_t = sb("gated", [P, D_EXPERT]), sb("hidden", [P, D_EXPERT]), sb("hidden_t", [P, FC, P])
        y = sb("y", [P, D_MODEL])
        carrier = [sb(f"carrier{n}", [P, 1]) for n in range(4)]
        turn_x = ctx.enter_context(nc.psum_tensor("ex_turn_x", [P, D_MODEL], F32))
        gate_bank = ctx.enter_context(nc.psum_tensor("ex_gate_bank", [P, 512], F32))
        up_bank = ctx.enter_context(nc.psum_tensor("ex_up_bank", [P, 512], F32))
        turn_h = ctx.enter_context(nc.psum_tensor("ex_turn_h", [P, 512], F32))
        down_bank = ctx.enter_context(nc.psum_tensor("ex_down_bank", [P, D_MODEL], F32))

        gathered = sem("gathered")
        x_turned, x_t_lo, x_t_hi = sem("x_turned"), sem("x_t_lo"), sem("x_t_hi")
        gate_done, up_done, gated_done, hidden_done = sem("gate_done"), sem("up_done"), sem("gated_done"), sem("hidden_done")
        h_turned, h_t_copied, down_done = sem("h_turned"), sem("h_t_copied"), sem("down_done")
        y_lo, y_hi, stored = sem("y_lo"), sem("y_hi"), sem("stored")
        token_copied, goal_copied = sem("token_copied"), sem("goal_copied")
        HALF_D = D_MODEL // 2

        def block_count(eng):
            return eng.value_load(t["block_expert"][0:1, MAX_BLOCKS:MAX_BLOCKS + 1], min_val=N_TOKENS * TOP_K // P, max_val=MAX_BLOCKS)

        def over_blocks(eng, count, step):
            step(0)
            with eng.Fori(1, count) as b:
                step(b)

        def quarters(ap):
            return ap.rearrange("p (a c) -> p a c", a=4)

        with nc.Block() as block:
            @block.sync
            def _(sp):
                count = block_count(sp)
                with sp.Fori(1, count) as b:
                    load_expert(sp, w, t, b, (gate_done, up_done, down_done))

            @block.gpsimd
            def _(gp):
                count = block_count(gp)

                def carry(n):
                    nc.gpsimd.tensor_tensor(carrier[n][:, 0:1], ident[:, 0:1], ident[:, 0:1], ALU.add)

                def gather(b):
                    if not (isinstance(b, int) and b == 0):
                        gp.wait_ge(x_turned, 2 * b)
                        carry(0)
                    nc.gpsimd.tensor_copy(token[:, :], tickets[:, bass.ds(b, 1), 0:1].rearrange("p a o -> p (a o)")).then_inc(token_copied, 1)
                    gp.wait_ge(token_copied, b + 1)
                    carry(1)
                    gp.indirect_dma_start(out=x[:, :], out_offset=None, in_=t["h_ffn"],
                                          in_offset=bass.IndirectOffsetOnAxis(ap=token[:, 0:1], axis=0)).then_inc(gathered, 16)

                def scatter(b, done):
                    if not (isinstance(done, int) and done == 1):
                        gp.wait_ge(stored, 16 * done - 16)
                        carry(2)
                    nc.gpsimd.tensor_copy(goal[:, :], tickets[:, bass.ds(b, 1), 1:2].rearrange("p a o -> p (a o)")).then_inc(goal_copied, 1)
                    gp.wait_ge(goal_copied, done)
                    gp.wait_ge(y_lo, done)
                    gp.wait_ge(y_hi, done)
                    carry(3)
                    gp.indirect_dma_start(out=t["expert_rows"], out_offset=bass.IndirectOffsetOnAxis(ap=goal[:, 0:1], axis=0),
                                          in_=y[:, :], in_offset=None).then_inc(stored, 16)

                gather(0)
                gather(1)
                gather(2)
                scatter(0, 1)
                with gp.Fori(2, count + 1) as b:
                    gather(b + 1)
                    scatter(b - 1, b)
                gp.wait_ge(gathered, count * 16 + 32)
                gp.wait_ge(stored, count * 16)

            @block.tensor
            def _(pe):
                mm, transpose = nc.tensor.matmul, nc.tensor.transpose
                count = block_count(pe)

                def turn(half):
                    of = x[:, :].rearrange("p (c k) -> p k c", k=KC)
                    for k in range(4 * half, 4 * half + 4):
                        last = transpose(turn_x[:, k * P:(k + 1) * P], of[:, k, :], ident[:, :])
                    last.then_inc(x_turned, 1)

                def step(b):
                    pe.wait_ge(x_t_lo, b + 1)
                    pe.wait_ge(x_t_hi, b + 1)
                    pe.wait_ge(gate_in, 16 * b + 16)
                    after(pe, gated_done, b)
                    for k in range(KC):
                        last = mm(gate_bank[:, :], x_t[:, k, :], w_gate[:, k, :], start=(k == 0), stop=(k == KC - 1))
                    last.then_inc(gate_done, 1)
                    pe.wait_ge(up_in, 16 * b + 16)
                    after(pe, hidden_done, b)
                    for k in range(KC):
                        last = mm(up_bank[:, :], x_t[:, k, :], w_up[:, k, :], start=(k == 0), stop=(k == KC - 1))
                    last.then_inc(up_done, 1)
                    pe.wait_ge(gathered, 16 * b + 32)
                    turn(0)
                    pe.wait_ge(hidden_done, b + 1)
                    after(pe, h_t_copied, b)
                    of = hidden[:, :].rearrange("p (c k) -> p k c", k=FC)
                    for k in range(FC):
                        last = transpose(turn_h[:, k * P:(k + 1) * P], of[:, k, :], ident[:, :])
                    last.then_inc(h_turned, 1)
                    turn(1)
                    pe.wait_ge(down_in, 16 * b + 16)
                    pe.wait_ge(h_t_copied, b + 1)
                    after(pe, y_lo, b)
                    after(pe, y_hi, b)
                    for k in range(FC):
                        for half in range(2):
                            cols = slice(half * HALF_D, (half + 1) * HALF_D)
                            last = mm(down_bank[:, cols], hidden_t[:, k, :], w_down[:, k, cols], start=(k == 0), stop=(k == FC - 1))
                    last.then_inc(down_done, 1)

                pe.wait_ge(gathered, 16)
                turn(0)
                turn(1)
                over_blocks(pe, count, step)

            @block.scalar
            def _(act):
                count = block_count(act)

                def copy_x(b):
                    act.wait_ge(x_turned, 2 * b + 2)
                    nc.scalar.activation(x_t[:, 4:8, :], quarters(turn_x[:, HALF_D:D_MODEL]), ACT.Copy).then_inc(x_t_hi, 1)

                def step(b):
                    act.wait_ge(gate_done, b + 1)
                    after(act, hidden_done, b)
                    nc.scalar.activation(gated[:, :], gate_bank[:, :], ACT.Silu).then_inc(gated_done, 1)
                    act.wait_ge(up_done, b + 1)
                    copy_x(b + 1)
                    act.wait_ge(down_done, b + 1)
                    after(act, stored, 16 * b)
                    nc.scalar.activation(y[:, HALF_D:D_MODEL], down_bank[:, HALF_D:D_MODEL], ACT.Copy).then_inc(y_hi, 1)

                copy_x(0)
                over_blocks(act, count, step)

            @block.vector
            def _(dve):
                v_ = nc.vector
                count = block_count(dve)

                def copy_x(b):
                    dve.wait_ge(x_turned, 2 * b + 1)
                    v_.tensor_copy(x_t[:, 0:4, :], quarters(turn_x[:, 0:HALF_D])).then_inc(x_t_lo, 1)

                def step(b):
                    dve.wait_ge(up_done, b + 1)
                    dve.wait_ge(gated_done, b + 1)
                    v_.tensor_tensor(hidden[:, :], gated[:, :], up_bank[:, :], ALU.mult).then_inc(hidden_done, 1)
                    copy_x(b + 1)
                    dve.wait_ge(h_turned, b + 1)
                    v_.tensor_copy(hidden_t[:, :, :], quarters(turn_h[:, :])).then_inc(h_t_copied, 1)
                    dve.wait_ge(down_done, b + 1)
                    after(dve, stored, 16 * b)
                    v_.tensor_copy(y[:, 0:HALF_D], down_bank[:, 0:HALF_D]).then_inc(y_lo, 1)

                copy_x(0)
                over_blocks(dve, count, step)


def combine(nc, t, ident):
    with ExitStack() as ctx:
        def sb(name, shape, dt=F32):
            return ctx.enter_context(nc.sbuf_tensor(f"com_{name}", shape, dt))

        def sem(name):
            return phase_semaphore(nc, t["phase_sems"], f"com_{name}")

        g_final = sb("g_final", [P, D_MODEL])
        gates_now = [sb(f"gates_now{u}", [P, 2]) for u in range(2)]
        x = t["expert"].x_kept
        y = [sb(f"y{u}", [P, 2, D_MODEL]) for u in range(2)]
        one, both, out = [[sb(f"{n}{u}", [P, D_MODEL]) for u in range(2)] for n in ("one", "both", "out")]
        stat = [sb(f"stat{u}", [P, 4]) for u in range(2)]
        eps = sb("eps", [P, 1])
        squares = sb("squares", [P, D_MODEL])

        def pair(name):
            return [sem(f"{name}{u}") for u in range(2)]

        gain_in, y_in, gates_copied = sem("gain_in"), pair("y_in"), sem("gates_copied")
        added, summed, squared, rooted, normed, stored = pair("added"), pair("summed"), pair("squared"), pair("rooted"), pair("normed"), pair("stored")
        tails_in, inverted, eps_set = sem("tails_in"), sem("inverted"), sem("eps_set")
        PAIRS = PROMPT_TILES // 2

        def rows_of(i):
            return N_TOKENS - i * P if isinstance(i, int) and i == TILES - 1 else P

        def by_pairs(eng, step):
            for u in range(2):
                step(u, u, 0)
            with eng.Fori(1, PAIRS) as r:
                for u in range(2):
                    step(2 * r + u, u, r)
            step(TILES - 1, 0, PAIRS)

        with nc.Block() as block:
            @block.sync
            def _(sp):
                sp.dma_start(g_final[:, :], row_broadcast(t["norm_final"])).then_inc(gain_in, 16)
                new = slice(WINDOW - DEC_SEQ, WINDOW)
                for out_name, rows in (("sw_k_new", "swk_all"), ("sw_v_new", "swv_all")):
                    sp.dma_start(t[out_name][:, new, :], t[rows][SEQ:N_TOKENS, :].rearrange("(b t) f -> b t f", t=DEC_SEQ)).then_inc(tails_in, 16)

                def step(i, u, r):
                    n = rows_of(i)
                    wait_apart(sp, t, summed[u], r)
                    for c in range(TOP_K):
                        sp.dma_start(y[u][0:n, c, :], t["expert_rows"][bass.ds(i * P + c * ROWS, n), :]).then_inc(y_in[u], 16)

                by_pairs(sp, step)
                sp.wait_ge(tails_in, 32)
                sp.wait_ge(t["shifted"], 16 * DEC_BATCH * (1 + SHIFT_PARTS))

            @block.vector
            def _(dve):
                v_ = nc.vector
                v_.memset(eps[:, :], EPS).then_inc(eps_set, 1)
                dve.wait_ge(gain_in, 16)

                def add(i, u, r):
                    n = rows_of(i)
                    dve.wait_ge(y_in[u], 32 * r + 32)
                    v_.tensor_copy(gates_now[u][:, :], t["gates"][:, bass.ds(2 * i, 2)]).then_inc(gates_copied, 1)
                    dve.wait_ge(gates_copied, i + 1)
                    v_.scalar_tensor_tensor(one[u][0:n, :], y[u][0:n, 0, :], gates_now[u][0:n, 0:1], x[0:n, bass.ds(i, 1), :].rearrange("p a n -> p (a n)"),
                                            ALU.mult, ALU.add).then_inc(added[u], 1)
                    dve.wait_ge(added[u], r + 1)
                    v_.scalar_tensor_tensor(both[u][0:n, :], y[u][0:n, 1, :], gates_now[u][0:n, 1:2], one[u][0:n, :], ALU.mult, ALU.add).then_inc(summed[u], 1)

                def norm(i, u, r):
                    n = rows_of(i)
                    dve.wait_ge(rooted[u], r + 1)
                    v_.reciprocal(stat[u][0:n, 2:3], stat[u][0:n, 1:2]).then_inc(inverted, 1)
                    dve.wait_ge(inverted, i + 1)
                    after(dve, stored[u], 16 * r)
                    v_.scalar_tensor_tensor(out[u][0:n, :], both[u][0:n, :], stat[u][0:n, 2:3], g_final[0:n, :], ALU.mult, ALU.mult).then_inc(normed[u], 1)

                def step(i, u, r):
                    add(i, u, r)
                    if not isinstance(i, int) or i > 0:
                        norm(i - 1, 1 - u, r - 1 + u)

                by_pairs(dve, step)
                norm(TILES - 1, 0, PAIRS)

            @block.scalar
            def _(act):
                act.wait_ge(eps_set, 1)

                def step(i, u, r):
                    n = rows_of(i)
                    act.wait_ge(summed[u], r + 1)
                    nc.scalar.activation(squares[0:n, :], both[u][0:n, :], ACT.Square, accum_out=stat[u][0:n, 0:1]).then_inc(squared[u], 1)
                    act.wait_ge(squared[u], r + 1)
                    nc.scalar.activation(stat[u][0:n, 1:2], stat[u][0:n, 0:1], ACT.Sqrt, scale=1.0 / D_MODEL, bias=eps[0:n, 0:1]).then_inc(rooted[u], 1)

                def store(i, u, r):
                    n = rows_of(i)
                    act.wait_ge(normed[u], r + 1)
                    act.dma_start(t["y_all"][bass.ds(i * P, n), :], out[u][0:n, :]).then_inc(stored[u], 16)

                def both_steps(i, u, r):
                    step(i, u, r)
                    if not isinstance(i, int) or i > 0:
                        store(i - 1, 1 - u, r - 1 + u)

                by_pairs(act, both_steps)
                store(TILES - 1, 0, PAIRS)
                act.wait_ge(stored[0], 16 * (PAIRS + 1))
                act.wait_ge(stored[1], 16 * PAIRS)


OUTPUTS = {
    "y_all": (N_TOKENS, D_MODEL), "kv_all": (ROWS, KV_LORA), "kr_all": (ROWS, ROPE), "swk_all": (ROWS, SW_WIDTH),
    "swv_all": (ROWS, SW_WIDTH), "sw_k_new": (DEC_BATCH, WINDOW, SW_WIDTH), "sw_v_new": (DEC_BATCH, WINDOW, SW_WIDTH),
}
SCRATCH = {
    "q_t": ((HEADS, QK, ROWS), F32), "kn_t": ((HEADS * NOPE, ROWS), F32), "kr_t": ((ROPE, ROWS), F32),
    "v_mla": ((ROWS, 512), F32), "q_sw_t": ((512, ROWS), F32), "k_sw_t": ((512, ROWS), F32),
    "o_cat": ((ROWS, D_MODEL), F32), "o_window": ((DEC_BATCH, HEADS * DEC_SEQ, 64), F32),
    "h_ffn": ((ROWS, D_MODEL), F32),
    "expert_rows": ((TOP_K * ROWS + P, D_MODEL), F32),
}
SCRATCH_KIND = {}


def window_rows(np):
    old = (16 * np.arange(OLD_J)[:, None] + np.arange(DEC_SEQ)[None, :]).ravel()
    return np.concatenate([old, np.arange(WINDOW - 512, WINDOW)])


def host_tables(np, a):
    f = np.float32
    slope = 2.0 ** (-8.0 * np.arange(1, HEADS + 1) / HEADS)

    def window_bias(dist):
        times = sum(((dist >= 0) & (dist <= w) & (dist % d == 0)).astype(np.int64) for w, d in PATTERNS)
        log_times = np.log(np.maximum(times, 1).astype(np.float64))
        shaped = slope.reshape([HEADS] + [1] * dist.ndim)
        return np.where(times > 0, log_times - shaped * dist, MASK).astype(f)

    dist = (SEQ - P) + np.arange(P)[:, None] - np.arange(SEQ)[None, :]
    a["c_causal"] = np.where(dist >= 0, 0.0, MASK).astype(f)[None].repeat(1, 0)
    a["c_window"] = window_bias(dist)
    row = np.concatenate([window_rows(np), WINDOW + np.arange(DEC_SEQ)])
    dist = WINDOW + np.arange(DEC_SEQ)[:, None] - row[None, :]
    a["c_window_sample"] = window_bias(dist).reshape(HEADS * DEC_SEQ, WIN_ALL)
    h = np.arange(HEADS * DEC_SEQ) // DEC_SEQ
    a["c_own_head"] = (h[:, None] == (np.arange(512) // 64)[None, :]).astype(f)
    new = np.where(np.arange(DEC_SEQ)[:, None] <= (np.arange(64) % DEC_SEQ)[None, :], 0.0, MASK).astype(f)
    a["c_new_mask"] = new
    a["c_page_part"] = (np.arange(P) % 8).astype(f)[:, None]
    a["c_before"] = (np.arange(P)[:, None] < np.arange(P)[None, :]).astype(f)
    row = np.arange(TILES)[None, :] * P + np.arange(P)[:, None]
    real = row < N_TOKENS
    goal = row[:, :, None] + (np.arange(TOP_K) - TOP_K) * ROWS
    a["c_choice"] = np.stack(np.broadcast_arrays(row[:, :, None], goal), -1).reshape(P, TILES * TOP_K, 2).astype(f)
    a["c_real"] = real.astype(f)
    a["c_spare"] = (TOP_K * ROWS + np.arange(P, dtype=f))[:, None].astype(f)
    a["c_iota"] = np.broadcast_to(np.arange(P, dtype=f)[None, :], (P, P)).copy()


def host_layout(np, a, x):
    order = window_rows(np)
    k, v = [x[n][0].reshape(DEC_BATCH, WINDOW, 512)[:, order] for n in ("state_sw_k", "state_sw_v")]
    a["window_k_t"] = k.reshape(DEC_BATCH, WIN_KEYS, 4, P).transpose(0, 3, 2, 1)
    a["window_v"] = v.reshape(DEC_BATCH, WIN_TILES, P, 512).transpose(0, 2, 1, 3)
    a["w_uk_t"] = x["w_uk"][0].transpose(2, 1, 0)
    a["cache_kv"] = x["cache_kv_latent"][0].reshape(-1, 16 * KV_LORA)
    a["cache_kr"] = x["cache_k_rope"][0].reshape(-1, 16 * ROPE)
    pages = x["page_table"].astype(np.int32).reshape(DEC_BATCH, 4, 16)
    a["page_rows"] = pages.transpose(2, 0, 1).reshape(16, 32).repeat(8, 0)
    a["norm_out"] = np.concatenate([x["norm_out_mla"][0], x["norm_out_sw"][0]])
    a["w_out"], a["norm_ffn"], a["norm_final"] = x["w_out"][0], x["norm_ffn"][0], x["norm_final"]
    a["w_router"] = np.concatenate([x["w_router_group"][0], x["w_router_expert"][0]], 1)
    a["b_router"] = np.concatenate([x["b_router_group"][0], x["b_router_expert"][0]])
    a["w_gate"], a["w_up"], a["w_down"] = x["w_expert_gate"][0], x["w_expert_up"][0], x["w_expert_down"][0]


def program(nc, t, phases):
    t["shifted"] = nc.alloc_semaphore("window_shifted")
    t["ident_in"] = nc.alloc_semaphore("ident_in")
    with ExitStack() as ctx:
        def sb(name, shape, dt):
            return ctx.enter_context(nc.sbuf_tensor(name, shape, dt))

        ident = sb("ident", [P, P], F32)
        t.update(gates=sb("gates", [P, TILES * TOP_K], F32), block_expert=sb("block_expert", [1, MAX_BLOCKS + 1], I32))
        with nc.Block() as block:
            @block.sync
            def _(sp):
                sp.dma_start(ident[:, :], t["c_ident"]).then_inc(t["ident_in"], 16)
                sp.wait_ge(t["ident_in"], 16)
        for phase in phases:
            if phase is attend_window:
                t["mix"] = MixWeights(nc, ctx)
            if phase is mix_and_route:
                t["expert"] = ExpertWeights(nc, ctx)
            t["phase_sems"] = []
            phase(nc, t, ident)
            nc.clear_and_free_semaphores(t["phase_sems"])
            nc.all_engine_barrier()


PHASES = [project, attend_prompt, attend_latent, attend_window, mix_and_route, experts, combine]


def kernel(**inputs):
    import numpy as np
    import concourse.bacc as bacc
    from concourse.bass_utils import run_bass_kernel_spmd as run

    x = {n: np.asarray(a) for n, a in inputs.items()}
    f = np.float32
    a = {
        "x_all": np.concatenate([x["x_prompt"].reshape(SEQ, D_MODEL), x["x_sample"].reshape(N_SAMPLE, D_MODEL),
                                 np.zeros((ROWS - SEQ - N_SAMPLE, D_MODEL), f)]),
        "w_in": x["w_in"][0], "norm_mix": x["norm_mix"][0], "norm_q_latent": x["norm_q_latent"][0],
        "norm_kv_latent": x["norm_kv_latent"][0], "w_uq": x["w_uq"][0].reshape(Q_LORA, HEADS * QK),
        "w_uk": x["w_uk"][0].reshape(KV_LORA, 512), "w_uv": x["w_uv"][0].reshape(KV_LORA, 512),
        "state_sw_k": x["state_sw_k"][0].reshape(DEC_BATCH, WINDOW, SW_WIDTH),
        "state_sw_v": x["state_sw_v"][0].reshape(DEC_BATCH, WINDOW, SW_WIDTH),
    }
    pos = np.zeros(ROWS, f)
    pos[:SEQ] = np.arange(SEQ)
    pos[SEQ:SEQ + N_SAMPLE] = PAST_LEN + np.tile(np.arange(DEC_SEQ), DEC_BATCH)
    angle = (pos[:, None] * (f(10000.0) ** (-np.arange(HALF, dtype=f) / f(HALF)))[None, :]).astype(np.float64)
    a["c_angles"] = np.concatenate([np.cos(angle), np.sin(angle)], 1).astype(f)
    a["c_ident"] = np.eye(P, dtype=f)
    host_tables(np, a)
    host_layout(np, a, x)

    nc = bacc.Bacc("TRN2", target_bir_lowering=False, num_devices=1)
    t, arrays = {}, {}
    for name, v in a.items():
        v = np.ascontiguousarray(v)
        arrays[name] = v
        t[name] = nc.dram_tensor(name, v.shape, mybir.dt.from_np(v.dtype), kind="ExternalInput").ap()
    for name, shape in OUTPUTS.items():
        t[name] = nc.dram_tensor(name, shape, F32, kind="ExternalOutput").ap()
    for name, (shape, dt) in SCRATCH.items():
        t[name] = nc.dram_tensor(name, shape, dt, **SCRATCH_KIND).ap()
    program(nc, t, PHASES)
    o = run(nc, [arrays], core_ids=[0]).results[0]
    sample = slice(SEQ, SEQ + N_SAMPLE)
    return (o["y_all"][:SEQ].reshape(1, SEQ, D_MODEL), o["y_all"][sample].reshape(DEC_BATCH, DEC_SEQ, D_MODEL),
            o["kv_all"][:SEQ].reshape(1, 1, SEQ, KV_LORA), o["kr_all"][:SEQ].reshape(1, 1, SEQ, ROPE),
            o["swk_all"][:SEQ].reshape(1, 1, SEQ, HEADS, 64), o["swv_all"][:SEQ].reshape(1, 1, SEQ, HEADS, 64),
            o["kv_all"][sample].reshape(1, DEC_BATCH, DEC_SEQ, KV_LORA),
            o["kr_all"][sample].reshape(1, DEC_BATCH, DEC_SEQ, ROPE),
            o["sw_k_new"].reshape(1, DEC_BATCH, WINDOW, HEADS, 64),
            o["sw_v_new"].reshape(1, DEC_BATCH, WINDOW, HEADS, 64))
```
